# Optimizing a Trainium2 kernel written in Bass

```python
import jax
import jax.numpy as jnp
from jax import lax
import numpy as np

D_MODEL = 1024
BATCH = 1
SEQ = 512
DEPTH = 2
DEC_BATCH = 8
DEC_SEQ = 8
PAST_LEN = 4096
PAGE_SIZE = 128

HEAD_SIZE = 64
N_HEADS = D_MODEL // HEAD_SIZE
DECAY_LORA = 64
AAA_LORA = 64
MV_LORA = 32
GATE_LORA = 160
CONV_WIDTH = 31
FFN_CONV_WIDTH = 3
D_FF = ((8 * D_MODEL // 3 + 127) // 128) * 128
N_RWKV = (DEPTH + 1) // 2
N_CONV = DEPTH // 2
NORM_EPS = 1e-6
LN_EPS = 1e-5
LNX_EPS = 64e-5

kernel_name = 'rwkv7_conformer_convffn_step'

def _rmsnorm(x, g):
    xf = x.astype(jnp.float32)
    y = xf * lax.rsqrt(jnp.mean(xf * xf, axis=-1, keepdims=True) + NORM_EPS)
    return (y * g.astype(jnp.float32)).astype(x.dtype)

def _layernorm(x, g, b, eps):
    xf = x.astype(jnp.float32)
    mu = jnp.mean(xf, axis=-1, keepdims=True)
    var = jnp.mean(jnp.square(xf - mu), axis=-1, keepdims=True)
    y = (xf - mu) * lax.rsqrt(var + eps) * g.astype(jnp.float32) + b.astype(jnp.float32)
    return y.astype(x.dtype)

def _causal_dwconv(x, buf, w, b):
    xp = jnp.concatenate([buf.astype(x.dtype), x], axis=1)
    y = lax.conv_general_dilated(xp, w[:, None, :].astype(x.dtype), window_strides=(1,),
                                 padding='VALID', dimension_numbers=('NWC', 'WIO', 'NWC'),
                                 feature_group_count=x.shape[-1])
    return y + b.astype(x.dtype), xp[:, xp.shape[1] - (w.shape[0] - 1):]

def _wkv7_scan(s0, r, w, k, v, a, b):
    def step(s, inp):
        r_t, w_t, k_t, v_t, a_t, b_t = inp
        sa = jnp.einsum('bhij,bhj->bhi', s, a_t)
        s = (s * w_t[:, :, None, :] + sa[..., None] * b_t[:, :, None, :]
             + v_t[..., None] * k_t[:, :, None, :])
        return s, jnp.einsum('bhij,bhj->bhi', s, r_t)
    xs = tuple(jnp.swapaxes(t.astype(jnp.float32), 0, 1) for t in (r, w, k, v, a, b))
    s_final, ys = lax.scan(step, s0.astype(jnp.float32), xs)
    return jnp.swapaxes(ys, 0, 1), s_final

def _rwkv7_time_mix(x, shift_prev, s0, v_first, vres, mix, wr, wk, wv, wo, w0, w1, w2,
                    a0, a1, a2, g1, g2, k_k, k_a, r_k, lnx_w, lnx_b):
    B, T, C = x.shape
    xprev = jnp.concatenate([shift_prev[:, None, :].astype(x.dtype), x[:, :-1]], axis=1)
    xx = xprev - x
    xr, xw, xk, xv, xa, xg = (x + xx * mix[m] for m in range(6))
    r = xr @ wr
    w_log = -jax.nn.softplus(-(w0 + jnp.tanh(xw @ w1) @ w2)) - 0.5
    k = xk @ wk
    v = xv @ wv
    if v_first is None:
        v_first = v
    else:
        v0, v1, v2 = vres
        v = v + (v_first - v) * jax.nn.sigmoid(v0 + (xv @ v1) @ v2)
    a = jax.nn.sigmoid(a0 + (xa @ a1) @ a2)
    g = jax.nn.sigmoid(xg @ g1) @ g2

    def heads(t):
        return t.reshape(B, T, N_HEADS, HEAD_SIZE).astype(jnp.float32)

    kk = heads(k * k_k)
    kk = kk / jnp.maximum(jnp.sqrt(jnp.sum(kk * kk, axis=-1, keepdims=True)), 1e-12)
    k = k * (1 + (a - 1) * k_a)
    decay = jnp.exp(-jnp.exp(heads(w_log)))
    rh, kh, vh = heads(r), heads(k), heads(v)
    y, s_new = _wkv7_scan(s0, rh, decay, kh, vh, -kk, kk * heads(a))
    mu = jnp.mean(y, axis=-1, keepdims=True)
    var = jnp.mean(jnp.square(y - mu), axis=-1, keepdims=True)
    y = ((y - mu) * lax.rsqrt(var + LNX_EPS)).reshape(B, T, C)
    y = y * lnx_w.astype(jnp.float32) + lnx_b.astype(jnp.float32)
    bonus = (jnp.sum(rh * kh * r_k.astype(jnp.float32), axis=-1, keepdims=True) * vh).reshape(B, T, C)
    out = ((y + bonus).astype(x.dtype) * g) @ wo
    return out, x[:, -1], s_new, v_first

def _conformer_conv(x, buf, w_in, b_in, dw_w, dw_b, ln_w, ln_b, w_out, b_out):
    C = x.shape[-1]
    h = x @ w_in + b_in
    h = h[..., :C] * jax.nn.sigmoid(h[..., C:])
    h, new_buf = _causal_dwconv(h, buf, dw_w, dw_b)
    h = jax.nn.silu(_layernorm(h, ln_w, ln_b, LN_EPS))
    return h @ w_out + b_out, new_buf

def _conv_ffn(x, buf, w_in, dw_w, dw_b, w_out):
    h, new_buf = _causal_dwconv(x @ w_in, buf, dw_w, dw_b)
    g, u = jnp.split(h, 2, axis=-1)
    return (jax.nn.silu(g) * u) @ w_out, new_buf

def _trunk(x, st_wkv, st_shift, st_glu, st_ffn, p):
    v_first = None
    wkv_l, shift_l, glu_l, ffn_l = [], [], [], []
    for i in range(DEPTH):
        j = i // 2
        h = _rmsnorm(x, p['norm_gain'][i, 0])
        if i % 2 == 0:
            vres = None if j == 0 else (p['rwkv_v0'][j - 1], p['rwkv_v1'][j - 1], p['rwkv_v2'][j - 1])
            m, sh, s_new, v_first = _rwkv7_time_mix(
                h, st_shift[j], st_wkv[j], v_first, vres, p['rwkv_mix'][j],
                p['rwkv_wr'][j], p['rwkv_wk'][j], p['rwkv_wv'][j], p['rwkv_wo'][j],
                p['rwkv_w0'][j], p['rwkv_w1'][j], p['rwkv_w2'][j],
                p['rwkv_a0'][j], p['rwkv_a1'][j], p['rwkv_a2'][j],
                p['rwkv_g1'][j], p['rwkv_g2'][j], p['rwkv_k_k'][j], p['rwkv_k_a'][j],
                p['rwkv_r_k'][j], p['rwkv_lnx_w'][j], p['rwkv_lnx_b'][j])
            wkv_l.append(s_new)
            shift_l.append(sh)
        else:
            m, gb = _conformer_conv(
                h, st_glu[j], p['conv_w_in'][j], p['conv_b_in'][j], p['conv_dw_w'][j],
                p['conv_dw_b'][j], p['conv_ln_w'][j], p['conv_ln_b'][j],
                p['conv_w_out'][j], p['conv_b_out'][j])
            glu_l.append(gb)
        x = x + _rmsnorm(m, p['norm_gain'][i, 1])
        h = _rmsnorm(x, p['norm_gain'][i, 2])
        f, fb = _conv_ffn(h, st_ffn[i], p['ffn_w_in'][i], p['ffn_dw_w'][i],
                          p['ffn_dw_b'][i], p['ffn_w_out'][i])
        ffn_l.append(fb)
        x = x + _rmsnorm(f, p['norm_gain'][i, 3])
    return x, jnp.stack(wkv_l), jnp.stack(shift_l), jnp.stack(glu_l), jnp.stack(ffn_l)

def setup_inputs(seed: int = 0) -> dict:
    key = jax.random.key(seed)
    ks = iter(jax.random.split(key, 64))
    D = D_MODEL
    F2 = 2 * D_FF

    def nrm(shape, scale):
        return scale * jax.random.normal(next(ks), shape, jnp.float32)

    def uni(shape, lo, hi):
        return jax.random.uniform(next(ks), shape, jnp.float32, lo, hi)

    n_vres = N_RWKV - 1
    return {
        'x_prompt': nrm((BATCH, SEQ, D), 1.0),
        'x_sample': nrm((DEC_BATCH, DEC_SEQ, D), 1.0),
        'state_rwkv_wkv': nrm((N_RWKV, DEC_BATCH, N_HEADS, HEAD_SIZE, HEAD_SIZE), 0.1),
        'state_rwkv_shift': nrm((N_RWKV, DEC_BATCH, D), 1.0),
        'state_conv_glu': nrm((N_CONV, DEC_BATCH, CONV_WIDTH - 1, D), 0.5),
        'state_ffn_conv': nrm((DEPTH, DEC_BATCH, FFN_CONV_WIDTH - 1, F2), 0.5),
        'norm_gain': 1.0 + nrm((DEPTH, 4, D), 0.05),
        'rwkv_mix': uni((N_RWKV, 6, D), 0.0, 1.0),
        'rwkv_wr': nrm((N_RWKV, D, D), D ** -0.5),
        'rwkv_wk': nrm((N_RWKV, D, D), D ** -0.5),
        'rwkv_wv': nrm((N_RWKV, D, D), D ** -0.5),
        'rwkv_wo': nrm((N_RWKV, D, D), D ** -0.5),
        'rwkv_w0': uni((N_RWKV, D), -6.0, -0.5),
        'rwkv_w1': nrm((N_RWKV, D, DECAY_LORA), D ** -0.5),
        'rwkv_w2': nrm((N_RWKV, DECAY_LORA, D), 0.3 * DECAY_LORA ** -0.5),
        'rwkv_a0': nrm((N_RWKV, D), 0.3),
        'rwkv_a1': nrm((N_RWKV, D, AAA_LORA), D ** -0.5),
        'rwkv_a2': nrm((N_RWKV, AAA_LORA, D), 0.3 * AAA_LORA ** -0.5),
        'rwkv_v0': 1.0 + nrm((n_vres, D), 0.3),
        'rwkv_v1': nrm((n_vres, D, MV_LORA), D ** -0.5),
        'rwkv_v2': nrm((n_vres, MV_LORA, D), 0.3 * MV_LORA ** -0.5),
        'rwkv_g1': nrm((N_RWKV, D, GATE_LORA), D ** -0.5),
        'rwkv_g2': nrm((N_RWKV, GATE_LORA, D), GATE_LORA ** -0.5),
        'rwkv_k_k': 0.85 + nrm((N_RWKV, D), 0.05),
        'rwkv_k_a': 1.0 + nrm((N_RWKV, D), 0.05),
        'rwkv_r_k': nrm((N_RWKV, N_HEADS, HEAD_SIZE), 0.1),
        'rwkv_lnx_w': 1.0 + nrm((N_RWKV, D), 0.05),
        'rwkv_lnx_b': nrm((N_RWKV, D), 0.01),
        'conv_w_in': nrm((N_CONV, D, 2 * D), D ** -0.5),
        'conv_b_in': nrm((N_CONV, 2 * D), 0.01),
        'conv_dw_w': nrm((N_CONV, CONV_WIDTH, D), CONV_WIDTH ** -0.5),
        'conv_dw_b': nrm((N_CONV, D), 0.01),
        'conv_ln_w': 1.0 + nrm((N_CONV, D), 0.05),
        'conv_ln_b': nrm((N_CONV, D), 0.01),
        'conv_w_out': nrm((N_CONV, D, D), D ** -0.5),
        'conv_b_out': nrm((N_CONV, D), 0.01),
        'ffn_w_in': nrm((DEPTH, D, F2), D ** -0.5),
        'ffn_dw_w': nrm((DEPTH, FFN_CONV_WIDTH, F2), FFN_CONV_WIDTH ** -0.5),
        'ffn_dw_b': nrm((DEPTH, F2), 0.01),
        'ffn_w_out': nrm((DEPTH, D_FF, D), D_FF ** -0.5),
    }

def reference(x_prompt, x_sample, state_rwkv_wkv, state_rwkv_shift, state_conv_glu,
              state_ffn_conv, norm_gain, rwkv_mix, rwkv_wr, rwkv_wk, rwkv_wv, rwkv_wo,
              rwkv_w0, rwkv_w1, rwkv_w2, rwkv_a0, rwkv_a1, rwkv_a2, rwkv_v0, rwkv_v1,
              rwkv_v2, rwkv_g1, rwkv_g2, rwkv_k_k, rwkv_k_a, rwkv_r_k, rwkv_lnx_w,
              rwkv_lnx_b, conv_w_in, conv_b_in, conv_dw_w, conv_dw_b, conv_ln_w,
              conv_ln_b, conv_w_out, conv_b_out, ffn_w_in, ffn_dw_w, ffn_dw_b, ffn_w_out):
    p = dict(norm_gain=norm_gain, rwkv_mix=rwkv_mix, rwkv_wr=rwkv_wr, rwkv_wk=rwkv_wk,
             rwkv_wv=rwkv_wv, rwkv_wo=rwkv_wo, rwkv_w0=rwkv_w0, rwkv_w1=rwkv_w1,
             rwkv_w2=rwkv_w2, rwkv_a0=rwkv_a0, rwkv_a1=rwkv_a1, rwkv_a2=rwkv_a2,
             rwkv_v0=rwkv_v0, rwkv_v1=rwkv_v1, rwkv_v2=rwkv_v2, rwkv_g1=rwkv_g1,
             rwkv_g2=rwkv_g2, rwkv_k_k=rwkv_k_k, rwkv_k_a=rwkv_k_a, rwkv_r_k=rwkv_r_k,
             rwkv_lnx_w=rwkv_lnx_w, rwkv_lnx_b=rwkv_lnx_b, conv_w_in=conv_w_in,
             conv_b_in=conv_b_in, conv_dw_w=conv_dw_w, conv_dw_b=conv_dw_b,
             conv_ln_w=conv_ln_w, conv_ln_b=conv_ln_b, conv_w_out=conv_w_out,
             conv_b_out=conv_b_out, ffn_w_in=ffn_w_in, ffn_dw_w=ffn_dw_w,
             ffn_dw_b=ffn_dw_b, ffn_w_out=ffn_w_out)
    bp = x_prompt.shape[0]
    dt = x_prompt.dtype
    z_wkv = jnp.zeros((N_RWKV, bp, N_HEADS, HEAD_SIZE, HEAD_SIZE), jnp.float32)
    z_shift = jnp.zeros((N_RWKV, bp, D_MODEL), dt)
    z_glu = jnp.zeros((N_CONV, bp, CONV_WIDTH - 1, D_MODEL), dt)
    z_ffn = jnp.zeros((DEPTH, bp, FFN_CONV_WIDTH - 1, 2 * D_FF), dt)
    y_prompt, p_wkv, p_shift, p_glu, p_ffn = _trunk(x_prompt, z_wkv, z_shift, z_glu, z_ffn, p)
    y_sample, s_wkv, s_shift, s_glu, s_ffn = _trunk(
        x_sample, state_rwkv_wkv, state_rwkv_shift, state_conv_glu, state_ffn_conv, p)
    p_wkv = p_wkv.astype(state_rwkv_wkv.dtype)
    s_wkv = s_wkv.astype(state_rwkv_wkv.dtype)
    return (y_prompt, y_sample, p_wkv, p_shift, p_glu, p_ffn, s_wkv, s_shift, s_glu, s_ffn)


_drawn_inputs = setup_inputs


def setup_inputs(seed=0):
    import zlib

    import numpy as np

    out = dict(_drawn_inputs(seed))
    spreads = {}
    factors = {'rwkv_w1': 3.797,
     'rwkv_w2': 3.859,
     'rwkv_lnx_b': 6.825,
     'conv_b_in': 5.468,
     'conv_dw_b': 5.226,
     'conv_ln_b': 8.0,
     'conv_b_out': 6.346,
     'ffn_dw_b': 5.176}
    for name, (base, spread) in spreads.items():
        noise = np.random.default_rng([zlib.crc32(name.encode()), seed]).standard_normal(out[name].shape)
        drawn = base * np.exp(spread * noise) if base else spread * noise
        out[name] = jnp.asarray(drawn.astype(out[name].dtype))
    for name, factor in factors.items():
        out[name] = (out[name] * factor).astype(out[name].dtype)
    return out
```

```python
from contextlib import ExitStack
import math

import numpy as np
import concourse.bass as bass
import concourse.mybir as mybir

ALU = mybir.AluOpType
ACT = mybir.ActivationFunctionType
F32 = mybir.dt.float32

P = 128
D = 1024
SEQ = 512
DB, DS = 8, 8
DEC = DB * DS
T = SEQ + DEC
KT = D // P
HS = 64
NH = D // HS
CH = 64
NCH = SEQ // CH
CW = 31
F = ((8 * D // 3 + 127) // 128) * 128
FT = F // P
LW, LA, LG = 64, 64, 160
NORM_EPS, LN_EPS, LNX_EPS = 1e-6, 1e-5, 64e-5
LAM = math.exp(-0.5)
NSTATE = CW - 1

C_ID, C_MEAN, C_HEAD = 0, 128, 256
C_MASK, C_MASKD = 384, 512
C_LVL = 640
LEVELS = [1, 2, 4, 8, 16, 32]
C_LOW1 = C_LVL + 64 * len(LEVELS)
C_IS = C_LOW1 + 64
C_SCAN = C_IS + 64
C_B8 = C_SCAN + T
C_EPS = C_B8 + 8
NCONST = C_EPS + 4


def constants():
    c = np.zeros((P, NCONST), np.float32)
    i = np.arange(P)
    s = i % CH
    t = np.arange(CH)
    c[i, C_ID + i] = 1.0
    c[:, C_MEAN:C_MEAN + P] = 1.0 / D
    c[:, C_HEAD:C_HEAD + P] = (i[:, None] // HS == i[None, :] // HS)
    same = s[:, None] // DS == t[None, :] // DS
    c[:, C_MASK:C_MASK + 64] = s[:, None] < t
    c[:, C_MASK + 64:C_MASK + 128] = s[:, None] <= t
    c[:, C_MASKD:C_MASKD + 64] = (s[:, None] < t) & same
    c[:, C_MASKD + 64:C_MASKD + 128] = (s[:, None] <= t) & same
    for n, m in enumerate(LEVELS):
        pair = (s[:, None] // (2 * m) == t // (2 * m)) & (s[:, None] % (2 * m) < m) & (t % (2 * m) >= m)
        c[:, C_LVL + 64 * n:C_LVL + 64 * n + 64] = pair
    c[:, C_LOW1:C_LOW1 + 64] = (s[:, None] // 2 == t // 2) & (s[:, None] > t)
    c[:, C_IS:C_IS + 64] = s[:, None] == t
    tok = np.arange(T)
    c[:, C_SCAN:C_SCAN + T] = np.where(tok < SEQ, tok % CH != 0, tok % DS != 0)
    c[:, C_B8:C_B8 + 8] = s[:, None] // DS == np.arange(DB)
    c[:, C_EPS:C_EPS + 4] = [NORM_EPS, LN_EPS, LNX_EPS, 0.0]
    return c


PARAMS = [("norm_gain", 8 * KT), ("rwkv_mix", 6 * KT), ("rwkv_w0", KT), ("rwkv_a0", KT), ("rwkv_k_k", KT),
          ("rwkv_k_a", KT), ("rwkv_r_k", KT), ("rwkv_lnx_w", KT), ("rwkv_lnx_b", KT), ("conv_b_in", 2 * KT),
          ("conv_dw_w", CW * KT), ("conv_dw_b", KT), ("conv_ln_w", KT), ("conv_ln_b", KT), ("conv_b_out", KT),
          ("ffn_dw_w", 2 * 3 * 2 * FT), ("ffn_dw_b", 2 * 2 * FT), ("state_rwkv_shift", DB * KT)]
PCOL = {}
_n = 0
for _name, _rows in PARAMS:
    PCOL[_name] = _n
    _n += _rows
NPC = _n
NPG = -(-NPC // P)
NFS = DB * 2 * 2 * FT
NFG = -(-NFS // P)
NGS = DB * NSTATE * KT
NGG = NGS // P

TILES = [("par", 2), ("xin", 10), ("n0", 1), ("shift", 1), ("lo1", 4), ("lo2", 2 * KT), ("k", KT),
         ("r", KT), ("v", KT), ("kk", KT), ("post", 4 * KT), ("wo", KT), ("n1", 1), ("fst0", 2), ("n2", 1),
         ("up0", 2 * FT), ("down0", KT), ("fo0", 2), ("n3", 1),
         ("gst", 4), ("fst1", 2), ("n4", 1), ("glu", 2 * KT), ("go", 2), ("ln", 2), ("co", KT), ("n5", 1), ("n6", 1),
         ("up1", 2 * FT), ("down1", KT), ("fo1", 2), ("n7", 1), ("yout", 10)]
TB = {}
_n = 0
for _name, _rows in TILES:
    TB[_name] = _n
    _n += _rows

WSEQ = [("k", KT), ("r", KT), ("v", KT), ("wo", KT), ("up0", 2 * FT), ("glu", 2 * KT), ("co", KT), ("up1", 2 * FT)]
WB = {}
_n = 0
for _name, _rows in WSEQ:
    WB[_name] = _n
    _n += _rows
RING = 4
WTILE = [TB[n] + j for n, m in WSEQ for j in range(m)]

RAW = 2 + SEQ + DB * (2 + DS)
GB = NSTATE + SEQ + DB * (NSTATE + DS)

REG = KT * T
A_H, A_XX, A_A, A_B, A_SG, A_AG, A_K, A_R = [REG * n for n in range(8)]
A_HID = A_XX
A_WO = A_HID + FT * T
A_RAW = A_WO + 2 * FT * P
A_CV = A_RAW + 4 * RAW
A_FO = A_CV + 4 * T
A_M = A_R
A_FST = A_FO + FT * 2 * 18
A_FR = A_FST + DB * 2 * 2 * FT
A_GB = A_XX
A_GR = A_GB + KT * GB
A_CO = A_GR + NGS
A_SIG = A_CO + REG
assert A_FR + NFG * P <= A_M and A_SIG + 2 * T <= A_M
STAGES = 15


def build(nc, a, out):
    with ExitStack() as ctx:
        def sb(name, shape):
            return ctx.enter_context(nc.sbuf_tensor(name, shape, F32))

        def sem(name):
            return ctx.enter_context(nc.semaphore(name))

        x = sb("x", [P, KT, T])
        arena = sb("arena", [P, 8 * REG])
        ring = sb("ring", [P, RING, KT, P])
        con = sb("con", [P, NCONST])
        par = sb("par", [P, NPC])
        hg = sb("hg", [P, 2, T])
        tmp = sb("tmp", [P, 4, T])
        ost = sb("ost", [P, 896])
        pend = sb("pend", [P, KT, 16])
        omka = sb("omka", [P, KT])
        ps = ctx.enter_context(nc.psum_tensor("ps", [P, 4096], F32))

        def region(at, n=KT, w=T):
            return arena[:, at:at + n * w].rearrange("p (k t) -> p k t", t=w)

        h, xx, bufA, bufB = region(A_H), region(A_XX), region(A_A), region(A_B)
        sg, ag, kb, rb, mb = region(A_SG), region(A_AG), region(A_K), region(A_R), region(A_M)
        kkb, vb, yb = xx, bufA, sg
        lo1 = arena[:, A_R:A_R + KT * 288].rearrange("p (k n) -> p k n", n=288)
        hwa = arena[0:64, A_R + KT * 288:A_R + KT * 288 + 2 * T].rearrange("p (k t) -> p k t", t=T)
        lo2 = arena[0:64, A_K:A_K + 2 * D].rearrange("p (k n) -> p k n", n=D)
        lg2 = arena[:, A_H:A_H + 2 * D].rearrange("p (k n) -> p k n", n=D)
        rows = arena[:, A_A:A_A + NPG * P].rearrange("p (g n) -> p g n", n=P)
        fst = arena[:, A_FST:A_FST + NFS]
        frows = arena[:, A_FR:A_FR + NFG * P].rearrange("p (g n) -> p g n", n=P)
        grows = arena[:, A_B + REG:A_B + REG + NGG * P].rearrange("p (g n) -> p g n", n=P)
        xrows = arena[:, A_SG:A_SG + 5 * D].rearrange("p (g n) -> p g n", n=D)
        hid = region(A_HID, FT)
        wos = arena[:, A_WO:A_WO + 2 * FT * P].rearrange("p (s k n) -> p s k n", s=2, n=P)
        raw = arena[:, A_RAW:A_RAW + 4 * RAW].rearrange("p (q n) -> p q n", q=4)
        cv = arena[:, A_CV:A_CV + 4 * T].rearrange("p (q n) -> p q n", q=4)
        fo = arena[:, A_FO:A_FO + 2 * FT * 18].rearrange("p (f n) -> p f n", n=18)
        gb = region(A_GB, KT, GB)
        gst = arena[:, A_GR:A_GR + NGS]
        cvo = region(A_CO)
        gsig = region(A_SIG, 2)
        ident = con[:, C_ID:C_ID + P]

        def small(at, n=64):
            return arena[:, at:at + KT * n].rearrange("p (k n) -> p k n", n=n)

        MbT = small(A_B, 128)
        Mn, TT, TI, Y, Vt, Bt, S = [small(A_B + 1024 + 512 * n) for n in range(7)]
        ringf = ring[:].rearrange("p s k n -> p (s k n)")
        MkT = ringf[:, 0:1024].rearrange("p (k n) -> p k n", n=128)
        Ktk = ringf[:, 1024:1536].rearrange("p (k n) -> p k n", n=64)
        bbar = ringf[:, 1536:2560].rearrange("p (v k n) -> p v k n", v=2, n=64)
        kbar = ringf[:, 2560:3584].rearrange("p (v k n) -> p v k n", v=2, n=64)
        Rm, SA = Y, TI
        Sd = arena[:, A_H:A_H + KT * DB * 64].rearrange("p (k b n) -> p k b n", b=DB, n=64)
        Snat = arena[:, A_B:A_B + KT * DB * 64].rearrange("p (k b n) -> p k b n", b=DB, n=64)
        yg = yb

        def pcol(name, i):
            return par[:, PCOL[name] + i:PCOL[name] + i + 1]

        def gain(n, kt):
            return pcol("norm_gain", n * KT + kt)

        NAMES = ["const_in", "par_in", "x_in", "lo1_in", "lo2_in", "lg2_in", "sd_in", "fst_in", "gst_in", "out_done",
                 "tile_full", "tile_read", "sq_ready", "sq_used", "x_ready", "h_ready", "xm_ready", "vec_done",
                 "act_done", "pool_done", "v_ready", "wide_ready", "prep_sq", "prep_e", "prep_s", "prep_done",
                 "gath_ready", "ost_ready", "ost_sent", "post_a", "post_v", "z_ready", "bar_ready", "sd_ready", "snat_ready",
                 "wkv_over", "state_out", "glu_s", "glu_ready", "glu_hist", "conv_done", "ln_a", "ln_v", "y_ready", "mix_free"]
        sm = {n: sem(n) for n in NAMES}
        w_in = [sem(f"w_in{i}") for i in range(RING)]
        wo_in = [[sem(f"wo_in{l}{i}") for i in range(2)] for l in range(2)]
        xt_in = [sem(f"xt_in{i}") for i in range(5)]
        mm_done = [sem(f"mm_done{g}") for g in range(2)]
        ev_done = [sem(f"ev_done{g}") for g in range(2)]
        FF = [{n: sem(f"{n}{l}") for n in ("raw_ready", "hist_ready", "conv_ready", "gate_ready", "hid_ready",
                                           "tails", "no_hist", "cvd")} for l in range(2)]
        block = ctx.enter_context(nc.Block())

        def tset(t):
            return (t % 4) * 1024

        def bank2(t, n=T, m=P):
            return ps[0:m, tset(t):tset(t) + n]

        @block.sync
        def _(eng):
            def load(dst, src, s):
                eng.dma_start(dst, src).then_inc(s, 16)

            load(con[:], a["consts"], sm["const_in"])
            r = 0
            n_par = 0
            for name, m in PARAMS:
                src = a[name]
                flat = src.rearrange(" ".join(f"d{i}" for i in range(len(src.shape))) + " -> ("
                                     + " ".join(f"d{i}" for i in range(len(src.shape))) + ")")
                flat = flat.rearrange("(r c) -> r c", c=P)
                at = 0
                while at < m:
                    g, p = (r + at) // P, (r + at) % P
                    k = min(m - at, P - p)
                    load(rows[p:p + k, g, :], flat[at:at + k, :], sm["par_in"])
                    n_par += 1
                    at += k
                r += m

            def load_fst(dst, l, s):
                f = a["state_ffn_conv"][l].rearrange("b w (k p) -> (b w k) p", p=P)
                full = NFS // P
                load(dst[:, 0:full, :], f[0:full * P, :].rearrange("(g p) c -> p g c", p=P), s)
                load(dst[0:NFS - full * P, full, :], f[full * P:NFS, :], s)

            for g in range(4):
                load(xrows[:, g, :], a["x_prompt"][0, g * P:(g + 1) * P, :], xt_in[g])
            load(xrows[0:DEC, 4, :], a["x_sample"].rearrange("b t d -> (b t) d"), xt_in[4])
            for name, o, m in (("rwkv_w1", 0, LW), ("rwkv_a1", LW, LA), ("rwkv_g1", LW + LA, LG)):
                load(lo1[:, :, o:o + m], a[name][0].rearrange("(k p) n -> p k n", p=P), sm["lo1_in"])
            load(lo2[:, 0, :], a["rwkv_w2"][0], sm["lo2_in"])
            load(lo2[:, 1, :], a["rwkv_a2"][0], sm["lo2_in"])

            def wtile(w, src, n):
                load(ring[:, w % RING], src[:, n * P:(n + 1) * P].rearrange("(k p) n -> p k n", p=P), w_in[w % RING])

            def weights(name, src, order, first=0):
                for j, n in list(enumerate(order))[first:]:
                    w = WB[name] + j
                    if w >= RING:
                        eng.wait_ge(sm["tile_full"], WTILE[w - RING] + 1)
                    wtile(w, src, n)

            weights("k", a["rwkv_wk"][0], range(KT))
            weights("r", a["rwkv_wr"][0], range(KT))
            weights("v", a["rwkv_wv"][0], range(KT))
            eng.wait_ge(sm["tile_full"], TB["v"] + KT)
            for b in range(DB):
                load(Snat[:, :, b, :], a["state_rwkv_wkv"][0, b].rearrange("(k e) i j -> (e i) k j", e=2), sm["sd_in"])

            def store(dst, src):
                eng.dma_start(dst, src).then_inc(sm["out_done"], 16)
                n_out[0] += 1

            n_out = [0]

            eng.wait_ge(sm["tile_read"], TB["shift"] + 1)
            for kt in range(KT):
                store(out["p_shift"][0, :, kt * P:(kt + 1) * P], ost[9 * kt:9 * kt + 1, P:2 * P])
                store(out["s_shift"][0, :, kt * P:(kt + 1) * P], ost[9 * kt + 1:9 * kt + 9, P:2 * P])
            eng.wait_ge(sm["state_out"], 1)
            store(out["p_wkv"][0, 0].rearrange("(k e) i j -> (e i) k j", e=2), ost[:, 256:768].rearrange("p (k j) -> p k j", j=64))
            eng.wait_ge(sm["state_out"], 1 + KT)
            for b in range(DB):
                store(out["s_wkv"][0, b].rearrange("(k e) i j -> (e i) k j", e=2), Snat[:, :, b, :])
            load(lg2[:, 0, :], a["rwkv_g2"][0, 0:P, :], sm["lg2_in"])
            load(lg2[0:LG - P, 1, :], a["rwkv_g2"][0, P:LG, :], sm["lg2_in"])
            weights("wo", a["rwkv_wo"][0], range(KT))
            eng.wait_ge(sm["z_ready"], KT)
            load_fst(frows, 0, sm["fst_in"])

            def ffn(l):
                up = a["ffn_w_in"][l]
                w0 = WB[f"up{l}"]
                for j in range(4):
                    f = (j // 2) * P + (j % 2) * F
                    eng.wait_ge(sm["tile_full"], WTILE[w0 + j - RING] + 1)
                    load(ring[:, j], up[:, f:f + P].rearrange("(k p) n -> p k n", p=P), w_in[j])
                with eng.Fori(1, FT // 2) as i:
                    for j in range(4):
                        eng.wait_ge(sm["tile_full"], i * 4 + (TB[f"up{l}"] + j - RING + 1))
                        f = (j // 2) * P + (j % 2) * F
                        load(ring[:, j], up[:, bass.ds(i * (2 * P) + f, P)].rearrange("(k p) n -> p k n", p=P), w_in[j])
                down = a["ffn_w_out"][l]
                for n in range(KT):
                    if n == 0:
                        eng.wait_ge(sm["tile_full"], TB[f"up{l}"])
                    if n >= 2:
                        eng.wait_ge(sm["tile_full"], TB[f"down{l}"] + n - 1)
                    load(wos[:, n % 2], down[:, n * P:(n + 1) * P].rearrange("(k p) n -> p k n", p=P), wo_in[l][n % 2])

            ffn(0)
            eng.wait_ge(sm["tile_full"], TB["down0"] + KT)
            load(grows, a["state_conv_glu"][0].rearrange("b w (k p) -> (b w k) p", p=P).rearrange("(g p) c -> p g c", p=P), sm["gst_in"])
            load_fst(frows, 1, sm["gst_in"])
            weights("glu", a["conv_w_in"][0], [n // 2 + KT * (n % 2) for n in range(2 * KT)])

            def ffn_state(l):
                eng.wait_ge(sm["tile_read"], TB[f"fo{l}"] + 2)
                for g in range(7):
                    m = min(7, 2 * FT - 7 * g)
                    for q in range(m):
                        f = 7 * g + q
                        store(out["p_ffn"][l, 0, :, f * P:(f + 1) * P], ost[18 * q:18 * q + 2, g * P:(g + 1) * P])
                        store(out["s_ffn"][l, :, :, f * P:(f + 1) * P].rearrange("b w n -> (b w) n"), ost[18 * q + 2:18 * q + 18, g * P:(g + 1) * P])

            ffn_state(0)
            eng.wait_ge(sm["tile_read"], TB["go"] + 2)
            for kt in range(KT):
                store(out["p_glu"][0, 0, :, kt * P:(kt + 1) * P], ost[30 * (kt % 4):30 * (kt % 4) + 30, (kt // 4) * P:(kt // 4 + 1) * P])
                for b in range(DB):
                    r = 64 * (kt % 2) + DS * b
                    store(out["s_glu"][0, b, NSTATE - DS:NSTATE, kt * P:(kt + 1) * P],
                          ost[r:r + DS, 256 + (kt // 2) * P:256 + (kt // 2 + 1) * P])
            store(out["s_glu"][0, :, 0:NSTATE - DS, :], a["state_conv_glu"][0, :, DS:NSTATE, :])
            weights("co", a["conv_w_out"][0], range(KT))
            ffn(1)
            ffn_state(1)
            for g in range(5):
                eng.wait_ge(sm["tile_read"], TB["yout"] + 2 * g + 2)
                if g < 4:
                    store(out["y_prompt"][0, g * P:(g + 1) * P, :], xrows[:, g, :])
                else:
                    store(out["y_sample"].rearrange("b t d -> (b t) d"), xrows[0:DEC, 4, :])
            eng.wait_ge(sm["out_done"], 16 * n_out[0])

        @block.tensor
        def _(pe):
            def begin(t):
                if t >= 4:
                    pe.wait_ge(sm["tile_read"], t - 3)

            def product(t, terms, m=P, mark=None):
                begin(t)
                for i, (lhs, rhs, pre) in enumerate(terms):
                    for w, v in pre:
                        pe.wait_ge(w, v)
                    st, sp = i == 0, i == len(terms) - 1
                    pe.matmul(ps[0:m, tset(t):tset(t) + SEQ], lhs, rhs[:, 0:SEQ], start=st, stop=sp)
                    ins = pe.matmul(ps[0:m, tset(t) + SEQ:tset(t) + T], lhs, rhs[:, SEQ:T], start=st, stop=sp)
                    if mark is not None and not sp:
                        ins.then_inc(mark, 1)
                ins.then_inc(sm["tile_full"], 1)

            def transposes(t, srcs):
                begin(t)
                for q, src in enumerate(srcs):
                    k = src.shape[0]
                    m = src.shape[1]
                    ins = pe.transpose(ps[0:m, tset(t) + P * q:tset(t) + P * q + k], src, ident[0:k, 0:k])
                ins.then_inc(sm["tile_full"], 1)

            def norm_sums(name, ones=C_MEAN, first=0):
                n = norm_i[0]
                product(TB[name] + first, [(con[:, ones:ones + P], tmp[:, kt % 2, :], [(sm["sq_ready"], KT * n + kt + 1)])
                                   for kt in range(KT)], mark=sm["sq_used"])
                norm_i[0] += 1

            norm_i = [0]

            def gemm(name, src, pre, first=0):
                for j in range(KT if name not in ("glu",) else 2 * KT):
                    w = WB[name] + j
                    terms = []
                    for kt in range(KT):
                        p = [(w_in[w % RING], 16 * (w // RING + 1))] if kt == 0 else []
                        if j == 0:
                            p.append((pre[0], pre[1] + kt + 1))
                        terms.append((ring[:, w % RING, kt, :], src[:, kt, :], p))
                    product(TB[name] + j, terms)

            def state_turns(name):
                for t in range(2):
                    transposes(TB[name] + t, [frows[0:min(P, NFS - P * g), g, :] for g in range(4 * t, min(4 * t + 4, NFG))])

            pe.wait_ge(sm["const_in"], 16)
            pe.wait_ge(sm["par_in"], 16 * n_par_dmas())
            for t in range(2):
                transposes(TB["par"] + t, [rows[0:min(P, NPC - P * g), g, :] for g in range(4 * t, min(4 * t + 4, NPG))])
            for g in range(5):
                pe.wait_ge(xt_in[g], 16)
                k = P if g < 4 else DEC
                for q in range(2):
                    transposes(TB["xin"] + 2 * g + q, [xrows[0:k, g, (4 * q + i) * P:(4 * q + i + 1) * P] for i in range(4)])
            norm_sums("n0")
            pe.wait_ge(sm["gath_ready"], 1)
            transposes(TB["shift"], [ost[:, 0:9 * KT]])
            pe.wait_ge(sm["lo1_in"], 48)
            for j, (src, o, m, q) in enumerate(((bufA, 0, LW, 0), (bufB, LW, LA, 1), (bufA, LW + LA, P, 2), (bufA, LW + LA + P, LG - P, 2))):
                product(TB["lo1"] + j, [(lo1[:, kt, o:o + m], src[:, kt, :], [(sm["xm_ready"], KT * q + kt + 1)] if j < 3 else [])
                                        for kt in range(KT)], m=m)
            pe.wait_ge(sm["lo2_in"], 32)
            pe.wait_ge(sm["tile_read"], TB["lo1"] + 2)
            for n in range(KT):
                for q in range(2):
                    product(TB["lo2"] + 2 * n + q, [(lo2[:, q, n * P:(n + 1) * P], hwa[:, q, :], [])])
            gemm("k", bufB, (sm["xm_ready"], 3 * KT))
            gemm("r", bufA, (sm["xm_ready"], 4 * KT))
            gemm("v", bufB, (sm["xm_ready"], 5 * KT))
            for kt in range(KT):
                product(TB["kk"] + kt, [(con[:, C_HEAD:C_HEAD + P], tmp[:, kt % 2, :], [(sm["prep_sq"], kt + 1)])])

            def pairs(g):
                return range(4 * g, 4 * g + 4)

            def both(o, lhs, rhs, start=True, stop=True):
                for e in (0, 64):
                    ins = pe.matmul(o[e:e + 64], lhs[e:e + 64], rhs[e:e + 64], start=start, stop=stop)
                return ins

            def pbank(g, b, q, w, n=None):
                o = 2048 * g + 512 * b + w * q
                return ps[:, o:o + (n or w)]

            eye = con[:, C_IS:C_IS + 64]
            pe.wait_ge(sm["prep_done"], KT)
            pe.wait_ge(sm["tile_read"], TB["kk"] + KT)
            pe.wait_ge(sm["sd_in"], 16 * DB)
            for k in range(KT):
                for b in range(DB):
                    ins = both(ps[:, 512 * k + 64 * b:512 * k + 64 * b + 64], Snat[:, k, b, :], eye)
                ins.then_inc(sm["sd_ready"], 1)
            ev = [0, 0]
            pe.wait_ge(sm["sd_ready"], 2 * KT)

            def step(g, ins):
                ins.then_inc(mm_done[g], 1)

            def turn(g):
                if ev[g]:
                    pe.wait_ge(ev_done[g], ev[g])
                ev[g] += 1

            def factors(g, c, tok):
                turn(g)
                for i, k in enumerate(pairs(g)):
                    for e in (0, 64):
                        for q in range(2):
                            pe.matmul(pbank(g, 0, i, 128)[e:e + 64, 64 * q:64 * q + 64], ag[e:e + 64, k, tok], (kkb, rb)[q][e:e + 64, k, tok], start=True, stop=True)
                            pe.matmul(pbank(g, 1, i, 128)[e:e + 64, 64 * q:64 * q + 64], kb[e:e + 64, k, tok], (kkb, rb)[q][e:e + 64, k, tok], start=True, stop=True)
                    ins = both(pbank(g, 2, i, 64), kkb[:, k, tok], ag[:, k, tok])
                step(g, ins)

            def to_tokens(g, c, tok):
                turn(g)
                pe.wait_ge(sm["bar_ready"], 2 * (2 * c + g) + 2)
                for i, k in enumerate(pairs(g)):
                    both(pbank(g, 0, i, 64), vb[:, k, tok], eye)
                    both(pbank(g, 1, i, 64), bbar[:, c % 2, k, :], eye)
                    ins = both(pbank(g, 2, i, 64), kbar[:, c % 2, k, :], eye)
                step(g, ins)

            def level(g, last, part):
                turn(g)
                for i, k in enumerate(pairs(g)):
                    if part == 0:
                        ins = both(pbank(g, 0, i, 64), Mn[:, k, :], TT[:, k, :])
                    else:
                        ins = both(pbank(g, 1, i, 64), TI[:, k, :], Y[:, k, :])
                        if not last:
                            ins = both(pbank(g, 2, i, 64), Y[:, k, :], TI[:, k, :])
                step(g, ins)

            for c in range(NCH):
                tok = slice(CH * c, CH * c + CH)
                for g in range(2):
                    factors(g, c, tok)
                for g in range(2):
                    to_tokens(g, c, tok)
                for n in range(1, len(LEVELS)):
                    for part in range(2):
                        for g in range(2):
                            level(g, n == len(LEVELS) - 1, part)
                for g in range(2):
                    turn(g)
                    for i, k in enumerate(pairs(g)):
                        if c:
                            both(pbank(g, 0, i, 64), kkb[:, k, tok], S[:, k, :], stop=False)
                        ins = both(pbank(g, 0, i, 64), MkT[:, k, 0:64], Vt[:, k, :], start=c == 0)
                    step(g, ins)
                for g in range(2):
                    turn(g)
                    for i, k in enumerate(pairs(g)):
                        ins = both(pbank(g, 1, i, 64), TT[:, k, :], Rm[:, k, :])
                    step(g, ins)
                for g in range(2):
                    turn(g)
                    for i, k in enumerate(pairs(g)):
                        both(pbank(g, 2, i, 64), Bt[:, k, :], SA[:, k, :], stop=False)
                        both(pbank(g, 2, i, 64), Ktk[:, k, :], Vt[:, k, :], start=False)
                        both(pbank(g, 3, i, 64), SA[:, k, :], MbT[:, k, 64:128], stop=False)
                        ins = both(pbank(g, 3, i, 64), Vt[:, k, :], MkT[:, k, 64:128], start=False, stop=c == 0)
                        if c:
                            ins = both(pbank(g, 3, i, 64), S[:, k, :], rb[:, k, tok], start=False)
                    step(g, ins)
            c = NCH
            tok = slice(SEQ, T)
            for g in range(2):
                factors(g, c, tok)
            for g in range(2):
                to_tokens(g, c, tok)
            for n in (1, 2):
                for part in range(2):
                    for g in range(2):
                        level(g, n == 2, part)
            for i in range(4):
                for g in range(2):
                    turn(g)
                    k = 4 * g + i
                    am = tmp[:, 2 * g + i % 2, 0:512].rearrange("p (b t) -> p b t", b=DB)
                    for b in range(DB):
                        both(pbank(g, 0, i, 64), am[:, b, :], Sd[:, k, b, :], start=b == 0, stop=False)
                    ins = both(pbank(g, 0, i, 64), MkT[:, k, 0:64], Vt[:, k, :], start=False)
                    step(g, ins)
            for g in range(2):
                turn(g)
                for i, k in enumerate(pairs(g)):
                    ins = both(pbank(g, 1, i, 64), TT[:, k, :], Rm[:, k, :])
                step(g, ins)
            for i in range(4):
                for g in range(2):
                    turn(g)
                    k = 4 * g + i
                    o = pbank(g, 3, 0, 64)
                    both(o, SA[:, k, :], MbT[:, k, 64:128], stop=False)
                    both(o, Vt[:, k, :], MkT[:, k, 64:128], start=False, stop=False)
                    for b in range(DB):
                        t = slice(8 * b, 8 * b + 8)
                        both(o[:, t], Sd[:, k, b, :], rb[:, k, SEQ + 8 * b:SEQ + 8 * b + 8], start=False, stop=b == DB - 1)
                    o = pbank(g, 2, 0, 512)
                    both(o, Bt[:, k, :], tmp[:, 2 * g, 0:512], stop=False)
                    ins = both(o, Ktk[:, k, :], tmp[:, 2 * g + 1, 0:512], start=False)
                    step(g, ins)
            for g in range(2):
                pe.wait_ge(ev_done[g], ev[g])
            for k in range(KT):
                ins = both(ps[:, 64 * k:64 * k + 64], S[:, k, :], eye)
            ins.then_inc(sm["snat_ready"], 1)
            for k in range(KT):
                o = 512 * ((k + 1) % 8)
                if k == 7:
                    pe.wait_ge(sm["state_out"], 1)
                for b in range(DB):
                    ins = both(ps[:, o + 64 * b:o + 64 * b + 64], Sd[:, k, b, :], eye)
                ins.then_inc(sm["snat_ready"], 1)
            pe.wait_ge(sm["state_out"], 1 + KT)
            pe.wait_ge(sm["lg2_in"], 32)
            for kt in range(KT):
                t = TB["post"] + 4 * kt
                product(t, [(con[:, C_HEAD:C_HEAD + P], yg[:, kt, :], [])])
                product(t + 1, [(con[:, C_HEAD:C_HEAD + P], tmp[:, 0, :], [(sm["post_a"], kt + 1)])])
                product(t + 2, [(con[:, C_HEAD:C_HEAD + P], tmp[:, 1, :], [(sm["post_v"], 2 * kt + 1)])])
                product(t + 3, [(lg2[:, 0, kt * P:(kt + 1) * P], hg[:, 0, :], []),
                                (lg2[0:LG - P, 1, kt * P:(kt + 1) * P], hg[0:LG - P, 1, :], [])])
            gemm("wo", yg, (sm["z_ready"], 0))
            norm_sums("n1")
            pe.wait_ge(sm["fst_in"], 32)
            state_turns("fst0")
            norm_sums("n2")

            def ffn(l):
                w = FF[l]
                t0, w0 = TB[f"up{l}"], WB[f"up{l}"]
                pe.wait_ge(sm["h_ready"], KT * (2 if l == 0 else 4))
                with pe.Fori(0, FT // 2) as i:
                    for j in range(4):
                        s = tset(t0 + j)
                        pe.wait_ge(sm["tile_read"], i * 4 + (t0 + j - 3))
                        pe.wait_ge(w_in[j], i * 16 + 16 * (w0 // RING + 1))
                        for kt in range(KT):
                            lhs = ring[:, j, kt, :]
                            pe.matmul(ps[:, s:s + SEQ], lhs, h[:, kt, 0:SEQ], start=kt == 0, stop=kt == KT - 1)
                            ins = pe.matmul(ps[:, s + SEQ:s + T], lhs, h[:, kt, SEQ:T], start=kt == 0, stop=kt == KT - 1)
                        ins.then_inc(sm["tile_full"], 1)
                for n in range(KT):
                    terms = []
                    for f in range(FT):
                        p = [(wo_in[l][n % 2], 16 * (n // 2 + 1))] if f == 0 else []
                        if n == 0:
                            p.append((w["hid_ready"], f + 1))
                        terms.append((wos[:, n % 2, f, :], hid[:, f, :], p))
                    product(TB[f"down{l}"] + n, terms)
                pe.wait_ge(w["tails"], 4 * FT)
                for t in range(2):
                    transposes(TB[f"fo{l}"] + t, [fo[:, 7 * g:min(7 * g + 7, 2 * FT), :].rearrange("p f n -> p (f n)")
                                                  for g in range(4 * t, min(4 * t + 4, 7))])

            ffn(0)
            norm_sums("n3")
            pe.wait_ge(sm["gst_in"], 48)
            for t in range(4):
                transposes(TB["gst"] + t, [grows[:, g, :] for g in range(4 * t, min(4 * t + 4, NGG))])
            state_turns("fst1")
            norm_sums("n4")
            gemm("glu", h, (sm["h_ready"], 2 * KT))
            pe.wait_ge(sm["gath_ready"], 2)
            gathp = arena[:, A_H:A_H + 240]
            gaths = arena[:, A_H + 240:A_H + 752]
            transposes(TB["go"], [gathp[:, 0:120], gathp[:, 120:240]])
            transposes(TB["go"] + 1, [gaths[:, P * q:P * q + P] for q in range(4)])
            product(TB["ln"], [(con[:, C_MEAN:C_MEAN + P], cvo[:, kt, :], [(sm["conv_done"], kt + 1)]) for kt in range(KT)])
            norm_sums("ln", first=1)
            gemm("co", cvo, (sm["z_ready"], KT))
            norm_sums("n5")
            norm_sums("n6")
            ffn(1)
            norm_sums("n7")
            for g in range(5):
                k = P if g < 4 else DEC
                for q in range(2):
                    if g == 0 and q == 0:
                        pe.wait_ge(sm["x_ready"], 4 * KT)
                    transposes(TB["yout"] + 2 * g + q, [x[:, 4 * q + i, g * P:g * P + k] for i in range(4)])

        @block.scalar
        def _(act):
            done = [0]
            read = [0]

            def take(t, ins=None):
                act.wait_ge(sm["tile_full"], t + 1)

            def freed(ins):
                ins.then_inc(sm["tile_read"], 1)

            f = nc.scalar.activation
            norm_i = [0]

            def norm(name, src, pre, eps=0, first=0):
                n = norm_i[0]
                for kt in range(KT):
                    if pre is not None:
                        act.wait_ge(pre[0], pre[1] + kt + 1)
                    if kt >= 2:
                        act.wait_ge(sm["sq_used"], (KT - 1) * n + kt - 1)
                    f(tmp[:, kt % 2, :], src[:, kt, :], ACT.Square).then_inc(sm["sq_ready"], 1)
                t = TB[name] + first
                take(t)
                freed(f(tmp[:, 2, :], bank2(t), ACT.Sqrt, bias=con[:, C_EPS + eps:C_EPS + eps + 1]))
                norm_i[0] += 1

            for t in range(2):
                m = min(512, NPC - 512 * t)
                take(TB["par"] + t)
                freed(f(par[:, 512 * t:512 * t + m], bank2(TB["par"] + t, m), ACT.Copy))

            def state_cols(name):
                for t in range(2):
                    m = min(512, NFS - 512 * t)
                    take(TB[name] + t)
                    freed(f(fst[:, 512 * t:512 * t + m], bank2(TB[name] + t, m), ACT.Copy))

            for g in range(5):
                k = P if g < 4 else DEC
                for q in range(2):
                    t = TB["xin"] + 2 * g + q
                    take(t)
                    src = ps[:, tset(t):tset(t) + 512].rearrange("p (i n) -> p i n", n=P)[:, :, 0:k]
                    freed(f(x[:, 4 * q:4 * q + 4, g * P:g * P + k], src, ACT.Copy))
            act.wait_ge(sm["tile_read"], TB["xin"] + 10)
            norm("n0", x, None)
            take(TB["shift"])
            freed(f(ost[0:9 * KT, 128:256], ps[0:9 * KT, tset(TB["shift"]):tset(TB["shift"]) + P], ACT.Copy))
            t = TB["lo1"]
            take(t)
            freed(f(hwa[:, 0, :], bank2(t, m=LW), ACT.Tanh))
            take(t + 1)
            freed(f(hwa[:, 1, :], bank2(t + 1, m=LA), ACT.Copy))
            take(t + 2)
            freed(f(hg[:, 0, :], bank2(t + 2), ACT.Sigmoid))
            take(t + 3)
            freed(f(hg[0:LG - P, 1, :], bank2(t + 3, m=LG - P), ACT.Sigmoid))
            for n in range(KT):
                for q, (dst, b) in enumerate(((sg, "rwkv_w0"), (ag, "rwkv_a0"))):
                    t = TB["lo2"] + 2 * n + q
                    take(t)
                    freed(f(dst[:, n, :], bank2(t), ACT.Sigmoid, bias=pcol(b, n)))
            for name, dst in (("k", kb), ("r", rb), ("v", vb)):
                for n in range(KT):
                    take(TB[name] + n)
                    freed(f(dst[:, n, :], bank2(TB[name] + n), ACT.Copy))
            for kt in range(KT):
                act.wait_ge(sm["prep_s"], kt + 1)
                if kt >= 2:
                    act.wait_ge(sm["tile_full"], TB["kk"] + kt - 1)
                f(tmp[:, kt % 2, :], kkb[:, kt, :], ACT.Square).then_inc(sm["prep_sq"], 1)
                if kt >= 1:
                    prev = kt - 1
                    if prev >= 2:
                        act.wait_ge(sm["prep_e"], prev - 1)
                    take(TB["kk"] + prev)
                    freed(f(tmp[:, 2 + prev % 2, :], bank2(TB["kk"] + prev), ACT.Sqrt))
            act.wait_ge(sm["prep_e"], KT - 2)
            take(TB["kk"] + KT - 1)
            freed(f(tmp[:, 2 + (KT - 1) % 2, :], bank2(TB["kk"] + KT - 1), ACT.Sqrt))
            for kt in range(KT):
                act.wait_ge(sm["wide_ready"], kt + 1)
                s = 2 * (kt % 2)
                f(tmp[:, s + 1, :], tmp[:, s, :], ACT.Exp, scale=-LAM).then_inc(sm["v_ready"], 1)
                f(sg[:, kt, :], sg[:, kt, :], ACT.Exp, scale=-LAM).then_inc(sm["v_ready"], 1)
                f(tmp[:, s, :], tmp[:, s, :], ACT.Exp, scale=LAM).then_inc(sm["v_ready"], 1)
            for k in range(KT):
                act.wait_ge(sm["sd_ready"], KT)
                f(Sd[:, k], ps[:, 512 * k:512 * k + 512].rearrange("p (b n) -> p b n", b=DB), ACT.Copy).then_inc(sm["sd_ready"], 1)
            act.wait_ge(sm["snat_ready"], 1)
            f(ost[:, 256:768], ps[:, 0:512], ACT.Copy).then_inc(sm["state_out"], 1)
            for k in range(KT):
                act.wait_ge(sm["snat_ready"], k + 2)
                o = 512 * ((k + 1) % 8)
                f(Snat[:, k], ps[:, o:o + 512].rearrange("p (b n) -> p b n", b=DB), ACT.Copy).then_inc(sm["state_out"], 1)
            for kt in range(KT):
                t = TB["post"] + 4 * kt
                take(t)
                if kt:
                    act.wait_ge(sm["z_ready"], kt)
                freed(f(tmp[:, 2, :], bank2(t), ACT.Copy, scale=1.0 / HS))
                act.wait_ge(sm["post_v"], 2 * kt + 2)
                f(tmp[:, 0, :], yg[:, kt, :], ACT.Square).then_inc(sm["post_a"], 1)
                take(t + 1)
                freed(f(tmp[:, 2, :], bank2(t + 1), ACT.Sqrt, scale=1.0 / HS, bias=con[:, C_EPS + 2:C_EPS + 3]))
                take(t + 2)
                freed(f(tmp[:, 3, :], bank2(t + 2), ACT.Copy))
                take(t + 3)
                freed(f(tmp[:, 0, :], bank2(t + 3), ACT.Copy))

            def outputs(name):
                for n in range(KT):
                    take(TB[name] + n)
                    freed(f(mb[:, n, :], bank2(TB[name] + n), ACT.Copy))

            outputs("wo")
            norm("n1", mb, (sm["tile_read"], TB["wo"]))
            state_cols("fst0")
            norm("n2", x, (sm["x_ready"], 0))

            def ffn(l):
                w = FF[l]
                t0 = TB[f"up{l}"]
                with act.Fori(0, FT // 2) as i:
                    for q in range(2):
                        for z in range(2):
                            j = 2 * q + z
                            act.wait_ge(sm["tile_full"], i * 4 + (t0 + j + 1))
                            act.wait_ge(w["hist_ready"], i * 4 + (j + 1))
                            s = tset(t0 + j)
                            f(raw[:, j, 2:2 + SEQ], ps[:, s:s + SEQ], ACT.Copy)
                            dst = raw[:, j, 2 + SEQ:RAW].rearrange("p (b t) -> p b t", b=DB)[:, :, 2:2 + DS]
                            freed(f(dst, ps[:, s + SEQ:s + T].rearrange("p (b t) -> p b t", b=DB), ACT.Copy))
                        act.wait_ge(w["conv_ready"], i * 4 + (2 * q + 1))
                        f(cv[:, 2 * q, :], cv[:, 2 * q, :], ACT.Silu).then_inc(w["gate_ready"], 1)
                outputs(f"down{l}")
                for t in range(2):
                    take(TB[f"fo{l}"] + t)
                    if l == 1 and t == 0:
                        act.wait_ge(sm["out_done"], 16 * (16 + 1 + 8 + 88 + KT * (1 + DB) + 1))
                    if l == 0 and t == 0:
                        act.wait_ge(sm["out_done"], 16 * (16 + 1 + 8))
                    s = tset(TB[f"fo{l}"] + t)
                    if t == 0:
                        ins = f(ost[0:126, 0:512], ps[0:126, s:s + 512], ACT.Copy)
                    else:
                        f(ost[0:126, 512:768], ps[0:126, s:s + 256], ACT.Copy)
                        ins = f(ost[0:36, 768:896], ps[0:36, s + 256:s + 384], ACT.Copy)
                    freed(ins)

            ffn(0)
            norm("n3", mb, None)
            for t in range(4):
                m = min(512, NGS - 512 * t)
                take(TB["gst"] + t)
                freed(f(gst[:, 512 * t:512 * t + m], bank2(TB["gst"] + t, m), ACT.Copy))
            state_cols("fst1")
            norm("n4", x, (sm["x_ready"], KT))
            for n in range(KT):
                ta, tb = TB["glu"] + 2 * n, TB["glu"] + 2 * n + 1
                if n >= 1:
                    act.wait_ge(sm["glu_ready"], n)
                take(ta)
                freed(f(gsig[:, 1, :], bank2(ta), ACT.Identity, bias=pcol("conv_b_in", n)))
                take(tb)
                freed(f(gsig[:, 0, :], bank2(tb), ACT.Sigmoid, bias=pcol("conv_b_in", KT + n)))
            take(TB["go"])
            act.wait_ge(sm["out_done"], 16 * (16 + 1 + 8 + 88))
            s = tset(TB["go"])
            freed(f(ost[0:120, 0:256], ps[0:120, s:s + 256], ACT.Copy))
            take(TB["go"] + 1)
            freed(f(ost[:, 256:768], bank2(TB["go"] + 1, 512), ACT.Copy))
            take(TB["ln"])
            freed(f(tmp[:, 3, :], bank2(TB["ln"]), ACT.Copy))
            norm("ln", cvo, (sm["ln_v"], 0), eps=1, first=1)
            for kt in range(KT):
                act.wait_ge(sm["ln_v"], KT + kt + 1)
                f(cvo[:, kt, :], cvo[:, kt, :], ACT.Silu, scale=pcol("conv_ln_w", kt), bias=pcol("conv_ln_b", kt)).then_inc(sm["z_ready"], 1)
            for n in range(KT):
                take(TB["co"] + n)
                freed(f(mb[:, n, :], bank2(TB["co"] + n), ACT.Identity, bias=pcol("conv_b_out", n)))
            norm("n5", mb, (sm["tile_read"], TB["co"]))
            norm("n6", x, (sm["x_ready"], 2 * KT))
            ffn(1)
            norm("n7", mb, None)
            for g in range(5):
                k = P if g < 4 else DEC
                for q in range(2):
                    t = TB["yout"] + 2 * g + q
                    take(t)
                    freed(f(xrows[0:k, g, 512 * q:512 * q + 512], ps[0:k, tset(t):tset(t) + 512], ACT.Copy))

        @block.vector
        def _(dve):
            done = [0]
            v = nc.vector

            def seq(ins):
                ins.then_inc(sm["vec_done"], 1)
                done[0] += 1

            def after():
                if done[0]:
                    dve.wait_ge(sm["vec_done"], done[0])

            def norm_scale(name, first=0):
                dve.wait_ge(sm["tile_read"], TB[name] + first + 1)
                seq(v.reciprocal(tmp[:, 2, :], tmp[:, 2, :]))
                after()

            def prenorm(name, n):
                norm_scale(name)
                for kt in range(KT):
                    v.scalar_tensor_tensor(h[:, kt, :], x[:, kt, :], gain(n, kt), tmp[:, 2, :], ALU.mult, ALU.mult)\
                        .then_inc(sm["h_ready"], 1)

            def postnorm(name, n):
                norm_scale(name)
                for kt in range(KT):
                    seq(v.scalar_tensor_tensor(mb[:, kt, :], mb[:, kt, :], gain(n, kt), tmp[:, 2, :], ALU.mult, ALU.mult))
                    after()
                    v.tensor_tensor(x[:, kt, :], x[:, kt, :], mb[:, kt, :], ALU.add).then_inc(sm["x_ready"], 1)

            dve.wait_ge(sm["const_in"], 16)
            prenorm("n0", 0)
            dve.wait_ge(sm["h_ready"], KT)
            hd = h[:, :, SEQ:T].rearrange("p k (b t) -> p k b t", b=DB)
            xd = xx[:, :, SEQ:T].rearrange("p k (b t) -> p k b t", b=DB)
            go = ost[:, 0:9 * KT].rearrange("p (k c) -> p k c", c=9)
            seq(v.tensor_copy(go[:, :, 0:1], h[:, :, SEQ - 1:SEQ]))
            v.tensor_copy(go[:, :, 1:9], hd[:, :, :, DS - 1]).then_inc(sm["gath_ready"], 1)
            shift = par[:, PCOL["state_rwkv_shift"]:PCOL["state_rwkv_shift"] + DB * KT].rearrange("p (b k) -> p k b", b=DB)
            seq(v.tensor_tensor(xx[:, :, 1:SEQ], h[:, :, 0:SEQ - 1], h[:, :, 1:SEQ], ALU.subtract))
            seq(v.tensor_scalar(xx[:, :, 0:1], h[:, :, 0:1], -1.0, None, ALU.mult))
            for kt in range(KT):
                seq(v.tensor_tensor(xd[:, kt, :, 1:DS], hd[:, kt, :, 0:DS - 1], hd[:, kt, :, 1:DS], ALU.subtract))
            seq(v.tensor_tensor(xd[:, :, :, 0], shift, hd[:, :, :, 0], ALU.subtract))
            seq(v.tensor_scalar(omka[:], par[:, PCOL["rwkv_k_a"]:PCOL["rwkv_k_a"] + KT], -1.0, 1.0, ALU.mult, ALU.add))
            after()
            free = {2: TB["lo1"] + 1, 3: TB["lo1"] + 2, 4: TB["lo1"] + 4, 5: TB["k"] + KT}
            for q, m in enumerate((1, 4, 5, 2, 0, 3)):
                if q in free:
                    dve.wait_ge(sm["tile_full"], free[q])
                for kt in range(KT):
                    v.scalar_tensor_tensor((bufA, bufB)[q % 2][:, kt, :], xx[:, kt, :], pcol("rwkv_mix", m * KT + kt),
                                           h[:, kt, :], ALU.mult, ALU.add).then_inc(sm["xm_ready"], 1)
            dve.wait_ge(sm["xm_ready"], 6 * KT)
            dve.wait_ge(sm["tile_read"], TB["k"] + KT)

            def unit_key(kt):
                dve.wait_ge(sm["tile_read"], TB["kk"] + kt + 1)
                t = tmp[:, 2 + kt % 2, :]
                seq(v.tensor_scalar(t, t, 1e-12, None, ALU.max))
                after()
                seq(v.reciprocal(t, t))
                after()
                v.tensor_tensor(kkb[:, kt, :], kkb[:, kt, :], t, ALU.mult).then_inc(sm["prep_e"], 1)

            for kt in range(KT):
                v.tensor_scalar(kkb[:, kt, :], kb[:, kt, :], pcol("rwkv_k_k", kt), None, ALU.mult).then_inc(sm["prep_s"], 1)
            for kt in range(KT):
                unit_key(kt)
            dve.wait_ge(sm["prep_e"], KT)
            def sums(kt):
                t = tmp[:, 2 * (kt % 2), :]
                u = tmp[:, 2 * (kt % 2) + 1, :]
                after()
                if kt >= 2:
                    dve.wait_ge(sm["prep_done"], kt - 1)
                seq(v.tensor_scalar(u, ag[:, kt, :], pcol("rwkv_k_a", kt), omka[:, kt:kt + 1], ALU.mult, ALU.add))
                seq(v.tensor_tensor_scan(t, con[:, C_SCAN:C_SCAN + T], sg[:, kt, :], 0.0, ALU.mult, ALU.add))
                after()
                seq(v.tensor_tensor(kb[:, kt, :], kb[:, kt, :], u, ALU.mult))
                seq(v.scalar_tensor_tensor(ag[:, kt, :], kkb[:, kt, :], -1.0, ag[:, kt, :], ALU.mult, ALU.mult))
                after()
                v.tensor_tensor(sg[:, kt, :], t, sg[:, kt, :], ALU.subtract).then_inc(sm["wide_ready"], 1)

            def scale(kt):
                t, u = tmp[:, 2 * (kt % 2), :], tmp[:, 2 * (kt % 2) + 1, :]
                dve.wait_ge(sm["v_ready"], 3 * kt + 3)
                seq(v.tensor_tensor(kkb[:, kt, :], kkb[:, kt, :], sg[:, kt, :], ALU.mult))
                seq(v.tensor_tensor(rb[:, kt, :], rb[:, kt, :], u, ALU.mult))
                seq(v.tensor_tensor(kb[:, kt, :], kb[:, kt, :], t, ALU.mult))
                seq(v.tensor_tensor(ag[:, kt, :], ag[:, kt, :], t, ALU.mult))
                seq(v.tensor_copy(pend[:, kt, 0:NCH], u[:, CH - 1:SEQ:CH]))
                after()
                v.tensor_copy(pend[:, kt, NCH:NCH + DB], u[:, SEQ + DS - 1:T:DS]).then_inc(sm["prep_done"], 1)

            sums(0)
            for kt in range(KT):
                if kt + 1 < KT:
                    sums(kt + 1)
                scale(kt)
            ident8 = con[:, C_IS:C_IS + 64].unsqueeze(1).to_broadcast([P, 4, 64])
            dve.wait_ge(sm["prep_done"], KT)
            dve.wait_ge(sm["sd_ready"], 2 * KT)
            seq(v.memset(S, 0.0))
            mm = [0, 0]

            def bk(g, b, n, w):
                o = 2048 * g + 512 * b
                return ps[:, o:o + n * w].rearrange("p (k n) -> p k n", n=w)

            def turn(g):
                mm[g] += 1
                dve.wait_ge(mm_done[g], mm[g])

            def fin(g, ins):
                ins.then_inc(ev_done[g], 1)

            def bc(col, n=64, m=4):
                return con[:, col:col + n].unsqueeze(1).to_broadcast([P, m, n])

            def factors(g, mask):
                turn(g)
                k = slice(4 * g, 4 * g + 4)
                seq(v.tensor_tensor(MbT[:, k, :], bk(g, 0, 4, 128), bc(mask, 128), ALU.mult))
                seq(v.tensor_tensor(MkT[:, k, :], bk(g, 1, 4, 128), bc(mask, 128), ALU.mult))
                seq(v.tensor_copy(Mn[:, k, :], bk(g, 2, 4, 64)))
                after()
                seq(v.tensor_tensor(TT[:, k, :], MbT[:, k, 0:64], bc(C_LVL), ALU.mult))
                seq(v.tensor_tensor(TI[:, k, :], Mn[:, k, :], bc(C_LOW1), ALU.mult))
                after()
                seq(v.tensor_tensor(TT[:, k, :], TT[:, k, :], ident8, ALU.add))
                after()
                fin(g, v.tensor_tensor(TI[:, k, :], TI[:, k, :], ident8, ALU.add))

            def to_tokens(g):
                turn(g)
                k = slice(4 * g, 4 * g + 4)
                seq(v.tensor_copy(Vt[:, k, :], bk(g, 0, 4, 64)))
                seq(v.tensor_copy(Bt[:, k, :], bk(g, 1, 4, 64)))
                after()
                fin(g, v.tensor_copy(Ktk[:, k, :], bk(g, 2, 4, 64)))

            def level(g, n, last, part):
                turn(g)
                k = slice(4 * g, 4 * g + 4)
                if part == 0:
                    fin(g, v.tensor_tensor(Y[:, k, :], bk(g, 0, 4, 64), bc(C_LVL + 64 * n), ALU.mult))
                else:
                    if not last:
                        seq(v.tensor_tensor(TI[:, k, :], TI[:, k, :], bk(g, 2, 4, 64), ALU.add))
                        after()
                    fin(g, v.tensor_tensor(TT[:, k, :], TT[:, k, :], bk(g, 1, 4, 64), ALU.add))

            def both_groups(fn, *args):
                for g in range(2):
                    fn(g, *args)

            def copy_bank(g, dst, b):
                turn(g)
                fin(g, v.tensor_copy(dst[:, 4 * g:4 * g + 4, :], bk(g, b, 4, 64)))

            for c in range(NCH):
                both_groups(factors, C_MASK)
                both_groups(to_tokens)
                for n in range(1, len(LEVELS)):
                    for part in range(2):
                        both_groups(level, n, n == len(LEVELS) - 1, part)
                both_groups(copy_bank, Rm, 0)
                both_groups(copy_bank, SA, 1)
                for g in range(2):
                    turn(g)
                    k = slice(4 * g, 4 * g + 4)
                    after()
                    seq(v.tensor_copy(yb[:, k, CH * c:CH * c + CH], bk(g, 3, 4, 64)))
                    seq(v.tensor_tensor(S[:, k, :], S[:, k, :], pend[:, k, c:c + 1].to_broadcast([P, 4, 64]), ALU.mult))
                    after()
                    fin(g, v.tensor_tensor(S[:, k, :], S[:, k, :], bk(g, 2, 4, 64), ALU.add))
            both_groups(factors, C_MASKD)
            both_groups(to_tokens)
            own = con[:, C_B8:C_B8 + 8].unsqueeze(2).to_broadcast([P, DB, 64])

            def masked_a(g, i):
                flat = tmp[:, 2 * g + i % 2, 0:512]
                am = flat.rearrange("p (b c t) -> p b c t", b=DB, t=DS)
                src = kkb[:, 4 * g + i, SEQ:T].rearrange("p (c t) -> p c t", t=DS)
                seq(v.memset(flat, 0.0))
                after()
                for b in range(DB):
                    seq(v.tensor_copy(am[:, b, b, :], src[:, b, :]))
                after()

            def masked_rows(g, i):
                for m, src in enumerate((SA, Vt)):
                    o = tmp[:, 2 * g + m, 0:512].rearrange("p (b n) -> p b n", b=DB)
                    seq(v.tensor_tensor(o, src[:, 4 * g + i, :].unsqueeze(1).to_broadcast([P, DB, 64]), own, ALU.mult))
                after()

            for n in (1, 2):
                for part in range(2):
                    for g in range(2):
                        if n == 2 and part == 1:
                            masked_a(g, 0)
                        level(g, n, n == 2, part)
            for i in range(4):
                for g in range(2):
                    turn(g)
                    if i < 3:
                        masked_a(g, i + 1)
                    fin(g, v.tensor_copy(Rm[:, 4 * g + i, :], bk(g, 0, 4, 64)[:, i, :]))
            for g in range(2):
                turn(g)
                seq(v.tensor_copy(SA[:, 4 * g:4 * g + 4, :], bk(g, 1, 4, 64)))
                after()
                masked_rows(g, 0)
                fin(g, v.tensor_copy(omka[:, g:g + 1], omka[:, g:g + 1]))
            for i in range(4):
                for g in range(2):
                    k = 4 * g + i
                    turn(g)
                    seq(v.tensor_copy(yb[:, k, SEQ:T], bk(g, 3, 1, 64)[:, 0, :]))
                    if i < 3:
                        masked_rows(g, i + 1)
                    seq(v.tensor_tensor(Sd[:, k], Sd[:, k], pend[:, k, NCH:NCH + DB].unsqueeze(2).to_broadcast([P, DB, 64]), ALU.mult))
                    after()
                    fin(g, v.tensor_tensor(Sd[:, k], Sd[:, k], bk(g, 2, DB, 64), ALU.add))
            dve.wait_ge(sm["state_out"], 1 + KT)
            for kt in range(KT):
                t = TB["post"] + 4 * kt
                if kt:
                    dve.wait_ge(sm["z_ready"], kt)
                v.scalar_tensor_tensor(tmp[:, 1, :], rb[:, kt, :], pcol("rwkv_r_k", kt), kb[:, kt, :], ALU.mult, ALU.mult)\
                    .then_inc(sm["post_v"], 1)
                dve.wait_ge(sm["tile_read"], t + 1)
                v.tensor_tensor(yg[:, kt, :], yg[:, kt, :], tmp[:, 2, :], ALU.subtract).then_inc(sm["post_v"], 1)
                dve.wait_ge(sm["tile_read"], t + 4)
                seq(v.reciprocal(tmp[:, 2, :], tmp[:, 2, :]))
                seq(v.tensor_tensor(tmp[:, 3, :], tmp[:, 3, :], vb[:, kt, :], ALU.mult))
                after()
                seq(v.scalar_tensor_tensor(yg[:, kt, :], yg[:, kt, :], pcol("rwkv_lnx_w", kt), tmp[:, 2, :], ALU.mult, ALU.mult))
                after()
                seq(v.scalar_tensor_tensor(yg[:, kt, :], yg[:, kt, :], pcol("rwkv_lnx_b", kt), tmp[:, 3, :], ALU.add, ALU.add))
                after()
                v.tensor_tensor(yg[:, kt, :], yg[:, kt, :], tmp[:, 0, :], ALU.mult).then_inc(sm["z_ready"], 1)
            postnorm("n1", 1)
            dve.wait_ge(sm["x_ready"], KT)
            prenorm("n2", 2)

            def ffn(l):
                w = FF[l]
                chain = w["cvd"]
                per = 4 * 5
                for z in range(4):
                    v.memset(raw[:, z, 0:2], 0.0).then_inc(w["no_hist"], 1)
                with dve.Fori(0, FT // 2) as i:
                    for q in range(2):
                        for z in range(2):
                            j = 2 * q + z
                            dve.wait_ge(sm["tile_read"], i * 4 + (TB[f"up{l}"] + j + 1))
                            rp = raw[:, j, 0:2 + SEQ]
                            rd = raw[:, j, 2 + SEQ:RAW].rearrange("p (b t) -> p b t", b=DB)
                            cd = cv[:, j, SEQ:T].rearrange("p (b t) -> p b t", b=DB)

                            def tap(n):
                                o = PCOL["ffn_dw_w"] + (3 * l + n) * 2 * FT + z * FT + q
                                return par[:, bass.ds(i * 2 + o, 1)]

                            bias = par[:, bass.ds(i * 2 + (PCOL["ffn_dw_b"] + l * 2 * FT + z * FT + q), 1)]
                            v.tensor_scalar(cv[:, j, 0:SEQ], rp[:, 0:SEQ], tap(0), bias, ALU.mult, ALU.add).then_inc(chain, 1)
                            v.tensor_scalar(cd, rd[:, :, 0:DS], tap(0), bias, ALU.mult, ALU.add).then_inc(chain, 1)
                            for n in (1, 2):
                                dve.wait_ge(chain, i * per + (5 * j + 2 * n))
                                v.scalar_tensor_tensor(cv[:, j, 0:SEQ], rp[:, n:n + SEQ], tap(n), cv[:, j, 0:SEQ], ALU.mult, ALU.add).then_inc(chain, 1)
                                ins = v.scalar_tensor_tensor(cd, rd[:, :, n:n + DS], tap(n), cd, ALU.mult, ALU.add)
                                ins.then_inc(chain if n == 1 else w["conv_ready"], 1)
                        dve.wait_ge(w["gate_ready"], i * 2 + (q + 1))
                        dve.wait_ge(w["conv_ready"], i * 4 + (2 * q + 2))
                        dve.wait_ge(chain, i * per + (10 * q + 10))
                        v.tensor_tensor(hid[:, bass.ds(i * 2 + q, 1), :], cv[:, 2 * q, :], cv[:, 2 * q + 1, :], ALU.mult)\
                            .then_inc(w["hid_ready"], 1)

            ffn(0)
            postnorm("n3", 3)
            dve.wait_ge(sm["x_ready"], 2 * KT)
            prenorm("n4", 4)
            gd = gb[:, :, NSTATE + SEQ:GB].rearrange("p k (b t) -> p k b t", b=DB)
            dve.wait_ge(sm["tile_read"], TB["fst1"] + 2)
            seq(v.memset(gb[:, :, 0:NSTATE], 0.0))
            gs = gst.rearrange("p (b w k) -> p k b w", b=DB, k=KT)
            for kt in range(KT):
                seq(v.tensor_copy(gd[:, kt, :, 0:NSTATE], gs[:, kt]))

            def glu(kt):
                dve.wait_ge(sm["tile_read"], TB["glu"] + 2 * kt + 2)
                seq(v.tensor_tensor(gb[:, kt, NSTATE:NSTATE + SEQ], gsig[:, 1, 0:SEQ], gsig[:, 0, 0:SEQ], ALU.mult))
                after()
                v.tensor_tensor(gd[:, kt, :, NSTATE:NSTATE + DS], gsig[:, 1, SEQ:T].rearrange("p (b t) -> p b t", b=DB),
                                gsig[:, 0, SEQ:T].rearrange("p (b t) -> p b t", b=DB), ALU.mult).then_inc(sm["glu_ready"], 1)

            def dwconv(kt):
                cd = cvo[:, kt, SEQ:T].rearrange("p (b t) -> p b t", b=DB)
                dve.wait_ge(sm["glu_ready"], kt + 1)
                for n in range(CW):
                    w = pcol("conv_dw_w", n * KT + kt)
                    after()
                    for dst, src in ((cvo[:, kt, 0:SEQ], gb[:, kt, n:n + SEQ]), (cd, gd[:, kt, :, n:n + DS])):
                        if n == 0:
                            ins = v.tensor_scalar(dst, src, w, pcol("conv_dw_b", kt), ALU.mult, ALU.add)
                        else:
                            ins = v.scalar_tensor_tensor(dst, src, w, dst, ALU.mult, ALU.add)
                        if n == CW - 1 and dst is cd:
                            ins.then_inc(sm["conv_done"], 1)
                        else:
                            seq(ins)

            glu(0)
            for kt in range(KT):
                if kt + 1 < KT:
                    glu(kt + 1)
                dwconv(kt)
            dve.wait_ge(sm["tile_full"], TB["glu"] + 2 * KT)
            dve.wait_ge(sm["glu_ready"], KT)
            gp = arena[:, A_H:A_H + 240].rearrange("p (k w) -> p k w", w=NSTATE)
            gt = arena[:, A_H + 240:A_H + 752].rearrange("p (k b t) -> p k b t", k=KT, b=DB)
            seq(v.tensor_copy(gp, gb[:, :, SEQ:SEQ + NSTATE]))
            for kt in range(KT):
                ins = v.tensor_copy(gt[:, kt], gd[:, kt, :, NSTATE:NSTATE + DS])
                if kt < KT - 1:
                    seq(ins)
            ins.then_inc(sm["gath_ready"], 1)
            dve.wait_ge(sm["tile_read"], TB["ln"] + 1)
            dve.wait_ge(sm["conv_done"], KT)
            for kt in range(KT):
                v.tensor_tensor(cvo[:, kt, :], cvo[:, kt, :], tmp[:, 3, :], ALU.subtract).then_inc(sm["ln_v"], 1)
            norm_scale("ln", 1)
            dve.wait_ge(sm["ln_v"], KT)
            for kt in range(KT):
                v.tensor_tensor(cvo[:, kt, :], cvo[:, kt, :], tmp[:, 2, :], ALU.mult).then_inc(sm["ln_v"], 1)
            postnorm("n5", 5)
            dve.wait_ge(sm["x_ready"], 3 * KT)
            prenorm("n6", 6)
            ffn(1)
            postnorm("n7", 7)

        @block.gpsimd
        def _(pool):
            p = nc.gpsimd
            pool.wait_ge(sm["prep_done"], KT)
            for c in range(NCH + 1):
                for g in range(2):
                    if c >= 2:
                        pool.wait_ge(mm_done[g], STAGES * (c - 2) + 2)
                    k = slice(4 * g, 4 * g + 4)
                    for dst, src in ((bbar, ag), (kbar, kb)):
                        if c < NCH:
                            ins = p.tensor_tensor(dst[:, c % 2, k, :], src[:, k, CH * c:CH * c + CH],
                                                  pend[:, k, c:c + 1].to_broadcast([P, 4, CH]), ALU.mult)
                            ins.then_inc(sm["bar_ready"], 1)
                        else:
                            for i in range(4):
                                o = dst[:, c % 2, 4 * g + i, :].rearrange("p (b t) -> p b t", b=DB)
                                ins = p.tensor_tensor(o, src[:, 4 * g + i, SEQ:T].rearrange("p (b t) -> p b t", b=DB),
                                                      pend[:, 4 * g + i, NCH:NCH + DB].unsqueeze(2).to_broadcast([P, DB, DS]), ALU.mult)
                                if i < 3:
                                    ins.then_inc(sm["pool_done"], 1)
                            pool.wait_ge(sm["pool_done"], 3 * (2 * g + (dst is kbar)) + 3)
                            ins.then_inc(sm["bar_ready"], 1)

            def ffn(l):
                w = FF[l]
                pool.wait_ge(w["no_hist"], 4)
                pool.wait_ge(sm["tile_read"], TB[f"fst{l}"] + 2)
                st = fst[:].rearrange("p (b w f) -> p b w f", b=DB, w=2)

                def decode(j):
                    return raw[:, j, 2 + SEQ:RAW].rearrange("p (b t) -> p b t", b=DB)

                def tails(i, j):
                    pool.wait_ge(sm["tile_read"], i * 4 + (TB[f"up{l}"] + j + 1))
                    f = (j % 2) * FT + j // 2
                    at = fo[:, bass.ds(i * 2 + f, 1), :]
                    p.tensor_copy(at[:, :, 0:2], raw[:, j:j + 1, SEQ:SEQ + 2]).then_inc(w["tails"], 1)
                    p.tensor_copy(at[:, :, 2:18].rearrange("p o (b t) -> p (o b) t", t=2), decode(j)[:, :, DS:DS + 2])\
                        .then_inc(w["tails"], 1)

                for j in range(4):
                    p.tensor_copy(decode(j)[:, :, 0:2], st[:, :, :, (j % 2) * FT + j // 2]).then_inc(w["hist_ready"], 1)
                with pool.Fori(0, FT // 2 - 1) as i:
                    for j in range(4):
                        tails(i, j)
                        pool.wait_ge(w["conv_ready"], i * 4 + (j + 1))
                        pool.wait_ge(w["tails"], i * 8 + (2 * j + 2))
                        f = (j % 2) * FT + j // 2 + 2
                        src = st[:, :, :, bass.ds(i * 2 + f, 1)].rearrange("p b w o -> p b (w o)")
                        p.tensor_copy(decode(j)[:, :, 0:2], src).then_inc(w["hist_ready"], 1)
                for j in range(4):
                    tails(FT // 2 - 1, j)

            ffn(0)
            ffn(1)


def n_par_dmas():
    n = r = 0
    for _, m in PARAMS:
        at = 0
        while at < m:
            k = min(m - at, P - (r + at) % P)
            n += 1
            at += k
        r += m
    return n


OUTS = [("y_prompt", (1, SEQ, D)), ("y_sample", (DB, DS, D)), ("p_wkv", (1, 1, NH, HS, HS)), ("p_shift", (1, 1, D)),
        ("p_glu", (1, 1, NSTATE, D)), ("p_ffn", (2, 1, 2, 2 * F)), ("s_wkv", (1, DB, NH, HS, HS)), ("s_shift", (1, DB, D)),
        ("s_glu", (1, DB, NSTATE, D)), ("s_ffn", (2, DB, 2, 2 * F))]


def kernel(**inputs):
    import concourse.bacc as bacc
    from concourse.bass_utils import run_bass_kernel_spmd

    nc = bacc.Bacc("TRN2", target_bir_lowering=False, num_devices=1)
    arrays = {n: np.ascontiguousarray(v) for n, v in inputs.items() if np.asarray(v).size}
    arrays["consts"] = constants()
    args = {n: nc.dram_tensor(n, v.shape, mybir.dt.from_np(v.dtype), kind="ExternalInput").ap() for n, v in arrays.items()}
    outs = {n: nc.dram_tensor("out_" + n, s, F32, kind="ExternalOutput").ap() for n, s in OUTS}
    build(nc, args, outs)
    got = run_bass_kernel_spmd(nc, [arrays], core_ids=[0]).results[0]
    return tuple(got["out_" + n] for n, _ in OUTS)
```

```python
from contextlib import ExitStack
import math

import numpy as np
import concourse.bass as bass
import concourse.mybir as mybir

ALU = mybir.AluOpType
ACT = mybir.ActivationFunctionType
F32 = mybir.dt.float32
F32R = mybir.dt.float32r

P = 128
D = 1024
SEQ = 512
DB, DS = 8, 8
DEC = DB * DS
T = SEQ + DEC
KT = D // P
HS = 64
NH = D // HS
CH = 64
NCH = SEQ // CH
CW = 31
F = ((8 * D // 3 + 127) // 128) * 128
FT = F // P
LW, LA, LG = 64, 64, 160
NORM_EPS, LN_EPS, LNX_EPS = 1e-6, 1e-5, 64e-5
LAM = math.exp(-0.5)
NSTATE = CW - 1

C_ID, C_MEAN, C_HEAD = 0, 128, 256
C_MASK, C_MASKD = 384, 512
C_LVL = 640
LEVELS = [1, 2, 4, 8, 16, 32]
C_LOW1 = C_LVL + 64 * len(LEVELS)
C_IS = C_LOW1 + 64
C_SCAN = C_IS + 64
C_B8 = C_SCAN + T
C_EPS = C_B8 + 8
NCONST = C_EPS + 4


def constants():
    c = np.zeros((P, NCONST), np.float32)
    i = np.arange(P)
    s = i % CH
    t = np.arange(CH)
    c[i, C_ID + i] = 1.0
    c[:, C_MEAN:C_MEAN + P] = 1.0 / D
    c[:, C_HEAD:C_HEAD + P] = (i[:, None] // HS == i[None, :] // HS)
    same = s[:, None] // DS == t[None, :] // DS
    c[:, C_MASK:C_MASK + 64] = s[:, None] < t
    c[:, C_MASK + 64:C_MASK + 128] = s[:, None] <= t
    c[:, C_MASKD:C_MASKD + 64] = (s[:, None] < t) & same
    c[:, C_MASKD + 64:C_MASKD + 128] = (s[:, None] <= t) & same
    for n, m in enumerate(LEVELS):
        pair = (s[:, None] // (2 * m) == t // (2 * m)) & (s[:, None] % (2 * m) < m) & (t % (2 * m) >= m)
        c[:, C_LVL + 64 * n:C_LVL + 64 * n + 64] = pair
    c[:, C_LOW1:C_LOW1 + 64] = (s[:, None] // 2 == t // 2) & (s[:, None] > t)
    c[:, C_IS:C_IS + 64] = s[:, None] == t
    tok = np.arange(T)
    c[:, C_SCAN:C_SCAN + T] = np.where(tok < SEQ, tok % CH != 0, tok % DS != 0)
    c[:, C_B8:C_B8 + 8] = s[:, None] // DS == np.arange(DB)
    c[:, C_EPS:C_EPS + 4] = [NORM_EPS, LN_EPS, LNX_EPS, 0.0]
    return c


PARAMS = [("norm_gain", 8 * KT), ("rwkv_mix", 6 * KT), ("rwkv_w0", KT), ("rwkv_a0", KT), ("rwkv_k_k", KT),
          ("rwkv_k_a", KT), ("rwkv_r_k", KT), ("rwkv_lnx_w", KT), ("rwkv_lnx_b", KT), ("conv_b_in", 2 * KT),
          ("conv_dw_w", CW * KT), ("conv_dw_b", KT), ("conv_ln_w", KT), ("conv_ln_b", KT), ("conv_b_out", KT),
          ("ffn_dw_w", 2 * 3 * 2 * FT), ("ffn_dw_b", 2 * 2 * FT), ("state_rwkv_shift", DB * KT)]
PCOL = {}
_n = 0
for _name, _rows in PARAMS:
    PCOL[_name] = _n
    _n += _rows
NPC = _n
NPG = -(-NPC // P)
NFS = DB * 2 * 2 * FT
NFG = -(-NFS // P)
NGS = DB * NSTATE * KT
NGG = NGS // P

PARTS = []
_n = 0
while _n < FT:
    PARTS.append((_n, min(KT, FT - _n)))
    _n += KT
NFFN = 2 * FT + len(PARTS) * KT
HALF = T // 2
LOOK = 3

TILES = [("par", 2), ("xin", 10), ("n0", 1), ("shift", 1), ("lo1", 4), ("lo2", 2 * KT), ("k", KT),
         ("r", KT), ("v", KT), ("kk", KT), ("post", 4 * KT), ("wo", KT), ("n1", 1), ("fst0", 2), ("n2", 1),
         ("f0", NFFN), ("fo0", 2), ("n3", 1),
         ("gst", 4), ("n4", 1), ("glu", 2 * KT), ("dw", 3), ("go", 2), ("ln", 2), ("co", KT), ("n5", 1), ("fst1", 2), ("n6", 1),
         ("f1", NFFN), ("fo1", 2), ("n7", 1), ("yout", 10)]
TB = {}
_n = 0
for _name, _rows in TILES:
    TB[_name] = _n
    _n += _rows

WSEQ = [("k", KT), ("r", KT), ("v", KT), ("wo", KT), ("glu", 2 * KT), ("co", KT)]
WB = {}
_n = 0
for _name, _rows in WSEQ:
    WB[_name] = _n
    _n += _rows
RING = 4
WTILE = [TB[n] + j for n, m in WSEQ for j in range(m)]

RAW = 2 + SEQ + DB * (2 + DS)
GB = NSTATE + SEQ + DB * (NSTATE + DS)

REG = KT * T
A_H, A_XX, A_A, A_B, A_SG, A_AG, A_K, A_R = [REG * n for n in range(8)]
A_M = A_R
A_RING = 8 * REG
A_H32 = 2 * REG
A_WSPLIT = 4 * REG
A_RAW = A_WSPLIT + 4 * 2 * KT * P
A_CV = A_RAW + 4 * RAW
A_FO = A_CV + 4 * T
A_FR = A_FO
A_FST = A_RING + 2 * KT * P
assert A_FO + max(FT * 2 * 18, NFG * P) <= A_M and A_FST + NFS <= A_RING + RING * KT * P
A_GB = A_XX
A_GR = A_GB + KT * GB
A_CO = A_GR + NGS
A_SIG = A_CO + REG
DW_DVE, DW_PE = (0, 1, 2, 4, 6), (3, 5, 7)
GLU_EVERY = 12
A_DIAG = A_SIG + 2 * T
assert A_DIAG + len(DW_PE) * CW * P <= A_FR
STAGES = 15


def build(nc, a, out):
    with ExitStack() as ctx:
        def sb(name, shape):
            return ctx.enter_context(nc.sbuf_tensor(name, shape, F32))

        def rounded(name, shape):
            return ctx.enter_context(nc.sbuf_tensor(name, shape, F32R))

        def sem(name):
            return ctx.enter_context(nc.semaphore(name))

        x = sb("x", [P, KT, T])
        con = sb("con", [P, NCONST])
        par = sb("par", [P, NPC])
        hg = sb("hg", [P, 2, T])
        tmp = sb("tmp", [P, 4, T])
        ost = sb("ost", [P, 896])
        pend = sb("pend", [P, KT, 16])
        omka = sb("omka", [P, KT])
        with nc.sbuf_tensor("arena", [P, A_RING + RING * KT * P], F32) as arena:
            pass
        hsplit = rounded("hsplit", [P, 2, KT, T])
        hidsplit = rounded("hidsplit", [P, 2, KT, T])
        wsplit = rounded("wsplit", [P, 4, 2, KT, P])
        ring = arena[:, A_RING:A_RING + RING * KT * P].rearrange("p (s k n) -> p s k n", s=RING, n=P)
        ps = ctx.enter_context(nc.psum_tensor("ps", [P, 4096], F32))

        def region(at, n=KT, w=T):
            return arena[:, at:at + n * w].rearrange("p (k t) -> p k t", t=w)

        h, xx, bufA, bufB = region(A_H), region(A_XX), region(A_A), region(A_B)
        sg, ag, kb, rb, mb = region(A_SG), region(A_AG), region(A_K), region(A_R), region(A_M)
        kkb, vb, yb = xx, bufA, sg
        lo1 = arena[:, A_R:A_R + KT * 288].rearrange("p (k n) -> p k n", n=288)
        hwa = arena[0:64, A_R + KT * 288:A_R + KT * 288 + 2 * T].rearrange("p (k t) -> p k t", t=T)
        lo2 = arena[0:64, A_K:A_K + 2 * D].rearrange("p (k n) -> p k n", n=D)
        lg2 = arena[:, A_H:A_H + 2 * D].rearrange("p (k n) -> p k n", n=D)
        rows = arena[:, A_A:A_A + NPG * P].rearrange("p (g n) -> p g n", n=P)
        fst = arena[:, A_FST:A_FST + NFS]
        frows = arena[:, A_FR:A_FR + NFG * P].rearrange("p (g n) -> p g n", n=P)
        grows = arena[:, A_B + REG:A_B + REG + NGG * P].rearrange("p (g n) -> p g n", n=P)
        xrows = arena[:, A_SG:A_SG + 5 * D].rearrange("p (g n) -> p g n", n=D)
        h32 = region(A_H32)
        raw = arena[:, A_RAW:A_RAW + 4 * RAW].rearrange("p (q n) -> p q n", q=4)
        cv = arena[:, A_CV:A_CV + 4 * T].rearrange("p (q n) -> p q n", q=4)
        fo = arena[:, A_FO:A_FO + 2 * FT * 18].rearrange("p (f n) -> p f n", n=18)
        gb = region(A_GB, KT, GB)
        gst = arena[:, A_GR:A_GR + NGS]
        cvo = region(A_CO)
        gsig = region(A_SIG, 2)
        gd = gb[:, :, NSTATE + SEQ:GB].rearrange("p k (b t) -> p k b t", b=DB)
        diag = arena[:, A_DIAG:A_DIAG + len(DW_PE) * CW * P].rearrange("p (m n c) -> p m n c", n=CW, c=P)
        ident = con[:, C_ID:C_ID + P]

        def small(at, n=64):
            return arena[:, at:at + KT * n].rearrange("p (k n) -> p k n", n=n)

        MbT = small(A_B, 128)
        Mn, TT, TI, Y, Vt, Bt, S = [small(A_B + 1024 + 512 * n) for n in range(7)]
        ringf = arena[:, A_RING:A_RING + RING * KT * P]
        MkT = ringf[:, 0:1024].rearrange("p (k n) -> p k n", n=128)
        Ktk = ringf[:, 1024:1536].rearrange("p (k n) -> p k n", n=64)
        bbar = ringf[:, 1536:2560].rearrange("p (v k n) -> p v k n", v=2, n=64)
        kbar = ringf[:, 2560:3584].rearrange("p (v k n) -> p v k n", v=2, n=64)
        Rm, SA = Y, TI
        Sd = arena[:, A_H:A_H + KT * DB * 64].rearrange("p (k b n) -> p k b n", b=DB, n=64)
        Snat = arena[:, A_B:A_B + KT * DB * 64].rearrange("p (k b n) -> p k b n", b=DB, n=64)
        yg = yb

        def pcol(name, i):
            return par[:, PCOL[name] + i:PCOL[name] + i + 1]

        def gain(n, kt):
            return pcol("norm_gain", n * KT + kt)

        NAMES = ["const_in", "par_in", "x_in", "lo1_in", "lo2_in", "lg2_in", "sd_in", "fst_in", "gst_in", "out_done",
                 "tile_full", "tile_read", "sq_ready", "sq_used", "x_ready", "h_ready", "xm_ready", "vec_done",
                 "act_done", "pool_done", "v_ready", "wide_ready", "prep_sq", "prep_e", "prep_s", "prep_done",
                 "gath_ready", "ost_ready", "ost_sent", "post_a", "post_v", "z_ready", "bar_ready", "sd_ready", "snat_ready",
                 "wkv_over", "state_out", "glu_s", "glu_ready", "glu_hist", "conv_done", "diag_ready", "ln_a", "ln_v", "y_ready", "mix_free"]
        sm = {n: sem(n) for n in NAMES}
        w_in = [sem(f"w_in{i}") for i in range(RING)]
        fw_in = [[sem(f"fw_in{l}{i}") for i in range(2)] for l in range(2)]
        xt_in = [sem(f"xt_in{i}") for i in range(5)]
        mm_done = [sem(f"mm_done{g}") for g in range(2)]
        ev_done = [sem(f"ev_done{g}") for g in range(2)]
        FF = [{n: sem(f"{n}{l}") for n in ("raw_ready", "hist_ready", "conv_ready", "gate_ready", "hid_ready",
                                           "tails", "no_hist", "cvd", "w_hi", "w_lo", "h32_ready",
                                           "h_hi", "h_lo", "hid32_ready", "hid_hi", "hid_lo")} for l in range(2)]
        block = ctx.enter_context(nc.Block())

        def tset(t):
            return (t % 4) * 1024

        def bank2(t, n=T, m=P):
            return ps[0:m, tset(t):tset(t) + n]

        @block.sync
        def _(eng):
            def load(dst, src, s):
                eng.dma_start(dst, src).then_inc(s, 16)

            load(con[:], a["consts"], sm["const_in"])
            r = 0
            n_par = 0
            for name, m in PARAMS:
                src = a[name]
                flat = src.rearrange(" ".join(f"d{i}" for i in range(len(src.shape))) + " -> ("
                                     + " ".join(f"d{i}" for i in range(len(src.shape))) + ")")
                flat = flat.rearrange("(r c) -> r c", c=P)
                at = 0
                while at < m:
                    g, p = (r + at) // P, (r + at) % P
                    k = min(m - at, P - p)
                    load(rows[p:p + k, g, :], flat[at:at + k, :], sm["par_in"])
                    n_par += 1
                    at += k
                r += m

            def load_fst(dst, l, s):
                f = a["state_ffn_conv"][l].rearrange("b w (k p) -> (b w k) p", p=P)
                full = NFS // P
                load(dst[:, 0:full, :], f[0:full * P, :].rearrange("(g p) c -> p g c", p=P), s)
                load(dst[0:NFS - full * P, full, :], f[full * P:NFS, :], s)

            for g in range(4):
                load(xrows[:, g, :], a["x_prompt"][0, g * P:(g + 1) * P, :], xt_in[g])
            load(xrows[0:DEC, 4, :], a["x_sample"].rearrange("b t d -> (b t) d"), xt_in[4])
            for name, o, m in (("rwkv_w1", 0, LW), ("rwkv_a1", LW, LA), ("rwkv_g1", LW + LA, LG)):
                load(lo1[:, :, o:o + m], a[name][0].rearrange("(k p) n -> p k n", p=P), sm["lo1_in"])
            load(lo2[:, 0, :], a["rwkv_w2"][0], sm["lo2_in"])
            load(lo2[:, 1, :], a["rwkv_a2"][0], sm["lo2_in"])

            def wtile(w, src, n):
                load(ring[:, w % RING], src[:, n * P:(n + 1) * P].rearrange("(k p) n -> p k n", p=P), w_in[w % RING])

            def weights(name, src, order, first=0):
                for j, n in list(enumerate(order))[first:]:
                    w = WB[name] + j
                    if w >= RING:
                        eng.wait_ge(sm["tile_full"], WTILE[w - RING] + 1)
                    wtile(w, src, n)

            weights("k", a["rwkv_wk"][0], range(KT))
            weights("r", a["rwkv_wr"][0], range(KT))
            weights("v", a["rwkv_wv"][0], range(KT))
            eng.wait_ge(sm["tile_full"], TB["v"] + KT)
            for b in range(DB):
                load(Snat[:, :, b, :], a["state_rwkv_wkv"][0, b].rearrange("(k e) i j -> (e i) k j", e=2), sm["sd_in"])

            def store(dst, src):
                eng.dma_start(dst, src).then_inc(sm["out_done"], 16)
                n_out[0] += 1

            n_out = [0]

            eng.wait_ge(sm["tile_read"], TB["shift"] + 1)
            for kt in range(KT):
                store(out["p_shift"][0, :, kt * P:(kt + 1) * P], ost[9 * kt:9 * kt + 1, P:2 * P])
                store(out["s_shift"][0, :, kt * P:(kt + 1) * P], ost[9 * kt + 1:9 * kt + 9, P:2 * P])
            eng.wait_ge(sm["state_out"], 1)
            store(out["p_wkv"][0, 0].rearrange("(k e) i j -> (e i) k j", e=2), ost[:, 256:768].rearrange("p (k j) -> p k j", j=64))
            eng.wait_ge(sm["state_out"], 1 + KT)
            for b in range(DB):
                store(out["s_wkv"][0, b].rearrange("(k e) i j -> (e i) k j", e=2), Snat[:, :, b, :])
            load(lg2[:, 0, :], a["rwkv_g2"][0, 0:P, :], sm["lg2_in"])
            load(lg2[0:LG - P, 1, :], a["rwkv_g2"][0, P:LG, :], sm["lg2_in"])
            weights("wo", a["rwkv_wo"][0], range(KT))
            eng.wait_ge(sm["z_ready"], KT)
            load_fst(frows, 0, sm["fst_in"])

            def ffn(l):
                w = FF[l]
                up, down = a["ffn_w_in"][l], a["ffn_w_out"][l]

                def cols(src):
                    return src.rearrange("(k p) n -> p k n", p=P)

                eng.wait_ge(sm["tile_full"], TB[("wo", "co")[l]] + KT - 2)
                at = 0
                for f0, nf in PARTS:
                    if at == 0:
                        for j in range(4):
                            if j >= 2:
                                eng.wait_ge(w["w_lo"], j - 1)
                            f = (j // 2) * P + (j % 2) * F
                            load(ring[:, j % 2], cols(up[:, f:f + P]), fw_in[l][j % 2])
                    with eng.Fori(1 if at == 0 else 0, nf // 2) as i:
                        for j in range(4):
                            eng.wait_ge(w["w_lo"], i * 4 + (at + j - 1))
                            f = (f0 + j // 2) * P + (j % 2) * F
                            load(ring[:, j % 2], cols(up[:, bass.ds(i * (2 * P) + f, P)]), fw_in[l][j % 2])
                    at += 2 * nf
                    for n in range(KT):
                        eng.wait_ge(w["w_lo"], at + n - 1)
                        load(ring[:, n % 2, 0:nf], cols(down[f0 * P:(f0 + nf) * P, n * P:(n + 1) * P]), fw_in[l][n % 2])
                    at += KT

            ffn(0)
            eng.wait_ge(sm["tile_full"], TB["fo0"] + 2)
            load(grows, a["state_conv_glu"][0].rearrange("b w (k p) -> (b w k) p", p=P).rearrange("(g p) c -> p g c", p=P), sm["gst_in"])
            load_fst(frows, 1, sm["gst_in"])
            eng.wait_ge(FF[0]["w_lo"], NFFN)
            eng.wait_ge(FF[0]["hist_ready"], 2 * FT)
            weights("glu", a["conv_w_in"][0], [n // 2 + KT * (n % 2) for n in range(2 * KT)])

            def ffn_state(l):
                eng.wait_ge(sm["tile_read"], TB[f"fo{l}"] + 2)
                for g in range(7):
                    m = min(7, 2 * FT - 7 * g)
                    for q in range(m):
                        f = 7 * g + q
                        store(out["p_ffn"][l, 0, :, f * P:(f + 1) * P], ost[18 * q:18 * q + 2, g * P:(g + 1) * P])
                        store(out["s_ffn"][l, :, :, f * P:(f + 1) * P].rearrange("b w n -> (b w) n"), ost[18 * q + 2:18 * q + 18, g * P:(g + 1) * P])

            ffn_state(0)
            eng.wait_ge(sm["tile_read"], TB["go"] + 2)
            for kt in range(KT):
                store(out["p_glu"][0, 0, :, kt * P:(kt + 1) * P], ost[30 * (kt % 4):30 * (kt % 4) + 30, (kt // 4) * P:(kt // 4 + 1) * P])
                for b in range(DB):
                    r = 64 * (kt % 2) + DS * b
                    store(out["s_glu"][0, b, NSTATE - DS:NSTATE, kt * P:(kt + 1) * P],
                          ost[r:r + DS, 256 + (kt // 2) * P:256 + (kt // 2 + 1) * P])
            store(out["s_glu"][0, :, 0:NSTATE - DS, :], a["state_conv_glu"][0, :, DS:NSTATE, :])
            weights("co", a["conv_w_out"][0], range(KT))
            ffn(1)
            ffn_state(1)
            for g in range(5):
                eng.wait_ge(sm["tile_read"], TB["yout"] + 2 * g + 2)
                if g < 4:
                    store(out["y_prompt"][0, g * P:(g + 1) * P, :], xrows[:, g, :])
                else:
                    store(out["y_sample"].rearrange("b t d -> (b t) d"), xrows[0:DEC, 4, :])
            eng.wait_ge(sm["out_done"], 16 * n_out[0])

        @block.tensor
        def _(pe):
            def begin(t):
                if t >= 4:
                    pe.wait_ge(sm["tile_read"], t - 3)

            def product(t, terms, m=P, mark=None):
                begin(t)
                for i, (lhs, rhs, pre) in enumerate(terms):
                    for w, v in pre:
                        pe.wait_ge(w, v)
                    st, sp = i == 0, i == len(terms) - 1
                    pe.matmul(ps[0:m, tset(t):tset(t) + SEQ], lhs, rhs[:, 0:SEQ], start=st, stop=sp)
                    ins = pe.matmul(ps[0:m, tset(t) + SEQ:tset(t) + T], lhs, rhs[:, SEQ:T], start=st, stop=sp)
                    if mark is not None and not sp:
                        ins.then_inc(mark, 1)
                ins.then_inc(sm["tile_full"], 1)

            def transposes(t, srcs):
                begin(t)
                for q, src in enumerate(srcs):
                    k = src.shape[0]
                    m = src.shape[1]
                    ins = pe.transpose(ps[0:m, tset(t) + P * q:tset(t) + P * q + k], src, ident[0:k, 0:k])
                ins.then_inc(sm["tile_full"], 1)

            def norm_sums(name, ones=C_MEAN, first=0):
                n = norm_i[0]
                product(TB[name] + first, [(con[:, ones:ones + P], tmp[:, kt % 2, :], [(sm["sq_ready"], KT * n + kt + 1)])
                                   for kt in range(KT)], mark=sm["sq_used"])
                norm_i[0] += 1

            norm_i = [0]

            def gemm(name, src, pre, first=0):
                for j in range(KT if name not in ("glu",) else 2 * KT):
                    w = WB[name] + j
                    terms = []
                    for kt in range(KT):
                        p = [(w_in[w % RING], 16 * (w // RING + 1))] if kt == 0 else []
                        if j == 0:
                            p.append((pre[0], pre[1] + kt + 1))
                        terms.append((ring[:, w % RING, kt, :], src[:, kt, :], p))
                    product(TB[name] + j, terms)

            def state_turns(name):
                for t in range(2):
                    transposes(TB[name] + t, [frows[0:min(P, NFS - P * g), g, :] for g in range(4 * t, min(4 * t + 4, NFG))])

            pe.wait_ge(sm["const_in"], 16)
            pe.wait_ge(sm["par_in"], 16 * n_par_dmas())
            for t in range(2):
                transposes(TB["par"] + t, [rows[0:min(P, NPC - P * g), g, :] for g in range(4 * t, min(4 * t + 4, NPG))])
            for g in range(5):
                pe.wait_ge(xt_in[g], 16)
                k = P if g < 4 else DEC
                for q in range(2):
                    transposes(TB["xin"] + 2 * g + q, [xrows[0:k, g, (4 * q + i) * P:(4 * q + i + 1) * P] for i in range(4)])
            norm_sums("n0")
            pe.wait_ge(sm["gath_ready"], 1)
            transposes(TB["shift"], [ost[:, 0:9 * KT]])
            pe.wait_ge(sm["lo1_in"], 48)
            for j, (src, o, m, q) in enumerate(((bufA, 0, LW, 0), (bufB, LW, LA, 1), (bufA, LW + LA, P, 2), (bufA, LW + LA + P, LG - P, 2))):
                product(TB["lo1"] + j, [(lo1[:, kt, o:o + m], src[:, kt, :], [(sm["xm_ready"], KT * q + kt + 1)] if j < 3 else [])
                                        for kt in range(KT)], m=m)
            pe.wait_ge(sm["lo2_in"], 32)
            pe.wait_ge(sm["tile_read"], TB["lo1"] + 2)
            for n in range(KT):
                for q in range(2):
                    product(TB["lo2"] + 2 * n + q, [(lo2[:, q, n * P:(n + 1) * P], hwa[:, q, :], [])])
            gemm("k", bufB, (sm["xm_ready"], 3 * KT))
            gemm("r", bufA, (sm["xm_ready"], 4 * KT))
            gemm("v", bufB, (sm["xm_ready"], 5 * KT))
            for kt in range(KT):
                product(TB["kk"] + kt, [(con[:, C_HEAD:C_HEAD + P], tmp[:, kt % 2, :], [(sm["prep_sq"], kt + 1)])])

            def pairs(g):
                return range(4 * g, 4 * g + 4)

            def both(o, lhs, rhs, start=True, stop=True):
                for e in (0, 64):
                    ins = pe.matmul(o[e:e + 64], lhs[e:e + 64], rhs[e:e + 64], start=start, stop=stop)
                return ins

            def pbank(g, b, q, w, n=None):
                o = 2048 * g + 512 * b + w * q
                return ps[:, o:o + (n or w)]

            eye = con[:, C_IS:C_IS + 64]
            pe.wait_ge(sm["prep_done"], KT)
            pe.wait_ge(sm["tile_read"], TB["kk"] + KT)
            pe.wait_ge(sm["sd_in"], 16 * DB)
            for k in range(KT):
                for b in range(DB):
                    ins = both(ps[:, 512 * k + 64 * b:512 * k + 64 * b + 64], Snat[:, k, b, :], eye)
                ins.then_inc(sm["sd_ready"], 1)
            ev = [0, 0]
            pe.wait_ge(sm["sd_ready"], 2 * KT)

            def step(g, ins):
                ins.then_inc(mm_done[g], 1)

            def turn(g):
                if ev[g]:
                    pe.wait_ge(ev_done[g], ev[g])
                ev[g] += 1

            def factors(g, c, tok):
                turn(g)
                for i, k in enumerate(pairs(g)):
                    for e in (0, 64):
                        for q in range(2):
                            pe.matmul(pbank(g, 0, i, 128)[e:e + 64, 64 * q:64 * q + 64], ag[e:e + 64, k, tok], (kkb, rb)[q][e:e + 64, k, tok], start=True, stop=True)
                            pe.matmul(pbank(g, 1, i, 128)[e:e + 64, 64 * q:64 * q + 64], kb[e:e + 64, k, tok], (kkb, rb)[q][e:e + 64, k, tok], start=True, stop=True)
                    ins = both(pbank(g, 2, i, 64), kkb[:, k, tok], ag[:, k, tok])
                step(g, ins)

            def to_tokens(g, c, tok):
                turn(g)
                pe.wait_ge(sm["bar_ready"], 2 * (2 * c + g) + 2)
                for i, k in enumerate(pairs(g)):
                    both(pbank(g, 0, i, 64), vb[:, k, tok], eye)
                    both(pbank(g, 1, i, 64), bbar[:, c % 2, k, :], eye)
                    ins = both(pbank(g, 2, i, 64), kbar[:, c % 2, k, :], eye)
                step(g, ins)

            def level(g, last, part):
                turn(g)
                for i, k in enumerate(pairs(g)):
                    if part == 0:
                        ins = both(pbank(g, 0, i, 64), Mn[:, k, :], TT[:, k, :])
                    else:
                        ins = both(pbank(g, 1, i, 64), TI[:, k, :], Y[:, k, :])
                        if not last:
                            ins = both(pbank(g, 2, i, 64), Y[:, k, :], TI[:, k, :])
                step(g, ins)

            for c in range(NCH):
                tok = slice(CH * c, CH * c + CH)
                for g in range(2):
                    factors(g, c, tok)
                for g in range(2):
                    to_tokens(g, c, tok)
                for n in range(1, len(LEVELS)):
                    for part in range(2):
                        for g in range(2):
                            level(g, n == len(LEVELS) - 1, part)
                for g in range(2):
                    turn(g)
                    for i, k in enumerate(pairs(g)):
                        if c:
                            both(pbank(g, 0, i, 64), kkb[:, k, tok], S[:, k, :], stop=False)
                        ins = both(pbank(g, 0, i, 64), MkT[:, k, 0:64], Vt[:, k, :], start=c == 0)
                    step(g, ins)
                for g in range(2):
                    turn(g)
                    for i, k in enumerate(pairs(g)):
                        ins = both(pbank(g, 1, i, 64), TT[:, k, :], Rm[:, k, :])
                    step(g, ins)
                for g in range(2):
                    turn(g)
                    for i, k in enumerate(pairs(g)):
                        both(pbank(g, 2, i, 64), Bt[:, k, :], SA[:, k, :], stop=False)
                        both(pbank(g, 2, i, 64), Ktk[:, k, :], Vt[:, k, :], start=False)
                        both(pbank(g, 3, i, 64), SA[:, k, :], MbT[:, k, 64:128], stop=False)
                        ins = both(pbank(g, 3, i, 64), Vt[:, k, :], MkT[:, k, 64:128], start=False, stop=c == 0)
                        if c:
                            ins = both(pbank(g, 3, i, 64), S[:, k, :], rb[:, k, tok], start=False)
                    step(g, ins)
            c = NCH
            tok = slice(SEQ, T)
            for g in range(2):
                factors(g, c, tok)
            for g in range(2):
                to_tokens(g, c, tok)
            for n in (1, 2):
                for part in range(2):
                    for g in range(2):
                        level(g, n == 2, part)
            for i in range(4):
                for g in range(2):
                    turn(g)
                    k = 4 * g + i
                    am = tmp[:, 2 * g + i % 2, 0:512].rearrange("p (b t) -> p b t", b=DB)
                    for b in range(DB):
                        both(pbank(g, 0, i, 64), am[:, b, :], Sd[:, k, b, :], start=b == 0, stop=False)
                    ins = both(pbank(g, 0, i, 64), MkT[:, k, 0:64], Vt[:, k, :], start=False)
                    step(g, ins)
            for g in range(2):
                turn(g)
                for i, k in enumerate(pairs(g)):
                    ins = both(pbank(g, 1, i, 64), TT[:, k, :], Rm[:, k, :])
                step(g, ins)
            for i in range(4):
                for g in range(2):
                    turn(g)
                    k = 4 * g + i
                    o = pbank(g, 3, 0, 64)
                    both(o, SA[:, k, :], MbT[:, k, 64:128], stop=False)
                    both(o, Vt[:, k, :], MkT[:, k, 64:128], start=False, stop=False)
                    for b in range(DB):
                        t = slice(8 * b, 8 * b + 8)
                        both(o[:, t], Sd[:, k, b, :], rb[:, k, SEQ + 8 * b:SEQ + 8 * b + 8], start=False, stop=b == DB - 1)
                    o = pbank(g, 2, 0, 512)
                    both(o, Bt[:, k, :], tmp[:, 2 * g, 0:512], stop=False)
                    ins = both(o, Ktk[:, k, :], tmp[:, 2 * g + 1, 0:512], start=False)
                    step(g, ins)
            for g in range(2):
                pe.wait_ge(ev_done[g], ev[g])
            for k in range(KT):
                ins = both(ps[:, 64 * k:64 * k + 64], S[:, k, :], eye)
            ins.then_inc(sm["snat_ready"], 1)
            for k in range(KT):
                o = 512 * ((k + 1) % 8)
                if k == 7:
                    pe.wait_ge(sm["state_out"], 1)
                for b in range(DB):
                    ins = both(ps[:, o + 64 * b:o + 64 * b + 64], Sd[:, k, b, :], eye)
                ins.then_inc(sm["snat_ready"], 1)
            pe.wait_ge(sm["state_out"], 1 + KT)
            pe.wait_ge(sm["lg2_in"], 32)
            for kt in range(KT):
                t = TB["post"] + 4 * kt
                product(t, [(con[:, C_HEAD:C_HEAD + P], yg[:, kt, :], [])])
                product(t + 1, [(con[:, C_HEAD:C_HEAD + P], tmp[:, 0, :], [(sm["post_a"], kt + 1)])])
                product(t + 2, [(con[:, C_HEAD:C_HEAD + P], tmp[:, 1, :], [(sm["post_v"], 2 * kt + 1)])])
                product(t + 3, [(lg2[:, 0, kt * P:(kt + 1) * P], hg[:, 0, :], []),
                                (lg2[0:LG - P, 1, kt * P:(kt + 1) * P], hg[0:LG - P, 1, :], [])])
            gemm("wo", yg, (sm["z_ready"], 0))
            norm_sums("n1")
            pe.wait_ge(sm["fst_in"], 32)
            state_turns("fst0")
            norm_sums("n2")

            def split_product(t, lhs, rhs, k, pre=None):
                s = tset(t)
                for i in range(k):
                    if pre is not None:
                        pe.wait_ge(pre[0], pre[1] + i + 1)
                    for n, (u, v) in enumerate(((0, 0), (0, 1), (1, 0))):
                        for z in range(2):
                            ins = pe.matmul(ps[:, s + 512 * z:s + 512 * z + HALF], lhs(u, i), rhs[:, v, i, HALF * z:HALF * z + HALF],
                                            start=i == 0 and n == 0, stop=i == k - 1 and n == 2)
                ins.then_inc(sm["tile_full"], 1)

            def ffn(l):
                w = FF[l]
                t0 = TB[f"f{l}"]
                at = 0
                for f0, nf in PARTS:
                    if at == 0:
                        pe.wait_ge(w["h_lo"], KT)
                    with pe.Fori(0, nf // 2) as i:
                        for j in range(4):
                            pe.wait_ge(sm["tile_read"], i * 4 + (t0 + at + j - 3))
                            pe.wait_ge(w["w_lo"], i * 4 + (at + j + 1))
                            split_product(t0 + j, lambda u, k: wsplit[:, j, u, k, :], hsplit, KT)
                    at += 2 * nf
                    for n in range(KT):
                        begin(t0 + at + n)
                        pe.wait_ge(w["w_lo"], at + n + 1)
                        split_product(t0 + at + n, lambda u, k: wsplit[:, n % 4, u, k, :], hidsplit, nf,
                                      (w["hid_lo"], f0) if n == 0 else None)
                    at += KT
                pe.wait_ge(w["tails"], 4 * FT)
                for t in range(2):
                    transposes(TB[f"fo{l}"] + t, [fo[:, 7 * g:min(7 * g + 7, 2 * FT), :].rearrange("p f n -> p (f n)")
                                                  for g in range(4 * t, min(4 * t + 4, 7))])

            ffn(0)
            norm_sums("n3")
            pe.wait_ge(sm["gst_in"], 48)
            for t in range(4):
                transposes(TB["gst"] + t, [grows[:, g, :] for g in range(4 * t, min(4 * t + 4, NGG))])
            norm_sums("n4")
            gemm("glu", h, (sm["h_ready"], KT))
            for m, kt in enumerate(DW_PE):
                t = TB["dw"] + m
                begin(t)
                pe.wait_ge(sm["glu_ready"], kt + 1)
                for n in range(CW):
                    pe.wait_ge(sm["diag_ready"], CW * m + n + 1)
                    st, sp = n == 0, n == CW - 1
                    pe.matmul(ps[:, tset(t):tset(t) + SEQ], diag[:, m, n, :], gb[:, kt, n:n + SEQ], start=st, stop=sp)
                    ins = pe.matmul(ps[:, tset(t) + SEQ:tset(t) + T].rearrange("p (b t) -> p b t", b=DB), diag[:, m, n, :],
                                    gd[:, kt, :, n:n + DS], start=st, stop=sp)
                ins.then_inc(sm["tile_full"], 1)
            pe.wait_ge(sm["gath_ready"], 2)
            gathp = arena[:, A_H:A_H + 240]
            gaths = arena[:, A_H + 240:A_H + 752]
            transposes(TB["go"], [gathp[:, 0:120], gathp[:, 120:240]])
            transposes(TB["go"] + 1, [gaths[:, P * q:P * q + P] for q in range(4)])
            by = {kt: (sm["conv_done"], m + 1) for m, kt in enumerate(DW_DVE)}
            by.update({kt: (sm["tile_read"], TB["dw"] + m + 1) for m, kt in enumerate(DW_PE)})
            product(TB["ln"], [(con[:, C_MEAN:C_MEAN + P], cvo[:, kt, :], [by[kt]]) for kt in DW_DVE[:-1] + DW_PE + DW_DVE[-1:]])
            norm_sums("ln", first=1)
            gemm("co", cvo, (sm["z_ready"], KT))
            norm_sums("n5")
            state_turns("fst1")
            norm_sums("n6")
            ffn(1)
            norm_sums("n7")
            for g in range(5):
                k = P if g < 4 else DEC
                for q in range(2):
                    if g == 0 and q == 0:
                        pe.wait_ge(sm["x_ready"], 4 * KT)
                    transposes(TB["yout"] + 2 * g + q, [x[:, 4 * q + i, g * P:g * P + k] for i in range(4)])

        @block.scalar
        def _(act):
            done = [0]
            read = [0]

            def take(t, ins=None):
                act.wait_ge(sm["tile_full"], t + 1)

            def freed(ins):
                ins.then_inc(sm["tile_read"], 1)

            f = nc.scalar.activation
            norm_i = [0]

            def norm(name, src, pre, eps=0, first=0):
                n = norm_i[0]
                for kt in range(KT):
                    if pre is not None:
                        act.wait_ge(pre[0], pre[1] + kt + 1)
                    if kt >= 2:
                        act.wait_ge(sm["sq_used"], (KT - 1) * n + kt - 1)
                    f(tmp[:, kt % 2, :], src[:, kt, :], ACT.Square).then_inc(sm["sq_ready"], 1)
                t = TB[name] + first
                take(t)
                freed(f(tmp[:, 2, :], bank2(t), ACT.Sqrt, bias=con[:, C_EPS + eps:C_EPS + eps + 1]))
                norm_i[0] += 1

            for t in range(2):
                m = min(512, NPC - 512 * t)
                take(TB["par"] + t)
                freed(f(par[:, 512 * t:512 * t + m], bank2(TB["par"] + t, m), ACT.Copy))

            def state_cols(name):
                for t in range(2):
                    m = min(512, NFS - 512 * t)
                    take(TB[name] + t)
                    freed(f(fst[:, 512 * t:512 * t + m], bank2(TB[name] + t, m), ACT.Copy))

            for g in range(5):
                k = P if g < 4 else DEC
                for q in range(2):
                    t = TB["xin"] + 2 * g + q
                    take(t)
                    src = ps[:, tset(t):tset(t) + 512].rearrange("p (i n) -> p i n", n=P)[:, :, 0:k]
                    freed(f(x[:, 4 * q:4 * q + 4, g * P:g * P + k], src, ACT.Copy))
            act.wait_ge(sm["tile_read"], TB["xin"] + 10)
            norm("n0", x, None)
            take(TB["shift"])
            freed(f(ost[0:9 * KT, 128:256], ps[0:9 * KT, tset(TB["shift"]):tset(TB["shift"]) + P], ACT.Copy))
            t = TB["lo1"]
            take(t)
            freed(f(hwa[:, 0, :], bank2(t, m=LW), ACT.Tanh))
            take(t + 1)
            freed(f(hwa[:, 1, :], bank2(t + 1, m=LA), ACT.Copy))
            take(t + 2)
            freed(f(hg[:, 0, :], bank2(t + 2), ACT.Sigmoid))
            take(t + 3)
            freed(f(hg[0:LG - P, 1, :], bank2(t + 3, m=LG - P), ACT.Sigmoid))
            for n in range(KT):
                for q, (dst, b) in enumerate(((sg, "rwkv_w0"), (ag, "rwkv_a0"))):
                    t = TB["lo2"] + 2 * n + q
                    take(t)
                    freed(f(dst[:, n, :], bank2(t), ACT.Sigmoid, bias=pcol(b, n)))
            for name, dst in (("k", kb), ("r", rb), ("v", vb)):
                for n in range(KT):
                    take(TB[name] + n)
                    freed(f(dst[:, n, :], bank2(TB[name] + n), ACT.Copy))
            for kt in range(KT):
                act.wait_ge(sm["prep_s"], kt + 1)
                if kt >= 2:
                    act.wait_ge(sm["tile_full"], TB["kk"] + kt - 1)
                f(tmp[:, kt % 2, :], kkb[:, kt, :], ACT.Square).then_inc(sm["prep_sq"], 1)
                if kt >= 1:
                    prev = kt - 1
                    if prev >= 2:
                        act.wait_ge(sm["prep_e"], prev - 1)
                    take(TB["kk"] + prev)
                    freed(f(tmp[:, 2 + prev % 2, :], bank2(TB["kk"] + prev), ACT.Sqrt))
            act.wait_ge(sm["prep_e"], KT - 2)
            take(TB["kk"] + KT - 1)
            freed(f(tmp[:, 2 + (KT - 1) % 2, :], bank2(TB["kk"] + KT - 1), ACT.Sqrt))
            for kt in range(KT):
                act.wait_ge(sm["wide_ready"], kt + 1)
                s = 2 * (kt % 2)
                f(tmp[:, s + 1, :], tmp[:, s, :], ACT.Exp, scale=-LAM).then_inc(sm["v_ready"], 1)
                f(sg[:, kt, :], sg[:, kt, :], ACT.Exp, scale=-LAM).then_inc(sm["v_ready"], 1)
                f(tmp[:, s, :], tmp[:, s, :], ACT.Exp, scale=LAM).then_inc(sm["v_ready"], 1)
            for k in range(KT):
                act.wait_ge(sm["sd_ready"], KT)
                f(Sd[:, k], ps[:, 512 * k:512 * k + 512].rearrange("p (b n) -> p b n", b=DB), ACT.Copy).then_inc(sm["sd_ready"], 1)
            act.wait_ge(sm["snat_ready"], 1)
            f(ost[:, 256:768], ps[:, 0:512], ACT.Copy).then_inc(sm["state_out"], 1)
            for k in range(KT):
                act.wait_ge(sm["snat_ready"], k + 2)
                o = 512 * ((k + 1) % 8)
                f(Snat[:, k], ps[:, o:o + 512].rearrange("p (b n) -> p b n", b=DB), ACT.Copy).then_inc(sm["state_out"], 1)
            for kt in range(KT):
                t = TB["post"] + 4 * kt
                take(t)
                if kt:
                    act.wait_ge(sm["z_ready"], kt)
                freed(f(tmp[:, 2, :], bank2(t), ACT.Copy, scale=1.0 / HS))
                act.wait_ge(sm["post_v"], 2 * kt + 2)
                f(tmp[:, 0, :], yg[:, kt, :], ACT.Square).then_inc(sm["post_a"], 1)
                take(t + 1)
                freed(f(tmp[:, 2, :], bank2(t + 1), ACT.Sqrt, scale=1.0 / HS, bias=con[:, C_EPS + 2:C_EPS + 3]))
                take(t + 2)
                freed(f(tmp[:, 3, :], bank2(t + 2), ACT.Copy))
                take(t + 3)
                freed(f(tmp[:, 0, :], bank2(t + 3), ACT.Copy))

            def outputs(name):
                for n in range(KT):
                    take(TB[name] + n)
                    freed(f(mb[:, n, :], bank2(TB[name] + n), ACT.Copy))

            def w_hi(l, at, i=None):
                act.wait_ge(fw_in[l][at % 2], 16 * (at // 2 + 1) + (0 if i is None else i * 32))
                if at >= 4 or i is not None:
                    act.wait_ge(sm["tile_full"], TB[f"f{l}"] + at - 3 + (0 if i is None else i * 4))
                f(wsplit[:, at % 4, 0], ring[:, at % 2], ACT.Copy).then_inc(FF[l]["w_hi"], 1)

            def halves(t):
                return ps[:, tset(t):tset(t) + 1024].rearrange("p (z n) -> p z n", z=2)[:, :, 0:HALF]

            def ffn_first(l):
                act.wait_ge(sm["tile_full"], TB[("wo", "co")[l]] + KT)
                for at in range(LOOK):
                    w_hi(l, at)

            outputs("wo")
            norm("n1", mb, (sm["tile_read"], TB["wo"]))
            ffn_first(0)
            state_cols("fst0")
            norm("n2", x, (sm["x_ready"], 0))

            def ffn(l):
                w = FF[l]
                t0 = TB[f"f{l}"]
                for kt in range(KT):
                    act.wait_ge(w["h32_ready"], kt + 1)
                    f(hsplit[:, 0, kt, :], h32[:, kt, :], ACT.Copy).then_inc(w["h_hi"], 1)
                at = 0
                for part, (f0, nf) in enumerate(PARTS):
                    act.wait_ge(sm["tile_read"], t0 + at)
                    with act.Fori(0, nf // 2) as i:
                        for q in range(2):
                            for z in range(2):
                                j = 2 * q + z
                                w_hi(l, at + j + LOOK, i)
                                act.wait_ge(sm["tile_full"], i * 4 + (t0 + at + j + 1))
                                act.wait_ge(w["hist_ready"], i * 4 + (2 * f0 + j + 1))
                                s = tset(t0 + j)
                                f(raw[:, j, 2:2 + HALF], ps[:, s:s + HALF], ACT.Copy)
                                f(raw[:, j, 2 + HALF:2 + SEQ], ps[:, s + 512:s + 512 + SEQ - HALF], ACT.Copy)
                                dst = raw[:, j, 2 + SEQ:RAW].rearrange("p (b t) -> p b t", b=DB)[:, :, 2:2 + DS]
                                freed(f(dst, ps[:, s + 512 + SEQ - HALF:s + 512 + HALF].rearrange("p (b t) -> p b t", b=DB), ACT.Copy))
                            act.wait_ge(w["conv_ready"], i * 4 + (2 * f0 + 2 * q + 1))
                            f(cv[:, 2 * q, :], cv[:, 2 * q, :], ACT.Silu).then_inc(w["gate_ready"], 1)
                            act.wait_ge(w["hid32_ready"], i * 2 + (f0 + q + 1))
                            f(hidsplit[:, 0, bass.ds(i * 2 + q, 1), :], cv[:, 2 * q:2 * q + 1, :], ACT.Copy).then_inc(w["hid_hi"], 1)
                    at += 2 * nf
                    for n in range(KT):
                        if at + n + LOOK < NFFN:
                            w_hi(l, at + n + LOOK)
                        if part == 0:
                            t = t0 + at + n
                            take(t)
                            freed(f(mb[:, n, :].rearrange("p (z n) -> p z n", z=2), halves(t), ACT.Copy))
                    at += KT
                act.wait_ge(sm["tile_read"], TB[f"fo{l}"])
                for t in range(2):
                    take(TB[f"fo{l}"] + t)
                    if l == 1 and t == 0:
                        act.wait_ge(sm["out_done"], 16 * (16 + 1 + 8 + 88 + KT * (1 + DB) + 1))
                    if l == 0 and t == 0:
                        act.wait_ge(sm["out_done"], 16 * (16 + 1 + 8))
                    s = tset(TB[f"fo{l}"] + t)
                    if t == 0:
                        ins = f(ost[0:126, 0:512], ps[0:126, s:s + 512], ACT.Copy)
                    else:
                        f(ost[0:126, 512:768], ps[0:126, s:s + 256], ACT.Copy)
                        ins = f(ost[0:36, 768:896], ps[0:36, s + 256:s + 384], ACT.Copy)
                    freed(ins)

            ffn(0)
            norm("n3", mb, (sm["tile_read"], TB["f0"] + NFFN - KT))
            for t in range(4):
                m = min(512, NGS - 512 * t)
                take(TB["gst"] + t)
                freed(f(gst[:, 512 * t:512 * t + m], bank2(TB["gst"] + t, m), ACT.Copy))
            norm("n4", x, (sm["x_ready"], KT))

            def diagonals(m, taps):
                for n in taps:
                    f(diag[:, m, n, :], ident, ACT.Copy, scale=pcol("conv_dw_w", n * KT + DW_PE[m])).then_inc(sm["diag_ready"], 1)

            per = -(-CW * len(DW_PE) // KT)
            jobs = [(m, n) for m in range(len(DW_PE)) for n in range(CW)]
            for n in range(KT):
                for m, tap in jobs[per * n:per * n + per]:
                    diagonals(m, [tap])
                ta, tb = TB["glu"] + 2 * n, TB["glu"] + 2 * n + 1
                if n >= 1:
                    act.wait_ge(sm["glu_ready"], n)
                take(ta)
                freed(f(gsig[:, 1, :], bank2(ta), ACT.Identity, bias=pcol("conv_b_in", n)))
                take(tb)
                freed(f(gsig[:, 0, :], bank2(tb), ACT.Sigmoid, bias=pcol("conv_b_in", KT + n)))
            for m, kt in enumerate(DW_PE):
                take(TB["dw"] + m)
                freed(f(cvo[:, kt, :], bank2(TB["dw"] + m), ACT.Identity, bias=pcol("conv_dw_b", kt)))
            take(TB["go"])
            act.wait_ge(sm["out_done"], 16 * (16 + 1 + 8 + 88))
            s = tset(TB["go"])
            freed(f(ost[0:120, 0:256], ps[0:120, s:s + 256], ACT.Copy))
            take(TB["go"] + 1)
            freed(f(ost[:, 256:768], bank2(TB["go"] + 1, 512), ACT.Copy))
            take(TB["ln"])
            freed(f(tmp[:, 3, :], bank2(TB["ln"]), ACT.Copy))
            norm("ln", cvo, (sm["ln_v"], 0), eps=1, first=1)
            for kt in range(KT):
                act.wait_ge(sm["ln_v"], KT + kt + 1)
                f(cvo[:, kt, :], cvo[:, kt, :], ACT.Silu, scale=pcol("conv_ln_w", kt), bias=pcol("conv_ln_b", kt)).then_inc(sm["z_ready"], 1)
            for n in range(KT):
                take(TB["co"] + n)
                freed(f(mb[:, n, :], bank2(TB["co"] + n), ACT.Identity, bias=pcol("conv_b_out", n)))
            norm("n5", mb, (sm["tile_read"], TB["co"]))
            ffn_first(1)
            state_cols("fst1")
            norm("n6", x, (sm["x_ready"], 2 * KT))
            ffn(1)
            norm("n7", mb, (sm["tile_read"], TB["f1"] + NFFN - KT))
            for g in range(5):
                k = P if g < 4 else DEC
                for q in range(2):
                    t = TB["yout"] + 2 * g + q
                    take(t)
                    freed(f(xrows[0:k, g, 512 * q:512 * q + 512], ps[0:k, tset(t):tset(t) + 512], ACT.Copy))

        @block.vector
        def _(dve):
            done = [0]
            v = nc.vector

            def seq(ins):
                ins.then_inc(sm["vec_done"], 1)
                done[0] += 1

            def after():
                if done[0]:
                    dve.wait_ge(sm["vec_done"], done[0])

            def norm_scale(name, first=0):
                dve.wait_ge(sm["tile_read"], TB[name] + first + 1)
                seq(v.reciprocal(tmp[:, 2, :], tmp[:, 2, :]))
                after()

            def prenorm(name, n):
                norm_scale(name)
                for kt in range(KT):
                    v.scalar_tensor_tensor(h[:, kt, :], x[:, kt, :], gain(n, kt), tmp[:, 2, :], ALU.mult, ALU.mult)\
                        .then_inc(sm["h_ready"], 1)

            def prenorm_split(name, n, l):
                norm_scale(name)
                for kt in range(KT + 1):
                    if kt < KT:
                        v.scalar_tensor_tensor(h32[:, kt, :], x[:, kt, :], gain(n, kt), tmp[:, 2, :], ALU.mult, ALU.mult)\
                            .then_inc(FF[l]["h32_ready"], 1)
                    if kt:
                        dve.wait_ge(FF[l]["h_hi"], kt)
                        v.tensor_tensor(hsplit[:, 1, kt - 1, :], h32[:, kt - 1, :], hsplit[:, 0, kt - 1, :].bitcast(F32), ALU.subtract)\
                            .then_inc(FF[l]["h_lo"], 1)

            def postnorm(name, n):
                norm_scale(name)
                for kt in range(KT):
                    seq(v.scalar_tensor_tensor(mb[:, kt, :], mb[:, kt, :], gain(n, kt), tmp[:, 2, :], ALU.mult, ALU.mult))
                    after()
                    v.tensor_tensor(x[:, kt, :], x[:, kt, :], mb[:, kt, :], ALU.add).then_inc(sm["x_ready"], 1)

            dve.wait_ge(sm["const_in"], 16)
            prenorm("n0", 0)
            dve.wait_ge(sm["h_ready"], KT)
            hd = h[:, :, SEQ:T].rearrange("p k (b t) -> p k b t", b=DB)
            xd = xx[:, :, SEQ:T].rearrange("p k (b t) -> p k b t", b=DB)
            go = ost[:, 0:9 * KT].rearrange("p (k c) -> p k c", c=9)
            seq(v.tensor_copy(go[:, :, 0:1], h[:, :, SEQ - 1:SEQ]))
            v.tensor_copy(go[:, :, 1:9], hd[:, :, :, DS - 1]).then_inc(sm["gath_ready"], 1)
            shift = par[:, PCOL["state_rwkv_shift"]:PCOL["state_rwkv_shift"] + DB * KT].rearrange("p (b k) -> p k b", b=DB)
            seq(v.tensor_tensor(xx[:, :, 1:SEQ], h[:, :, 0:SEQ - 1], h[:, :, 1:SEQ], ALU.subtract))
            seq(v.tensor_scalar(xx[:, :, 0:1], h[:, :, 0:1], -1.0, None, ALU.mult))
            for kt in range(KT):
                seq(v.tensor_tensor(xd[:, kt, :, 1:DS], hd[:, kt, :, 0:DS - 1], hd[:, kt, :, 1:DS], ALU.subtract))
            seq(v.tensor_tensor(xd[:, :, :, 0], shift, hd[:, :, :, 0], ALU.subtract))
            seq(v.tensor_scalar(omka[:], par[:, PCOL["rwkv_k_a"]:PCOL["rwkv_k_a"] + KT], -1.0, 1.0, ALU.mult, ALU.add))
            after()
            free = {2: TB["lo1"] + 1, 3: TB["lo1"] + 2, 4: TB["lo1"] + 4, 5: TB["k"] + KT}
            for q, m in enumerate((1, 4, 5, 2, 0, 3)):
                if q in free:
                    dve.wait_ge(sm["tile_full"], free[q])
                for kt in range(KT):
                    v.scalar_tensor_tensor((bufA, bufB)[q % 2][:, kt, :], xx[:, kt, :], pcol("rwkv_mix", m * KT + kt),
                                           h[:, kt, :], ALU.mult, ALU.add).then_inc(sm["xm_ready"], 1)
            dve.wait_ge(sm["xm_ready"], 6 * KT)
            dve.wait_ge(sm["tile_read"], TB["k"] + KT)

            def unit_key(kt):
                dve.wait_ge(sm["tile_read"], TB["kk"] + kt + 1)
                t = tmp[:, 2 + kt % 2, :]
                seq(v.tensor_scalar(t, t, 1e-12, None, ALU.max))
                after()
                seq(v.reciprocal(t, t))
                after()
                v.tensor_tensor(kkb[:, kt, :], kkb[:, kt, :], t, ALU.mult).then_inc(sm["prep_e"], 1)

            for kt in range(KT):
                v.tensor_scalar(kkb[:, kt, :], kb[:, kt, :], pcol("rwkv_k_k", kt), None, ALU.mult).then_inc(sm["prep_s"], 1)
            for kt in range(KT):
                unit_key(kt)
            dve.wait_ge(sm["prep_e"], KT)
            def sums(kt):
                t = tmp[:, 2 * (kt % 2), :]
                u = tmp[:, 2 * (kt % 2) + 1, :]
                after()
                if kt >= 2:
                    dve.wait_ge(sm["prep_done"], kt - 1)
                seq(v.tensor_scalar(u, ag[:, kt, :], pcol("rwkv_k_a", kt), omka[:, kt:kt + 1], ALU.mult, ALU.add))
                seq(v.tensor_tensor_scan(t, con[:, C_SCAN:C_SCAN + T], sg[:, kt, :], 0.0, ALU.mult, ALU.add))
                after()
                seq(v.tensor_tensor(kb[:, kt, :], kb[:, kt, :], u, ALU.mult))
                seq(v.scalar_tensor_tensor(ag[:, kt, :], kkb[:, kt, :], -1.0, ag[:, kt, :], ALU.mult, ALU.mult))
                after()
                v.tensor_tensor(sg[:, kt, :], t, sg[:, kt, :], ALU.subtract).then_inc(sm["wide_ready"], 1)

            def scale(kt):
                t, u = tmp[:, 2 * (kt % 2), :], tmp[:, 2 * (kt % 2) + 1, :]
                dve.wait_ge(sm["v_ready"], 3 * kt + 3)
                seq(v.tensor_tensor(kkb[:, kt, :], kkb[:, kt, :], sg[:, kt, :], ALU.mult))
                seq(v.tensor_tensor(rb[:, kt, :], rb[:, kt, :], u, ALU.mult))
                seq(v.tensor_tensor(kb[:, kt, :], kb[:, kt, :], t, ALU.mult))
                seq(v.tensor_tensor(ag[:, kt, :], ag[:, kt, :], t, ALU.mult))
                seq(v.tensor_copy(pend[:, kt, 0:NCH], u[:, CH - 1:SEQ:CH]))
                after()
                v.tensor_copy(pend[:, kt, NCH:NCH + DB], u[:, SEQ + DS - 1:T:DS]).then_inc(sm["prep_done"], 1)

            sums(0)
            for kt in range(KT):
                if kt + 1 < KT:
                    sums(kt + 1)
                scale(kt)
            ident8 = con[:, C_IS:C_IS + 64].unsqueeze(1).to_broadcast([P, 4, 64])
            dve.wait_ge(sm["prep_done"], KT)
            dve.wait_ge(sm["sd_ready"], 2 * KT)
            seq(v.memset(S, 0.0))
            mm = [0, 0]

            def bk(g, b, n, w):
                o = 2048 * g + 512 * b
                return ps[:, o:o + n * w].rearrange("p (k n) -> p k n", n=w)

            def turn(g):
                mm[g] += 1
                dve.wait_ge(mm_done[g], mm[g])

            def fin(g, ins):
                ins.then_inc(ev_done[g], 1)

            def bc(col, n=64, m=4):
                return con[:, col:col + n].unsqueeze(1).to_broadcast([P, m, n])

            def factors(g, mask):
                turn(g)
                k = slice(4 * g, 4 * g + 4)
                seq(v.tensor_tensor(MbT[:, k, :], bk(g, 0, 4, 128), bc(mask, 128), ALU.mult))
                seq(v.tensor_tensor(MkT[:, k, :], bk(g, 1, 4, 128), bc(mask, 128), ALU.mult))
                seq(v.tensor_copy(Mn[:, k, :], bk(g, 2, 4, 64)))
                after()
                seq(v.tensor_tensor(TT[:, k, :], MbT[:, k, 0:64], bc(C_LVL), ALU.mult))
                seq(v.tensor_tensor(TI[:, k, :], Mn[:, k, :], bc(C_LOW1), ALU.mult))
                after()
                seq(v.tensor_tensor(TT[:, k, :], TT[:, k, :], ident8, ALU.add))
                after()
                fin(g, v.tensor_tensor(TI[:, k, :], TI[:, k, :], ident8, ALU.add))

            def to_tokens(g):
                turn(g)
                k = slice(4 * g, 4 * g + 4)
                seq(v.tensor_copy(Vt[:, k, :], bk(g, 0, 4, 64)))
                seq(v.tensor_copy(Bt[:, k, :], bk(g, 1, 4, 64)))
                after()
                fin(g, v.tensor_copy(Ktk[:, k, :], bk(g, 2, 4, 64)))

            def level(g, n, last, part):
                turn(g)
                k = slice(4 * g, 4 * g + 4)
                if part == 0:
                    fin(g, v.tensor_tensor(Y[:, k, :], bk(g, 0, 4, 64), bc(C_LVL + 64 * n), ALU.mult))
                else:
                    if not last:
                        seq(v.tensor_tensor(TI[:, k, :], TI[:, k, :], bk(g, 2, 4, 64), ALU.add))
                        after()
                    fin(g, v.tensor_tensor(TT[:, k, :], TT[:, k, :], bk(g, 1, 4, 64), ALU.add))

            def both_groups(fn, *args):
                for g in range(2):
                    fn(g, *args)

            def copy_bank(g, dst, b):
                turn(g)
                fin(g, v.tensor_copy(dst[:, 4 * g:4 * g + 4, :], bk(g, b, 4, 64)))

            for c in range(NCH):
                both_groups(factors, C_MASK)
                both_groups(to_tokens)
                for n in range(1, len(LEVELS)):
                    for part in range(2):
                        both_groups(level, n, n == len(LEVELS) - 1, part)
                both_groups(copy_bank, Rm, 0)
                both_groups(copy_bank, SA, 1)
                for g in range(2):
                    turn(g)
                    k = slice(4 * g, 4 * g + 4)
                    after()
                    seq(v.tensor_copy(yb[:, k, CH * c:CH * c + CH], bk(g, 3, 4, 64)))
                    seq(v.tensor_tensor(S[:, k, :], S[:, k, :], pend[:, k, c:c + 1].to_broadcast([P, 4, 64]), ALU.mult))
                    after()
                    fin(g, v.tensor_tensor(S[:, k, :], S[:, k, :], bk(g, 2, 4, 64), ALU.add))
            both_groups(factors, C_MASKD)
            both_groups(to_tokens)
            own = con[:, C_B8:C_B8 + 8].unsqueeze(2).to_broadcast([P, DB, 64])

            def masked_a(g, i):
                flat = tmp[:, 2 * g + i % 2, 0:512]
                am = flat.rearrange("p (b c t) -> p b c t", b=DB, t=DS)
                src = kkb[:, 4 * g + i, SEQ:T].rearrange("p (c t) -> p c t", t=DS)
                seq(v.memset(flat, 0.0))
                after()
                for b in range(DB):
                    seq(v.tensor_copy(am[:, b, b, :], src[:, b, :]))
                after()

            def masked_rows(g, i):
                for m, src in enumerate((SA, Vt)):
                    o = tmp[:, 2 * g + m, 0:512].rearrange("p (b n) -> p b n", b=DB)
                    seq(v.tensor_tensor(o, src[:, 4 * g + i, :].unsqueeze(1).to_broadcast([P, DB, 64]), own, ALU.mult))
                after()

            for n in (1, 2):
                for part in range(2):
                    for g in range(2):
                        if n == 2 and part == 1:
                            masked_a(g, 0)
                        level(g, n, n == 2, part)
            for i in range(4):
                for g in range(2):
                    turn(g)
                    if i < 3:
                        masked_a(g, i + 1)
                    fin(g, v.tensor_copy(Rm[:, 4 * g + i, :], bk(g, 0, 4, 64)[:, i, :]))
            for g in range(2):
                turn(g)
                seq(v.tensor_copy(SA[:, 4 * g:4 * g + 4, :], bk(g, 1, 4, 64)))
                after()
                masked_rows(g, 0)
                fin(g, v.tensor_copy(omka[:, g:g + 1], omka[:, g:g + 1]))
            for i in range(4):
                for g in range(2):
                    k = 4 * g + i
                    turn(g)
                    seq(v.tensor_copy(yb[:, k, SEQ:T], bk(g, 3, 1, 64)[:, 0, :]))
                    if i < 3:
                        masked_rows(g, i + 1)
                    seq(v.tensor_tensor(Sd[:, k], Sd[:, k], pend[:, k, NCH:NCH + DB].unsqueeze(2).to_broadcast([P, DB, 64]), ALU.mult))
                    after()
                    fin(g, v.tensor_tensor(Sd[:, k], Sd[:, k], bk(g, 2, DB, 64), ALU.add))
            dve.wait_ge(sm["state_out"], 1 + KT)
            for kt in range(KT):
                t = TB["post"] + 4 * kt
                if kt:
                    dve.wait_ge(sm["z_ready"], kt)
                v.scalar_tensor_tensor(tmp[:, 1, :], rb[:, kt, :], pcol("rwkv_r_k", kt), kb[:, kt, :], ALU.mult, ALU.mult)\
                    .then_inc(sm["post_v"], 1)
                dve.wait_ge(sm["tile_read"], t + 1)
                v.tensor_tensor(yg[:, kt, :], yg[:, kt, :], tmp[:, 2, :], ALU.subtract).then_inc(sm["post_v"], 1)
                dve.wait_ge(sm["tile_read"], t + 4)
                seq(v.reciprocal(tmp[:, 2, :], tmp[:, 2, :]))
                seq(v.tensor_tensor(tmp[:, 3, :], tmp[:, 3, :], vb[:, kt, :], ALU.mult))
                after()
                seq(v.scalar_tensor_tensor(yg[:, kt, :], yg[:, kt, :], pcol("rwkv_lnx_w", kt), tmp[:, 2, :], ALU.mult, ALU.mult))
                after()
                seq(v.scalar_tensor_tensor(yg[:, kt, :], yg[:, kt, :], pcol("rwkv_lnx_b", kt), tmp[:, 3, :], ALU.add, ALU.add))
                after()
                v.tensor_tensor(yg[:, kt, :], yg[:, kt, :], tmp[:, 0, :], ALU.mult).then_inc(sm["z_ready"], 1)
            postnorm("n1", 1)
            dve.wait_ge(sm["x_ready"], KT)
            prenorm_split("n2", 2, 0)

            def ffn(l):
                w = FF[l]
                chain = w["cvd"]
                per = 4 * 5
                for z in range(4):
                    v.memset(raw[:, z, 0:2], 0.0).then_inc(w["no_hist"], 1)
                t0 = TB[f"f{l}"]
                at = 0
                for part, (f0, nf) in enumerate(PARTS):
                    with dve.Fori(0, nf // 2) as i:
                        for q in range(2):
                            for z in range(2):
                                j = 2 * q + z
                                dve.wait_ge(sm["tile_read"], i * 4 + (t0 + at + j + 1))
                                rp = raw[:, j, 0:2 + SEQ]
                                rd = raw[:, j, 2 + SEQ:RAW].rearrange("p (b t) -> p b t", b=DB)
                                cd = cv[:, j, SEQ:T].rearrange("p (b t) -> p b t", b=DB)

                                def tap(n):
                                    o = PCOL["ffn_dw_w"] + (3 * l + n) * 2 * FT + z * FT + f0 + q
                                    return par[:, bass.ds(i * 2 + o, 1)]

                                bias = par[:, bass.ds(i * 2 + (PCOL["ffn_dw_b"] + l * 2 * FT + z * FT + f0 + q), 1)]
                                v.tensor_scalar(cv[:, j, 0:SEQ], rp[:, 0:SEQ], tap(0), bias, ALU.mult, ALU.add).then_inc(chain, 1)
                                v.tensor_scalar(cd, rd[:, :, 0:DS], tap(0), bias, ALU.mult, ALU.add).then_inc(chain, 1)
                                for n in (1, 2):
                                    dve.wait_ge(chain, i * per + (f0 // 2 * per + 5 * j + 2 * n))
                                    v.scalar_tensor_tensor(cv[:, j, 0:SEQ], rp[:, n:n + SEQ], tap(n), cv[:, j, 0:SEQ], ALU.mult, ALU.add).then_inc(chain, 1)
                                    ins = v.scalar_tensor_tensor(cd, rd[:, :, n:n + DS], tap(n), cd, ALU.mult, ALU.add)
                                    ins.then_inc(chain if n == 1 else w["conv_ready"], 1)
                            dve.wait_ge(w["gate_ready"], i * 2 + (f0 + q + 1))
                            dve.wait_ge(w["conv_ready"], i * 4 + (2 * f0 + 2 * q + 2))
                            dve.wait_ge(chain, i * per + (f0 // 2 * per + 10 * q + 10))
                            v.tensor_tensor(cv[:, 2 * q, :], cv[:, 2 * q, :], cv[:, 2 * q + 1, :], ALU.mult)\
                                .then_inc(w["hid32_ready"], 1)
                            dve.wait_ge(w["hid_hi"], i * 2 + (f0 + q + 1))
                            v.tensor_tensor(hidsplit[:, 1, bass.ds(i * 2 + q, 1), :], cv[:, 2 * q:2 * q + 1, :],
                                            hidsplit[:, 0, bass.ds(i * 2 + q, 1), :].bitcast(F32), ALU.subtract)\
                                .then_inc(w["hid_lo"], 1)
                    at += 2 * nf
                    if part:
                        for n in range(KT):
                            t = t0 + at + n
                            if n == 0:
                                dve.wait_ge(sm["tile_read"], t)
                            dve.wait_ge(sm["tile_full"], t + 1)
                            o = mb[:, n, :].rearrange("p (z n) -> p z n", z=2)
                            b = ps[:, tset(t):tset(t) + 1024].rearrange("p (z n) -> p z n", z=2)[:, :, 0:HALF]
                            ins = v.tensor_tensor(o, o, b, ALU.add)
                            ins.then_inc(sm["tile_read"], 1)
                    at += KT

            ffn(0)
            postnorm("n3", 3)
            dve.wait_ge(sm["x_ready"], 2 * KT)
            prenorm("n4", 4)
            dve.wait_ge(sm["tile_read"], TB["gst"] + 4)
            seq(v.memset(gb[:, :, 0:NSTATE], 0.0))
            gs = gst.rearrange("p (b w k) -> p k b w", b=DB, k=KT)
            for kt in range(KT):
                seq(v.tensor_copy(gd[:, kt, :, 0:NSTATE], gs[:, kt]))

            def glu(kt):
                dve.wait_ge(sm["tile_read"], TB["glu"] + 2 * kt + 2)
                seq(v.tensor_tensor(gb[:, kt, NSTATE:NSTATE + SEQ], gsig[:, 1, 0:SEQ], gsig[:, 0, 0:SEQ], ALU.mult))
                after()
                v.tensor_tensor(gd[:, kt, :, NSTATE:NSTATE + DS], gsig[:, 1, SEQ:T].rearrange("p (b t) -> p b t", b=DB),
                                gsig[:, 0, SEQ:T].rearrange("p (b t) -> p b t", b=DB), ALU.mult).then_inc(sm["glu_ready"], 1)

            glu(0)
            done_glu = 1
            step = 0
            for kt in DW_DVE:
                cd = cvo[:, kt, SEQ:T].rearrange("p (b t) -> p b t", b=DB)
                while done_glu <= kt:
                    glu(done_glu)
                    done_glu += 1
                dve.wait_ge(sm["glu_ready"], kt + 1)
                for n in range(CW):
                    if step % GLU_EVERY == GLU_EVERY - 1 and done_glu < KT:
                        glu(done_glu)
                        done_glu += 1
                    step += 1
                    w = pcol("conv_dw_w", n * KT + kt)
                    after()
                    for dst, src in ((cvo[:, kt, 0:SEQ], gb[:, kt, n:n + SEQ]), (cd, gd[:, kt, :, n:n + DS])):
                        if n == 0:
                            ins = v.tensor_scalar(dst, src, w, pcol("conv_dw_b", kt), ALU.mult, ALU.add)
                        else:
                            ins = v.scalar_tensor_tensor(dst, src, w, dst, ALU.mult, ALU.add)
                        if n == CW - 1 and dst is cd:
                            ins.then_inc(sm["conv_done"], 1)
                        else:
                            seq(ins)
            dve.wait_ge(sm["tile_full"], TB["glu"] + 2 * KT)
            dve.wait_ge(sm["glu_ready"], KT)
            gp = arena[:, A_H:A_H + 240].rearrange("p (k w) -> p k w", w=NSTATE)
            gt = arena[:, A_H + 240:A_H + 752].rearrange("p (k b t) -> p k b t", k=KT, b=DB)
            seq(v.tensor_copy(gp, gb[:, :, SEQ:SEQ + NSTATE]))
            for kt in range(KT):
                ins = v.tensor_copy(gt[:, kt], gd[:, kt, :, NSTATE:NSTATE + DS])
                if kt < KT - 1:
                    seq(ins)
            ins.then_inc(sm["gath_ready"], 1)
            dve.wait_ge(sm["tile_read"], TB["ln"] + 1)
            dve.wait_ge(sm["conv_done"], len(DW_DVE))
            for kt in range(KT):
                v.tensor_tensor(cvo[:, kt, :], cvo[:, kt, :], tmp[:, 3, :], ALU.subtract).then_inc(sm["ln_v"], 1)
            norm_scale("ln", 1)
            dve.wait_ge(sm["ln_v"], KT)
            for kt in range(KT):
                v.tensor_tensor(cvo[:, kt, :], cvo[:, kt, :], tmp[:, 2, :], ALU.mult).then_inc(sm["ln_v"], 1)
            postnorm("n5", 5)
            dve.wait_ge(sm["x_ready"], 3 * KT)
            prenorm_split("n6", 6, 1)
            ffn(1)
            postnorm("n7", 7)

        @block.gpsimd
        def _(pool):
            p = nc.gpsimd
            pool.wait_ge(sm["prep_done"], KT)
            for c in range(NCH + 1):
                for g in range(2):
                    if c >= 2:
                        pool.wait_ge(mm_done[g], STAGES * (c - 2) + 2)
                    k = slice(4 * g, 4 * g + 4)
                    for dst, src in ((bbar, ag), (kbar, kb)):
                        if c < NCH:
                            ins = p.tensor_tensor(dst[:, c % 2, k, :], src[:, k, CH * c:CH * c + CH],
                                                  pend[:, k, c:c + 1].to_broadcast([P, 4, CH]), ALU.mult)
                            ins.then_inc(sm["bar_ready"], 1)
                        else:
                            for i in range(4):
                                o = dst[:, c % 2, 4 * g + i, :].rearrange("p (b t) -> p b t", b=DB)
                                ins = p.tensor_tensor(o, src[:, 4 * g + i, SEQ:T].rearrange("p (b t) -> p b t", b=DB),
                                                      pend[:, 4 * g + i, NCH:NCH + DB].unsqueeze(2).to_broadcast([P, DB, DS]), ALU.mult)
                                if i < 3:
                                    ins.then_inc(sm["pool_done"], 1)
                            pool.wait_ge(sm["pool_done"], 3 * (2 * g + (dst is kbar)) + 3)
                            ins.then_inc(sm["bar_ready"], 1)

            def ffn(l):
                w = FF[l]
                st = fst[:].rearrange("p (b w f) -> p b w f", b=DB, w=2)

                def decode(j):
                    return raw[:, j, 2 + SEQ:RAW].rearrange("p (b t) -> p b t", b=DB)

                def w_lo(at, i=None):
                    pool.wait_ge(w["w_hi"], at + 1 + (0 if i is None else i * 4))
                    p.tensor_tensor(wsplit[:, at % 4, 1], ring[:, at % 2], wsplit[:, at % 4, 0].bitcast(F32), ALU.subtract)\
                        .then_inc(w["w_lo"], 1)

                def tails(i, j):
                    pool.wait_ge(sm["tile_read"], i * 4 + (t0 + at + j + 1))
                    f = (j % 2) * FT + j // 2 + f0
                    o = fo[:, bass.ds(i * 2 + f, 1), :]
                    p.tensor_copy(o[:, :, 0:2], raw[:, j:j + 1, SEQ:SEQ + 2]).then_inc(w["tails"], 1)
                    p.tensor_copy(o[:, :, 2:18].rearrange("p o (b t) -> p (o b) t", t=2), decode(j)[:, :, DS:DS + 2])\
                        .then_inc(w["tails"], 1)

                t0 = TB[f"f{l}"]
                for n in range(LOOK):
                    w_lo(n)
                pool.wait_ge(w["no_hist"], 4)
                pool.wait_ge(sm["tile_read"], TB[f"fst{l}"] + 2)
                for j in range(4):
                    p.tensor_copy(decode(j)[:, :, 0:2], st[:, :, :, (j % 2) * FT + j // 2]).then_inc(w["hist_ready"], 1)
                at = 0
                for part, (f0, nf) in enumerate(PARTS):
                    last = part == len(PARTS) - 1
                    with pool.Fori(0, nf // 2 - last) as i:
                        for j in range(4):
                            w_lo(at + j + LOOK, i)
                            tails(i, j)
                            pool.wait_ge(w["conv_ready"], i * 4 + (2 * f0 + j + 1))
                            pool.wait_ge(w["tails"], i * 8 + (4 * f0 + 2 * j + 2))
                            f = (j % 2) * FT + j // 2 + 2 + f0
                            src = st[:, :, :, bass.ds(i * 2 + f, 1)].rearrange("p b w o -> p b (w o)")
                            p.tensor_copy(decode(j)[:, :, 0:2], src).then_inc(w["hist_ready"], 1)
                    if last:
                        for j in range(4):
                            w_lo(at + 2 * nf - 4 + j + LOOK)
                            tails(nf // 2 - 1, j)
                    at += 2 * nf
                    for n in range(KT):
                        if at + n + LOOK < NFFN:
                            w_lo(at + n + LOOK)
                    at += KT

            ffn(0)
            ffn(1)


def n_par_dmas():
    n = r = 0
    for _, m in PARAMS:
        at = 0
        while at < m:
            k = min(m - at, P - (r + at) % P)
            n += 1
            at += k
        r += m
    return n


OUTS = [("y_prompt", (1, SEQ, D)), ("y_sample", (DB, DS, D)), ("p_wkv", (1, 1, NH, HS, HS)), ("p_shift", (1, 1, D)),
        ("p_glu", (1, 1, NSTATE, D)), ("p_ffn", (2, 1, 2, 2 * F)), ("s_wkv", (1, DB, NH, HS, HS)), ("s_shift", (1, DB, D)),
        ("s_glu", (1, DB, NSTATE, D)), ("s_ffn", (2, DB, 2, 2 * F))]


def kernel(**inputs):
    import concourse.bacc as bacc
    from concourse.bass_utils import run_bass_kernel_spmd

    nc = bacc.Bacc("TRN2", target_bir_lowering=False, num_devices=1)
    arrays = {n: np.ascontiguousarray(v) for n, v in inputs.items() if np.asarray(v).size}
    arrays["consts"] = constants()
    args = {n: nc.dram_tensor(n, v.shape, mybir.dt.from_np(v.dtype), kind="ExternalInput").ap() for n, v in arrays.items()}
    outs = {n: nc.dram_tensor("out_" + n, s, F32, kind="ExternalOutput").ap() for n, s in OUTS}
    build(nc, args, outs)
    got = run_bass_kernel_spmd(nc, [arrays], core_ids=[0]).results[0]
    return tuple(got["out_" + n] for n, _ in OUTS)
```

```python
from contextlib import ExitStack
import math

import numpy as np
import concourse.bass as bass
import concourse.mybir as mybir

ALU = mybir.AluOpType
ACT = mybir.ActivationFunctionType
F32 = mybir.dt.float32
F32R = mybir.dt.float32r

P = 128
D = 1024
SEQ = 512
DB, DS = 8, 8
DEC = DB * DS
T = SEQ + DEC
KT = D // P
HS = 64
NH = D // HS
CH = 64
NCH = SEQ // CH
CW = 31
F = ((8 * D // 3 + 127) // 128) * 128
FT = F // P
LW, LA, LG = 64, 64, 160
NORM_EPS, LN_EPS, LNX_EPS = 1e-6, 1e-5, 64e-5
LAM = math.exp(-0.5)
NSTATE = CW - 1

C_ID, C_MEAN, C_HEAD = 0, 128, 256
C_CEN, C_HSUM = 384, 512
C_MASK, C_MASKD = C_HSUM + 32, C_HSUM + 96
LEVELS = [1, 2, 4, 8, 16, 32]
C_LVL = C_MASKD + 64
C_LOW1 = C_LVL + 64 * (len(LEVELS) - 1)
C_IS = C_LOW1 + 64
C_BD = C_IS + 64
C_SCAN = C_BD + 3 * P
C_B8 = C_SCAN + T
C_EPS = C_B8 + 8
NCONST = C_EPS + 4


def constants():
    c = np.zeros((P, NCONST), np.float32)
    i = np.arange(P)
    s = i % CH
    t = np.arange(CH)
    c[i, C_ID + i] = 1.0
    c[:, C_MEAN:C_MEAN + P] = 1.0 / D
    c[:, C_HEAD:C_HEAD + P] = (i[:, None] // HS == i[None, :] // HS)
    same = s[:, None] // DS == t[None, :] // DS
    head = i[:, None] // HS == i[None, :] // HS
    c[:, C_CEN:C_CEN + P] = (i[:, None] == i[None, :]) - head / HS
    c[:, C_HSUM + 14] = i < HS
    c[:, C_HSUM + 15] = i >= HS
    c[:, C_MASK:C_MASK + 64] = s[:, None] <= t
    c[:, C_MASKD:C_MASKD + 64] = (s[:, None] <= t) & same
    strict = (s[:, None] < t, (s[:, None] < t) & same)
    for n, m in enumerate(LEVELS):
        pair = (s[:, None] // (2 * m) == t // (2 * m)) & (s[:, None] % (2 * m) < m) & (t % (2 * m) >= m)
        if n == 0:
            strict += (pair,)
        else:
            c[:, C_LVL + 64 * (n - 1):C_LVL + 64 * n] = pair
    for n, m in enumerate(strict):
        c[:, C_BD + P * n:C_BD + P * n + P] = np.tile(m, 2) * head
    c[:, C_LOW1:C_LOW1 + 64] = (s[:, None] // 2 == t // 2) & (s[:, None] > t)
    c[:, C_IS:C_IS + 64] = s[:, None] == t
    tok = np.arange(T)
    c[:, C_SCAN:C_SCAN + T] = np.where(tok < SEQ, tok % CH != 0, tok % DS != 0)
    c[:, C_B8:C_B8 + 8] = s[:, None] // DS == np.arange(DB)
    c[:, C_EPS:C_EPS + 4] = [NORM_EPS, LN_EPS, LNX_EPS, 0.0]
    return c


PARAMS = [("norm_gain", 8 * KT), ("rwkv_mix", 6 * KT), ("rwkv_w0", KT), ("rwkv_a0", KT), ("rwkv_k_k", KT),
          ("rwkv_k_a", KT), ("rwkv_r_k", KT), ("rwkv_lnx_w", KT), ("rwkv_lnx_b", KT), ("conv_b_in", 2 * KT),
          ("conv_dw_w", CW * KT), ("conv_dw_b", KT), ("conv_ln_w", KT), ("conv_ln_b", KT), ("conv_b_out", KT),
          ("ffn_dw_w", 2 * 3 * 2 * FT), ("ffn_dw_b", 2 * 2 * FT), ("state_rwkv_shift", DB * KT)]
PCOL = {}
_n = 0
for _name, _rows in PARAMS:
    PCOL[_name] = _n
    _n += _rows
NPC = _n
NPG = -(-NPC // P)
NFS = DB * 2 * 2 * FT
NFG = -(-NFS // P)
NGS = DB * NSTATE * KT
NGG = NGS // P

PARTS = []
_n = 0
while _n < FT:
    PARTS.append((_n, min(KT, FT - _n)))
    _n += KT
NFFN = 2 * FT + len(PARTS) * KT
HALF = T // 2
LOOK = 3

DW_DVE, DW_POOL, DW_PE = (0, 2, 4, 6, 7), 1, (5, 3)
DW_TAPS = {5: 20, 3: CW}
DW_JOBS = [(kt, n) for kt in DW_PE for n in range(DW_TAPS[kt])]

TILES = [("xin", 10), ("n0", 1), ("par", 2), ("shift", 1), ("lo1", 4), ("lo2", 2 * KT), ("k", KT),
         ("r", KT), ("v", 3), ("kks", 1), ("v3", 2), ("kk", KT), ("v5", 3), ("pc", KT), ("pv", 1), ("pb", 1),
         ("pz", 3 * KT), ("wo", KT), ("n1", 1), ("fst0", 2), ("n2", 1),
         ("f0", NFFN), ("fo0", 2), ("n3", 1),
         ("gst", 4), ("n4", 1), ("glu", 2 * KT), ("dw", len(DW_PE)), ("go", 2), ("ln", 2), ("co", KT), ("n5", 1), ("fst1", 2), ("n6", 1),
         ("f1", NFFN), ("fo1", 2), ("n7", 1), ("yout", 10)]
TB = {}
_n = 0
for _name, _rows in TILES:
    TB[_name] = _n
    _n += _rows

WSEQ = [("k", KT), ("r", KT), ("v", KT), ("wo", KT), ("glu", 2 * KT), ("co", KT)]
WB = {}
_n = 0
for _name, _rows in WSEQ:
    WB[_name] = _n
    _n += _rows
RING = 4
VTILES = [TB["v"] + j for j in range(3)] + [TB["v3"] + j for j in range(2)] + [TB["v5"] + j for j in range(3)]
WTILE = [VTILES[j] if n == "v" else TB[n] + j for n, m in WSEQ for j in range(m)]

RAW = 2 + SEQ + DB * (2 + DS)
GB = NSTATE + SEQ + DB * (NSTATE + DS)

REG = KT * T
A_H, A_XX, A_A, A_B, A_SG, A_AG, A_K, A_R = [REG * n for n in range(8)]
A_M = A_R
A_RING = 8 * REG
A_H32 = 2 * REG
A_WSPLIT = 4 * REG
A_RAW = A_WSPLIT + 4 * 2 * KT * P
A_CV = A_RAW + 4 * RAW
A_FO = A_CV + 4 * T
A_FR = A_FO
A_FST = A_RING + 2 * KT * P
assert A_FO + max(FT * 2 * 18, NFG * P) <= A_M and A_FST + NFS <= A_RING + RING * KT * P
A_GB = A_XX
A_GR = A_GB + KT * GB
A_CO = A_GR + NGS
A_SIG = A_CO + REG
GLU_EVERY = 16
A_DIAG = A_SIG + 2 * T
A_PTMP = A_DIAG + len(DW_JOBS) * P
assert A_PTMP + T <= A_FR
NSOUT = 2 * DB


def build(nc, a, out):
    with ExitStack() as ctx:
        def sb(name, shape):
            return ctx.enter_context(nc.sbuf_tensor(name, shape, F32))

        def rounded(name, shape):
            return ctx.enter_context(nc.sbuf_tensor(name, shape, F32R))

        def sem(name):
            return ctx.enter_context(nc.semaphore(name))

        x = sb("x", [P, KT, T])
        con = sb("con", [P, NCONST])
        par = sb("par", [P, NPC])
        hg = sb("hg", [P, 2, T])
        tmp = sb("tmp", [P, 4, T])
        ost = sb("ost", [P, 896])
        pend = sb("pend", [P, KT, 16])
        omka = sb("omka", [P, KT])
        scrap = sb("scrap", [P, 12])
        with nc.sbuf_tensor("arena", [P, A_RING + RING * KT * P], F32) as arena:
            pass
        hsplit = rounded("hsplit", [P, 2, KT, T])
        hidsplit = rounded("hidsplit", [P, 2, KT, T])
        wsplit = rounded("wsplit", [P, 4, 2, KT, P])
        ring = arena[:, A_RING:A_RING + RING * KT * P].rearrange("p (s k n) -> p s k n", s=RING, n=P)
        ps = ctx.enter_context(nc.psum_tensor("ps", [P, 4096], F32))

        def region(at, n=KT, w=T):
            return arena[:, at:at + n * w].rearrange("p (k t) -> p k t", t=w)

        h, xx, bufA, bufB = region(A_H), region(A_XX), region(A_A), region(A_B)
        sg, ag, kb, rb, mb = region(A_SG), region(A_AG), region(A_K), region(A_R), region(A_M)
        kkb, vb, yb = xx, bufA, sg
        lo1 = arena[:, A_R:A_R + KT * 288].rearrange("p (k n) -> p k n", n=288)
        hwa = arena[0:64, A_R + KT * 288:A_R + KT * 288 + 2 * T].rearrange("p (k t) -> p k t", t=T)
        lo2 = arena[0:64, A_K:A_K + 2 * D].rearrange("p (k n) -> p k n", n=D)
        lg2 = arena[:, A_H:A_H + 2 * D].rearrange("p (k n) -> p k n", n=D)
        rows = arena[:, A_A:A_A + NPG * P].rearrange("p (g n) -> p g n", n=P)
        fst = arena[:, A_FST:A_FST + NFS]
        frows = arena[:, A_FR:A_FR + NFG * P].rearrange("p (g n) -> p g n", n=P)
        grows = arena[:, A_B + REG:A_B + REG + NGG * P].rearrange("p (g n) -> p g n", n=P)
        xrows = arena[:, A_SG:A_SG + 5 * D].rearrange("p (g n) -> p g n", n=D)
        h32 = region(A_H32)
        raw = arena[:, A_RAW:A_RAW + 4 * RAW].rearrange("p (q n) -> p q n", q=4)
        cv = arena[:, A_CV:A_CV + 4 * T].rearrange("p (q n) -> p q n", q=4)
        fo = arena[:, A_FO:A_FO + 2 * FT * 18].rearrange("p (f n) -> p f n", n=18)
        gb = region(A_GB, KT, GB)
        gst = arena[:, A_GR:A_GR + NGS]
        cvo = region(A_CO)
        gsig = region(A_SIG, 2)
        gd = gb[:, :, NSTATE + SEQ:GB].rearrange("p k (b t) -> p k b t", b=DB)
        diag = region(A_DIAG, len(DW_JOBS), P)
        ident = con[:, C_ID:C_ID + P]

        def small(at, n=P, k=KT):
            return arena[:, at:at + k * n].rearrange("p (k n) -> p k n", n=n)

        Bf, Kf, Af = [small(A_H + KT * P * n) for n in range(3)]
        MbTr, MkTr = [small(A_H + 3 * KT * P + KT * 64 * n, 64) for n in range(2)]
        Vt, Bt, Ktk, MkT = [small(A_B + KT * P * n) for n in range(4)]
        S = [small(at + 4 * KT * P, k=4) for at in (A_H, A_B)]
        Mn, TT, TI, Y = [small(A_RING + KT * P * n) for n in range(4)]
        Rm, SA, Vf = Y, TI, Y
        AR = tmp[:].rearrange("p q t -> p (q t)")[:, 0:2 * KT * P].rearrange("p (v k n) -> p v k n", v=2, n=P)
        Snat = ag[:, :, 0:SEQ].rearrange("p k (b n) -> p k b n", n=P)
        Sd = kkb[:, :, 0:SEQ]
        Rf, Yr = Kf, Bf
        kn = ost[0:NH, 256:256 + T]
        hsum = [arena[0:NH, A_H + 2 * D + T * n:A_H + 2 * D + T * n + T] for n in range(2)]
        sqh = region(A_B)
        sel = [arena[0:NH, at:at + D] for at in (A_H, A_H + 2 * D + 2 * T)]
        rinv = [h[:, k + 2, :] if k + 2 < KT else tmp[:, k + 2 - KT, :] for k in range(KT)]
        yg = yb

        def pcol(name, i):
            return par[:, PCOL[name] + i:PCOL[name] + i + 1]

        def gain(n, kt):
            return pcol("norm_gain", n * KT + kt)

        NAMES = ["const_in", "par_in", "lo1_in", "lo2_in", "lg2_in", "sd_in", "fst_in", "gst_in", "out_done",
                 "tile_full", "tile_read", "sq_ready", "sq_used", "x_ready", "h_ready", "xm_ready", "vec_done",
                 "v_ready", "wide_ready", "prep_sq", "prep_s", "prep_done", "kn_ready", "unit_done", "gath_ready",
                 "rk_ready", "sel_ready", "rstd_ready", "z_ready", "zeroed", "sd_turned", "sd_ready", "rf_ready",
                 "rows_ready", "snat_ready", "state_out", "glu_ready", "conv_done", "conv_pool", "pool_tap",
                 "diag_ready", "ln_v"]
        sm = {n: sem(n) for n in NAMES}
        w_in = [sem(f"w_in{i}") for i in range(RING)]
        fw_in = [[sem(f"fw_in{l}{i}") for i in range(2)] for l in range(2)]
        xt_in = [sem(f"xt_in{i}") for i in range(5)]
        mm_done = [sem(f"mm_done{g}") for g in range(2)]
        ev_done = [sem(f"ev_done{g}") for g in range(2)]
        exp_ready = [sem(f"exp_ready{g}") for g in range(2)]
        mn_ready = [sem(f"mn_ready{g}") for g in range(2)]
        y_read = [sem(f"y_read{g}") for g in range(2)]
        FF = [{n: sem(f"{n}{l}") for n in ("raw_ready", "hist_ready", "conv_ready", "gate_ready", "hid_ready",
                                           "tails", "no_hist", "cvd", "w_hi", "w_lo", "h32_ready",
                                           "h_hi", "h_lo", "hid32_ready", "hid_hi", "hid_lo")} for l in range(2)]
        block = ctx.enter_context(nc.Block())

        def tset(t):
            return (t % 4) * 1024

        def bank2(t, n=T, m=P):
            return ps[0:m, tset(t):tset(t) + n]

        @block.sync
        def _(eng):
            def load(dst, src, s):
                eng.dma_start(dst, src).then_inc(s, 16)

            load(con[:], a["consts"], sm["const_in"])
            for g in range(4):
                load(xrows[:, g, :], a["x_prompt"][0, g * P:(g + 1) * P, :], xt_in[g])
            load(xrows[0:DEC, 4, :], a["x_sample"].rearrange("b t d -> (b t) d"), xt_in[4])
            r = 0
            for name, m in PARAMS:
                src = a[name]
                flat = src.rearrange(" ".join(f"d{i}" for i in range(len(src.shape))) + " -> ("
                                     + " ".join(f"d{i}" for i in range(len(src.shape))) + ")")
                flat = flat.rearrange("(r c) -> r c", c=P)
                at = 0
                while at < m:
                    g, p = (r + at) // P, (r + at) % P
                    k = min(m - at, P - p)
                    load(rows[p:p + k, g, :], flat[at:at + k, :], sm["par_in"])
                    at += k
                r += m

            def load_fst(dst, l, s):
                f = a["state_ffn_conv"][l].rearrange("b w (k p) -> (b w k) p", p=P)
                full = NFS // P
                load(dst[:, 0:full, :], f[0:full * P, :].rearrange("(g p) c -> p g c", p=P), s)
                load(dst[0:NFS - full * P, full, :], f[full * P:NFS, :], s)

            for name, o, m in (("rwkv_w1", 0, LW), ("rwkv_a1", LW, LA), ("rwkv_g1", LW + LA, LG)):
                load(lo1[:, :, o:o + m], a[name][0].rearrange("(k p) n -> p k n", p=P), sm["lo1_in"])
            load(lo2[:, 0, :], a["rwkv_w2"][0], sm["lo2_in"])
            load(lo2[:, 1, :], a["rwkv_a2"][0], sm["lo2_in"])

            def wtile(w, src, n):
                load(ring[:, w % RING], src[:, n * P:(n + 1) * P].rearrange("(k p) n -> p k n", p=P), w_in[w % RING])

            def weights(name, src, order, first=0):
                for j, n in list(enumerate(order))[first:]:
                    w = WB[name] + j
                    if w >= RING:
                        eng.wait_ge(sm["tile_full"], WTILE[w - RING] + 1)
                    wtile(w, src, n)

            weights("k", a["rwkv_wk"][0], range(KT))
            weights("r", a["rwkv_wr"][0], range(KT))
            weights("v", a["rwkv_wv"][0], range(KT))
            def store(dst, src):
                eng.dma_start(dst, src).then_inc(sm["out_done"], 16)
                n_out[0] += 1

            n_out = [0]

            eng.wait_ge(sm["tile_read"], TB["shift"] + 1)
            for kt in range(KT):
                store(out["p_shift"][0, :, kt * P:(kt + 1) * P], ost[9 * kt:9 * kt + 1, P:2 * P])
                store(out["s_shift"][0, :, kt * P:(kt + 1) * P], ost[9 * kt + 1:9 * kt + 9, P:2 * P])
            for b in range(DB // 2):
                for g in range(2):
                    eng.wait_ge(exp_ready[g], 2 * b + 2)
                for q in range(2):
                    for e in range(2):
                        src = a["state_rwkv_wkv"][0, 2 * b + q].rearrange("(k e) i j -> e i k j", e=2)[e]
                        load(Snat[64 * q:64 * q + 64, :, b, 64 * e:64 * e + 64], src, sm["sd_in"])
            eng.wait_ge(sm["snat_ready"], 1)
            load(lg2[:, 0, :], a["rwkv_g2"][0, 0:P, :], sm["lg2_in"])
            load(lg2[0:LG - P, 1, :], a["rwkv_g2"][0, P:LG, :], sm["lg2_in"])
            for j in range(RING):
                wtile(WB["wo"] + j, a["rwkv_wo"][0], j)
            eng.wait_ge(sm["state_out"], 1)
            store(out["p_wkv"][0, 0].rearrange("(k e) i j -> (e i) k j", e=2), ost[:, 256:768].rearrange("p (k j) -> p k j", j=64))
            eng.wait_ge(sm["state_out"], 1 + KT)
            for b in range(DB):
                for e in range(2):
                    store(out["s_wkv"][0, b].rearrange("(k e) i j -> e i k j", e=2)[e],
                          Snat[64 * (b % 2):64 * (b % 2) + 64, :, b // 2, 64 * e:64 * e + 64])
            weights("wo", a["rwkv_wo"][0], range(KT), first=RING)
            eng.wait_ge(sm["z_ready"], KT)
            load_fst(frows, 0, sm["fst_in"])

            def ffn(l):
                w = FF[l]
                up, down = a["ffn_w_in"][l], a["ffn_w_out"][l]

                def cols(src):
                    return src.rearrange("(k p) n -> p k n", p=P)

                eng.wait_ge(sm["tile_full"], TB[("wo", "co")[l]] + KT - 2)
                at = 0
                for f0, nf in PARTS:
                    if at == 0:
                        for j in range(4):
                            if j >= 2:
                                eng.wait_ge(w["w_lo"], j - 1)
                            f = (j // 2) * P + (j % 2) * F
                            load(ring[:, j % 2], cols(up[:, f:f + P]), fw_in[l][j % 2])
                    with eng.Fori(1 if at == 0 else 0, nf // 2) as i:
                        for j in range(4):
                            eng.wait_ge(w["w_lo"], i * 4 + (at + j - 1))
                            f = (f0 + j // 2) * P + (j % 2) * F
                            load(ring[:, j % 2], cols(up[:, bass.ds(i * (2 * P) + f, P)]), fw_in[l][j % 2])
                    at += 2 * nf
                    for n in range(KT):
                        eng.wait_ge(w["w_lo"], at + n - 1)
                        load(ring[:, n % 2, 0:nf], cols(down[f0 * P:(f0 + nf) * P, n * P:(n + 1) * P]), fw_in[l][n % 2])
                    at += KT

            ffn(0)
            eng.wait_ge(sm["tile_full"], TB["fo0"] + 2)
            load(grows, a["state_conv_glu"][0].rearrange("b w (k p) -> (b w k) p", p=P).rearrange("(g p) c -> p g c", p=P), sm["gst_in"])
            load_fst(frows, 1, sm["gst_in"])
            eng.wait_ge(FF[0]["w_lo"], NFFN)
            eng.wait_ge(FF[0]["hist_ready"], 2 * FT)
            weights("glu", a["conv_w_in"][0], [n // 2 + KT * (n % 2) for n in range(2 * KT)])

            def ffn_state(l):
                eng.wait_ge(sm["tile_read"], TB[f"fo{l}"] + 2)
                for g in range(7):
                    m = min(7, 2 * FT - 7 * g)
                    for q in range(m):
                        f = 7 * g + q
                        store(out["p_ffn"][l, 0, :, f * P:(f + 1) * P], ost[18 * q:18 * q + 2, g * P:(g + 1) * P])
                        store(out["s_ffn"][l, :, :, f * P:(f + 1) * P].rearrange("b w n -> (b w) n"), ost[18 * q + 2:18 * q + 18, g * P:(g + 1) * P])

            ffn_state(0)
            eng.wait_ge(sm["tile_read"], TB["go"] + 2)
            for kt in range(KT):
                store(out["p_glu"][0, 0, :, kt * P:(kt + 1) * P], ost[30 * (kt % 4):30 * (kt % 4) + 30, (kt // 4) * P:(kt // 4 + 1) * P])
                for b in range(DB):
                    r = 64 * (kt % 2) + DS * b
                    store(out["s_glu"][0, b, NSTATE - DS:NSTATE, kt * P:(kt + 1) * P],
                          ost[r:r + DS, 256 + (kt // 2) * P:256 + (kt // 2 + 1) * P])
            store(out["s_glu"][0, :, 0:NSTATE - DS, :], a["state_conv_glu"][0, :, DS:NSTATE, :])
            weights("co", a["conv_w_out"][0], range(KT))
            ffn(1)
            ffn_state(1)
            for q in range(2):
                half = slice(512 * q, 512 * q + 512)
                for g in range(5):
                    eng.wait_ge(sm["tile_read"], TB["yout"] + 5 * q + g + 1)
                    if g < 4:
                        store(out["y_prompt"][0, g * P:(g + 1) * P, half], xrows[:, g, half])
                    else:
                        store(out["y_sample"].rearrange("b t d -> (b t) d")[:, half], xrows[0:DEC, 4, half])
            eng.wait_ge(sm["out_done"], 16 * n_out[0])

        @block.tensor
        def _(pe):
            def begin(t):
                if t >= 4:
                    pe.wait_ge(sm["tile_read"], t - 3)

            def product(t, terms, m=P, mark=None):
                begin(t)
                for i, (lhs, rhs, pre) in enumerate(terms):
                    for w, v in pre:
                        pe.wait_ge(w, v)
                    st, sp = i == 0, i == len(terms) - 1
                    pe.matmul(ps[0:m, tset(t):tset(t) + SEQ], lhs, rhs[:, 0:SEQ], start=st, stop=sp)
                    ins = pe.matmul(ps[0:m, tset(t) + SEQ:tset(t) + T], lhs, rhs[:, SEQ:T], start=st, stop=sp)
                    if mark is not None and not sp:
                        ins.then_inc(mark, 1)
                ins.then_inc(sm["tile_full"], 1)

            def transposes(t, srcs):
                begin(t)
                for q, src in enumerate(srcs):
                    k = src.shape[0]
                    m = src.shape[1]
                    ins = pe.transpose(ps[0:m, tset(t) + P * q:tset(t) + P * q + k], src, ident[0:k, 0:k])
                ins.then_inc(sm["tile_full"], 1)

            def norm_sums(name, ones=C_MEAN, first=0):
                n = norm_i[0]
                product(TB[name] + first, [(con[:, ones:ones + P], tmp[:, kt % 2, :], [(sm["sq_ready"], KT * n + kt + 1)])
                                   for kt in range(KT)], mark=sm["sq_used"])
                norm_i[0] += 1

            norm_i = [0]

            def gemm(name, src, pre, first=0):
                for j in range(KT if name not in ("glu",) else 2 * KT):
                    w = WB[name] + j
                    terms = []
                    for kt in range(KT):
                        p = [(w_in[w % RING], 16 * (w // RING + 1))] if kt == 0 else []
                        if j == 0:
                            p.append((pre[0], pre[1] + kt + 1))
                        terms.append((ring[:, w % RING, kt, :], src[:, kt, :], p))
                    if name == "v":
                        if j == 3:
                            head_sums(TB["kks"], h, (sm["prep_sq"], 0))
                        if j == 5:
                            pe.wait_ge(sm["kn_ready"], 1)
                            pe.wait_ge(sm["sel_ready"], 1)
                            for k in range(KT):
                                product(TB["kk"] + k, [(sel[0][:, P * k:P * k + P], kn, [])])
                    product(WTILE[w], terms)

            def head_sums(t, src, pre):
                product(t, [(con[:, C_HSUM + 14 - 2 * k:C_HSUM + 14 - 2 * k + NH], src[:, k, :], [(pre[0], pre[1] + k + 1)])
                            for k in range(KT)], m=NH)

            def state_turns(name):
                for t in range(2):
                    transposes(TB[name] + t, [frows[0:min(P, NFS - P * g), g, :] for g in range(4 * t, min(4 * t + 4, NFG))])

            pe.wait_ge(sm["const_in"], 16)
            for g in range(5):
                pe.wait_ge(xt_in[g], 16)
                k = P if g < 4 else DEC
                for q in range(2):
                    transposes(TB["xin"] + 2 * g + q, [xrows[0:k, g, (4 * q + i) * P:(4 * q + i + 1) * P] for i in range(4)])
            norm_sums("n0")
            pe.wait_ge(sm["par_in"], 16 * n_par_dmas())
            for t in range(2):
                transposes(TB["par"] + t, [rows[0:min(P, NPC - P * g), g, :] for g in range(4 * t, min(4 * t + 4, NPG))])
            pe.wait_ge(sm["gath_ready"], 1)
            transposes(TB["shift"], [ost[:, 0:9 * KT]])
            pe.wait_ge(sm["lo1_in"], 48)
            for j, (src, o, m, q) in enumerate(((bufA, 0, LW, 0), (bufB, LW, LA, 1), (bufA, LW + LA, P, 2), (bufA, LW + LA + P, LG - P, 2))):
                product(TB["lo1"] + j, [(lo1[:, kt, o:o + m], src[:, kt, :], [(sm["xm_ready"], KT * q + kt + 1)] if j < 3 else [])
                                        for kt in range(KT)], m=m)
            pe.wait_ge(sm["lo2_in"], 32)
            pe.wait_ge(sm["tile_read"], TB["lo1"] + 2)
            for n in range(KT):
                for q in range(2):
                    product(TB["lo2"] + 2 * n + q, [(lo2[:, q, n * P:(n + 1) * P], hwa[:, q, :], [])])
            gemm("k", bufB, (sm["xm_ready"], 3 * KT))
            gemm("r", bufA, (sm["xm_ready"], 4 * KT))
            gemm("v", bufB, (sm["xm_ready"], 5 * KT))
            def pairs(g):
                return range(4 * g, 4 * g + 4)

            def mm(o, lhs, rhs, start=True, stop=True):
                return pe.matmul(o, lhs, rhs, start=start, stop=stop)

            def pbank(g, b, q, w, n=None):
                o = 2048 * g + 512 * b + w * q
                return ps[:, o:o + (n or w)]

            eye = con[:, C_IS:C_IS + 64]
            pe.wait_ge(sm["tile_read"], TB["pc"])
            ev = [0, 0]

            def step(g, ins):
                ins.then_inc(mm_done[g], 1)

            def turn(g):
                if ev[g]:
                    pe.wait_ge(ev_done[g], ev[g])
                ev[g] += 1

            def to_tokens(g, c):
                turn(g)
                pe.wait_ge(exp_ready[g], c + 1)
                if c:
                    pe.wait_ge(y_read[g], c)
                for i, k in enumerate(pairs(g)):
                    pe.transpose(pbank(g, 0, i, P), Vf[:, k, :], ident)
                    pe.transpose(pbank(g, 1, i, P), Bf[:, k, :], ident)
                    ins = pe.transpose(pbank(g, 2, i, P), Kf[:, k, :], ident)
                step(g, ins)

            def factors(g, c):
                turn(g)
                for i, k in enumerate(pairs(g)):
                    mm(pbank(g, 0, i, P), Bf[:, k, :], AR[:, c % 2, k, :])
                    mm(pbank(g, 1, i, P), Kf[:, k, :], AR[:, c % 2, k, :])
                    ins = mm(pbank(g, 2, i, P), Af[:, k, :], Bf[:, k, :])
                step(g, ins)

            def level(g, c, n, last, part):
                turn(g)
                if n == 1 and part == 0:
                    pe.wait_ge(mn_ready[g], c + 1)
                for i, k in enumerate(pairs(g)):
                    if part == 0:
                        ins = mm(pbank(g, 2 if n == 1 else 0, i, P), Mn[:, k, :], TT[:, k, :])
                    else:
                        ins = mm(pbank(g, 3, i, P), TI[:, k, :], Y[:, k, :])
                        if not last:
                            ins = mm(pbank(g, 2, i, P), Y[:, k, :], TI[:, k, :])
                step(g, ins)

            def inverse(c, levels):
                for n in range(1, levels):
                    for part in range(2):
                        for g in range(2):
                            level(g, c, n, n == levels - 1, part)

            def deltas(g):
                turn(g)
                for i, k in enumerate(pairs(g)):
                    ins = mm(pbank(g, 3, i, P), TT[:, k, :], Rm[:, k, :])
                step(g, ins)

            for c in range(NCH):
                for g in range(2):
                    to_tokens(g, c)
                for g in range(2):
                    factors(g, c)
                inverse(c, len(LEVELS))
                for g in range(2):
                    turn(g)
                    for i, k in enumerate(pairs(g)):
                        if c:
                            mm(pbank(g, 2, i, P), Af[:, k, :], S[g][:, i, :], stop=False)
                        ins = mm(pbank(g, 2, i, P), MkT[:, k, :], Vt[:, k, :], start=c == 0)
                    step(g, ins)
                for g in range(2):
                    deltas(g)
                for g in range(2):
                    turn(g)
                    for i, k in enumerate(pairs(g)):
                        mm(pbank(g, 0, i, P), Bt[:, k, :], SA[:, k, :], stop=False)
                        mm(pbank(g, 0, i, P), Ktk[:, k, :], Vt[:, k, :], start=False)
                        mm(pbank(g, 1, i, 64), SA[:, k, :], MbTr[:, k, :], stop=False)
                        ins = mm(pbank(g, 1, i, 64), Vt[:, k, :], MkTr[:, k, :], start=False, stop=c == 0)
                        if c:
                            ins = mm(pbank(g, 1, i, 64), S[g][:, i, :], AR[:, c % 2, k, 64:P], start=False)
                    step(g, ins)
            c = NCH
            for g in range(2):
                to_tokens(g, c)
            for g in range(2):
                factors(g, c)
            inverse(c, 3)
            pe.wait_ge(sm["sd_in"], 16 * 2 * DB)
            for k in range(KT):
                g, b = k % 2, 0
                pe.wait_ge(ev_done[g], ev[g])
                if k >= 2:
                    pe.wait_ge(sm["sd_ready"], k - 1)
                for q in range(DB // 2):
                    ins = pe.transpose(ps[:, 2048 * g + P * q:2048 * g + P * q + P], Snat[:, k, q, :], ident)
                ins.then_inc(sm["sd_turned"], 1)
            pe.wait_ge(sm["sd_ready"], KT)
            pe.wait_ge(sm["rf_ready"], 2)
            for i in range(4):
                for g in range(2):
                    turn(g)
                    k = 4 * g + i
                    mm(pbank(g, 0, 0, 512), Af[:, k, :], Sd[:, k, :])
                    mm(pbank(g, 1, 0, 512), Rf[:, k, :], Sd[:, k, :])
                    ins = mm(pbank(g, 2, 0, P), MkT[:, k, :], Vt[:, k, :])
                    step(g, ins)
            for g in range(2):
                deltas(g)
            pe.wait_ge(sm["rows_ready"], 2)
            for i in range(4):
                for g in range(2):
                    turn(g)
                    k = 4 * g + i
                    o = pbank(g, 1, 0, 64)
                    mm(o, SA[:, k, :], MbTr[:, k, :], stop=False)
                    mm(o, Vt[:, k, :], MkTr[:, k, :], start=False, stop=False)
                    mm(o, Yr[:, k, :], eye, start=False)
                    o = pbank(g, 0, 0, 512)
                    mm(o, Bt[:, k, :], tmp[:, 2 * g, 0:512], stop=False)
                    ins = mm(o, Ktk[:, k, :], tmp[:, 2 * g + 1, 0:512], start=False)
                    step(g, ins)
            for g in range(2):
                pe.wait_ge(ev_done[g], ev[g])
            for k in range(KT):
                ins = pe.transpose(ps[:, P * k:P * k + P], S[k // 4][:, k % 4, :], ident)
            ins.then_inc(sm["snat_ready"], 1)
            for k in range(KT):
                o = 1024 + 512 * (k % 6)
                if k >= 6:
                    pe.wait_ge(sm["state_out"], 1 + k - 5)
                for q in range(DB // 2):
                    ins = pe.transpose(ps[:, o + P * q:o + P * q + P], Sd[:, k, P * q:P * q + P], ident)
                ins.then_inc(sm["snat_ready"], 1)
            pe.wait_ge(sm["state_out"], 1 + KT)
            for kt in range(KT):
                product(TB["pc"] + kt, [(con[:, C_CEN:C_CEN + P], yg[:, kt, :], [])])
            head_sums(TB["pv"], sqh, (sm["tile_read"], TB["pc"]))
            head_sums(TB["pb"], rb, (sm["rk_ready"], 0))
            pe.wait_ge(sm["lg2_in"], 32)
            pe.wait_ge(sm["sel_ready"], 2)
            for kt in range(KT):
                t = TB["pz"] + 3 * kt
                product(t, [(lg2[:, 0, kt * P:(kt + 1) * P], hg[:, 0, :], []),
                            (lg2[0:LG - P, 1, kt * P:(kt + 1) * P], hg[0:LG - P, 1, :], [])])
                product(t + 1, [(sel[1][:, P * kt:P * kt + P], hsum[1], [(sm["tile_read"], TB["pb"] + 1)])])
                product(t + 2, [(sel[1][:, P * kt:P * kt + P], hsum[0], [(sm["rstd_ready"], 1)])])
            gemm("wo", yg, (sm["z_ready"], 0))
            norm_sums("n1")
            pe.wait_ge(sm["fst_in"], 32)
            state_turns("fst0")

            PASSES = ((0, 0), (0, 1), (1, 0))

            def parts(t, lhs, rhs, i, k):
                s = tset(t)
                for n, (u, v) in enumerate(PASSES):
                    for z in range(2):
                        ins = pe.matmul(ps[:, s + 512 * z:s + 512 * z + HALF], lhs(u, i), rhs[:, v, i, HALF * z:HALF * z + HALF],
                                        start=i == 0 and n == 0, stop=i == k - 1 and n == len(PASSES) - 1)
                return ins

            def split_product(t, lhs, rhs, k, pre=None):
                for i in range(k):
                    if pre is not None:
                        pe.wait_ge(pre[0], pre[1] + i + 1)
                    ins = parts(t, lhs, rhs, i, k)
                ins.then_inc(sm["tile_full"], 1)

            def weight(j):
                return lambda u, k: wsplit[:, j, u, k, :]

            def ffn(l):
                w = FF[l]
                t0 = TB[f"f{l}"]
                name = ("n2", "n6")[l]
                s, n0 = tset(TB[name]), KT * norm_i[0]
                norm_i[0] += 1
                begin(t0 + LOOK - 1)
                pe.wait_ge(w["w_lo"], LOOK)
                for kt in range(KT):
                    pe.wait_ge(sm["sq_ready"], n0 + kt + 1)
                    pe.matmul(ps[:, s:s + SEQ], con[:, C_MEAN:C_MEAN + P], tmp[:, kt % 2, 0:SEQ], start=kt == 0, stop=kt == KT - 1)
                    ins = pe.matmul(ps[:, s + SEQ:s + T], con[:, C_MEAN:C_MEAN + P], tmp[:, kt % 2, SEQ:T], start=kt == 0, stop=kt == KT - 1)
                    ins.then_inc(sm["sq_used"] if kt < KT - 1 else sm["tile_full"], 1)
                    pe.wait_ge(w["h_lo"], kt + 1)
                    for j in range(LOOK):
                        ins = parts(t0 + j, weight(j), hsplit, kt, KT)
                        if kt == KT - 1:
                            ins.then_inc(sm["tile_full"], 1)
                pe.wait_ge(w["w_lo"], LOOK + 1)
                begin(t0 + LOOK)
                split_product(t0 + LOOK, weight(LOOK), hsplit, KT)
                at = 0
                for f0, nf in PARTS:
                    with pe.Fori(0 if at else 1, nf // 2) as i:
                        for j in range(4):
                            pe.wait_ge(sm["tile_read"], i * 4 + (t0 + at + j - 3))
                            pe.wait_ge(w["w_lo"], i * 4 + (at + j + 1))
                            split_product(t0 + j, weight(j), hsplit, KT)
                    at += 2 * nf
                    for n in range(KT):
                        begin(t0 + at + n)
                        pe.wait_ge(w["w_lo"], at + n + 1)
                        split_product(t0 + at + n, weight(n % 4), hidsplit, nf, (w["hid_lo"], f0) if n == 0 else None)
                    at += KT
                pe.wait_ge(w["tails"], 4 * FT)
                for t in range(2):
                    transposes(TB[f"fo{l}"] + t, [fo[:, 7 * g:min(7 * g + 7, 2 * FT), :].rearrange("p f n -> p (f n)")
                                                  for g in range(4 * t, min(4 * t + 4, 7))])

            ffn(0)
            norm_sums("n3")
            pe.wait_ge(sm["gst_in"], 48)
            for t in range(4):
                transposes(TB["gst"] + t, [grows[:, g, :] for g in range(4 * t, min(4 * t + 4, NGG))])
            norm_sums("n4")
            gemm("glu", h, (sm["h_ready"], KT))
            job = 0
            for m, kt in enumerate(DW_PE):
                t = TB["dw"] + m
                begin(t)
                pe.wait_ge(sm["glu_ready"], kt + 1)
                for n in range(DW_TAPS[kt]):
                    pe.wait_ge(sm["diag_ready"], job + 1)
                    st, sp = n == 0, n == DW_TAPS[kt] - 1
                    pe.matmul(ps[:, tset(t):tset(t) + SEQ], diag[:, job, :], gb[:, kt, n:n + SEQ], start=st, stop=sp)
                    ins = pe.matmul(ps[:, tset(t) + SEQ:tset(t) + T].rearrange("p (b t) -> p b t", b=DB), diag[:, job, :],
                                    gd[:, kt, :, n:n + DS], start=st, stop=sp)
                    job += 1
                ins.then_inc(sm["tile_full"], 1)
            pe.wait_ge(sm["gath_ready"], 2)
            gathp = arena[:, A_H:A_H + 240]
            gaths = arena[:, A_H + 240:A_H + 752]
            transposes(TB["go"], [gathp[:, 0:120], gathp[:, 120:240]])
            transposes(TB["go"] + 1, [gaths[:, P * q:P * q + P] for q in range(4)])
            by = {kt: (sm["conv_done"], m + 1) for m, kt in enumerate(DW_DVE + DW_PE[:1])}
            by[DW_DVE[-1]] = by[DW_PE[0]]
            by[DW_PE[1]] = (sm["tile_read"], TB["dw"] + 2)
            by[DW_POOL] = (sm["conv_pool"], 1)
            product(TB["ln"], [(con[:, C_MEAN:C_MEAN + P], cvo[:, kt, :], [by[kt]]) for kt in (0, 2, 4, 6, 3, 1, 7, 5)])
            norm_sums("ln", first=1)
            gemm("co", cvo, (sm["z_ready"], KT))
            norm_sums("n5")
            state_turns("fst1")
            ffn(1)
            norm_sums("n7")
            for q in range(2):
                pe.wait_ge(sm["x_ready"], 3 * KT + 4 * (q + 1))
                for g in range(5):
                    k = P if g < 4 else DEC
                    transposes(TB["yout"] + 5 * q + g, [x[:, 4 * q + i, g * P:g * P + k] for i in range(4)])

        @block.scalar
        def _(act):
            def take(t):
                act.wait_ge(sm["tile_full"], t + 1)

            def freed(ins):
                ins.then_inc(sm["tile_read"], 1)

            f = nc.scalar.activation
            norm_i = [0]

            loads = [0]

            def tables(func):
                f(scrap[:, loads[0]:loads[0] + 1], con[:, C_EPS:C_EPS + 1], func)
                loads[0] += 1

            def norm(name, src, pre, eps=0, first=0, split=None):
                n = norm_i[0]
                for kt in range(KT):
                    if pre is not None:
                        act.wait_ge(pre[0], pre[1] + kt + 1)
                    if kt >= 2:
                        act.wait_ge(sm["sq_used"], (KT - 1) * n + kt - 1)
                    f(tmp[:, kt % 2, :], src[:, kt, :], ACT.Square).then_inc(sm["sq_ready"], 1)
                    if split is not None:
                        act.wait_ge(FF[split]["h32_ready"], kt + 1)
                        f(hsplit[:, 0, kt, :], h32[:, kt, :], ACT.Copy).then_inc(FF[split]["h_hi"], 1)
                t = TB[name] + first
                tables(ACT.Sqrt)
                take(t)
                freed(f(tmp[:, 2, :], bank2(t), ACT.Sqrt, bias=con[:, C_EPS + eps:C_EPS + eps + 1]))
                norm_i[0] += 1

            def state_cols(name):
                for t in range(2):
                    m = min(512, NFS - 512 * t)
                    take(TB[name] + t)
                    freed(f(fst[:, 512 * t:512 * t + m], bank2(TB[name] + t, m), ACT.Copy))

            for g in range(5):
                k = P if g < 4 else DEC
                for q in range(2):
                    t = TB["xin"] + 2 * g + q
                    take(t)
                    src = ps[:, tset(t):tset(t) + 512].rearrange("p (i n) -> p i n", n=P)[:, :, 0:k]
                    freed(f(x[:, 4 * q:4 * q + 4, g * P:g * P + k], src, ACT.Copy))
            act.wait_ge(sm["tile_read"], TB["xin"] + 10)
            norm("n0", x, None)
            for t in range(2):
                m = min(512, NPC - 512 * t)
                take(TB["par"] + t)
                freed(f(par[:, 512 * t:512 * t + m], bank2(TB["par"] + t, m), ACT.Copy))
            take(TB["shift"])
            freed(f(ost[0:9 * KT, 128:256], ps[0:9 * KT, tset(TB["shift"]):tset(TB["shift"]) + P], ACT.Copy))
            t = TB["lo1"]
            take(t)
            freed(f(hwa[:, 0, :], bank2(t, m=LW), ACT.Tanh))
            take(t + 1)
            freed(f(hwa[:, 1, :], bank2(t + 1, m=LA), ACT.Copy))
            take(t + 2)
            freed(f(hg[:, 0, :], bank2(t + 2), ACT.Sigmoid))
            take(t + 3)
            freed(f(hg[0:LG - P, 1, :], bank2(t + 3, m=LG - P), ACT.Sigmoid))
            for n in range(KT):
                for q, (dst, b) in enumerate(((sg, "rwkv_w0"), (ag, "rwkv_a0"))):
                    t = TB["lo2"] + 2 * n + q
                    take(t)
                    freed(f(dst[:, n, :], bank2(t), ACT.Sigmoid, bias=pcol(b, n)))
            for n in range(KT):
                take(TB["k"] + n)
                freed(f(kb[:, n, :], bank2(TB["k"] + n), ACT.Copy))

            def decays(kt):
                act.wait_ge(sm["prep_s"], kt + 1)
                f(h[:, kt, :], kkb[:, kt, :], ACT.Square).then_inc(sm["prep_sq"], 1)
                act.wait_ge(sm["wide_ready"], kt + 1)
                s = 2 * (kt % 2)
                f(tmp[:, s + 1, :], tmp[:, s, :], ACT.Exp, scale=-LAM).then_inc(sm["v_ready"], 1)
                f(sg[:, kt, :], sg[:, kt, :], ACT.Exp, scale=-LAM).then_inc(sm["v_ready"], 1)
                f(tmp[:, s, :], tmp[:, s, :], ACT.Exp, scale=LAM).then_inc(sm["v_ready"], 1)

            for n in range(KT):
                take(TB["r"] + n)
                freed(f(rb[:, n, :], bank2(TB["r"] + n), ACT.Copy))
                if n:
                    decays(n - 1)
            def blocks(dst, src, k, tok):
                for e in (0, 64):
                    ins = f(dst[e:e + 64, k, e:e + 64], src[e:e + 64, k, tok], ACT.Copy)
                return ins

            for n in range(KT):
                if n == KT - 1:
                    act.wait_ge(sm["unit_done"], KT)
                    act.wait_ge(sm["zeroed"], 3)
                    for g in range(2):
                        k = slice(4 * g, 4 * g + 4)
                        tok = slice(0, CH)
                        blocks(Bf, ag, k, tok)
                        blocks(Kf, kb, k, tok)
                        f(AR[:, 0, k, 0:64], kkb[:, k, tok], ACT.Copy)
                        f(AR[:, 0, k, 64:P], rb[:, k, tok], ACT.Copy)
                        blocks(Af, kkb, k, tok)
                if n == 3:
                    take(TB["kks"])
                    freed(f(kn, bank2(TB["kks"], m=NH), ACT.Sqrt))
                if n == 5:
                    for k in range(KT):
                        take(TB["kk"] + k)
                        if k + 2 == KT:
                            act.wait_ge(sm["prep_done"], KT)
                        freed(f(rinv[k], bank2(TB["kk"] + k), ACT.Copy))
                take(VTILES[n])
                freed(f(vb[:, n, :], bank2(VTILES[n]), ACT.Copy))
                if n == 0:
                    decays(KT - 1)
            mmn = [0, 0]

            def turn(g):
                mmn[g] += 1
                act.wait_ge(mm_done[g], mmn[g])

            def skip(n):
                for g in range(2):
                    mmn[g] += n

            def bk(g, b, n, w):
                o = 2048 * g + 512 * b
                return ps[:, o:o + n * w].rearrange("p (k n) -> p k n", n=w)

            act.wait_ge(sm["tile_read"], TB["pc"])
            act.wait_ge(sm["zeroed"], 4)
            for g in range(2):
                blocks(Vf, vb, slice(4 * g, 4 * g + 4), slice(0, CH)).then_inc(exp_ready[g], 1)
            for c in range(NCH + 1):
                nxt = slice(CH * (c + 1), CH * (c + 2))
                for g in range(2):
                    turn(g)
                    k = slice(4 * g, 4 * g + 4)
                    f(Vt[:, k, :], bk(g, 0, 4, P), ACT.Copy)
                    f(Bt[:, k, :], bk(g, 1, 4, P), ACT.Copy)
                    f(Ktk[:, k, :], bk(g, 2, 4, P), ACT.Copy).then_inc(ev_done[g], 1)
                for g in range(2):
                    turn(g)
                    k = slice(4 * g, 4 * g + 4)
                    f(Mn[:, k, :], bk(g, 2, 4, P), ACT.Copy).then_inc(mn_ready[g], 1)
                if c == NCH:
                    break
                for g in range(2):
                    k = slice(4 * g, 4 * g + 4)
                    blocks(Bf, ag, k, nxt)
                    blocks(Kf, kb, k, nxt)
                    f(AR[:, (c + 1) % 2, k, 0:64], kkb[:, k, nxt], ACT.Copy)
                    f(AR[:, (c + 1) % 2, k, 64:P], rb[:, k, nxt], ACT.Copy)
                skip(2 * (len(LEVELS) - 1))
                for g in range(2):
                    turn(g)
                    blocks(Af, kkb, slice(4 * g, 4 * g + 4), nxt)
                for g in range(2):
                    turn(g)
                    k = slice(4 * g, 4 * g + 4)
                    f(SA[:, k, :], bk(g, 3, 4, P), ACT.Copy).then_inc(ev_done[g], 1)
                    blocks(Vf, vb, k, nxt).then_inc(exp_ready[g], 1)
                for g in range(2):
                    turn(g)
                    k = slice(4 * g, 4 * g + 4)
                    f(yb[:, k, CH * c:CH * c + CH], bk(g, 1, 4, 64), ACT.Copy).then_inc(y_read[g], 1)
            for g in range(2):
                blocks(Rf, rb, slice(4 * g, 4 * g + 4), slice(SEQ, T)).then_inc(sm["rf_ready"], 1)
            skip(4)
            for k in range(KT):
                act.wait_ge(sm["sd_turned"], k + 1)
                g = k % 2
                f(Sd[:, k, :], ps[:, 2048 * g:2048 * g + 512], ACT.Copy).then_inc(sm["sd_ready"], 1)
            skip(4)
            for g in range(2):
                turn(g)
                f(SA[:, 4 * g:4 * g + 4, :], bk(g, 3, 4, P), ACT.Copy).then_inc(ev_done[g], 1)
            act.wait_ge(sm["snat_ready"], 1)
            so = ps[:, 0:1024].rearrange("p (k n) -> p k n", n=P)
            oo = ost[:, 256:768].rearrange("p (k n) -> p k n", n=64)
            for e in (0, 64):
                ins = f(oo[e:e + 64], so[e:e + 64, :, e:e + 64], ACT.Copy)
            ins.then_inc(sm["state_out"], 1)
            for k in range(KT):
                act.wait_ge(sm["snat_ready"], k + 2)
                o = 1024 + 512 * (k % 6)
                f(Snat[:, k], ps[:, o:o + 512].rearrange("p (b n) -> p b n", n=P), ACT.Copy).then_inc(sm["state_out"], 1)
            for kt in range(KT):
                t = TB["pc"] + kt
                take(t)
                f(yg[:, kt, :], bank2(t), ACT.Copy)
                freed(f(sqh[:, kt, :], bank2(t), ACT.Square))
            take(TB["pv"])
            freed(f(hsum[0], bank2(TB["pv"], m=NH), ACT.Sqrt, scale=1.0 / HS, bias=con[0:NH, C_EPS + 2:C_EPS + 3]))
            take(TB["pb"])
            freed(f(hsum[1], bank2(TB["pb"], m=NH), ACT.Copy))

            def outputs(name):
                for n in range(KT):
                    take(TB[name] + n)
                    freed(f(mb[:, n, :], bank2(TB[name] + n), ACT.Copy))

            def w_hi(l, at, i=None):
                act.wait_ge(fw_in[l][at % 2], 16 * (at // 2 + 1) + (0 if i is None else i * 32))
                if at >= 4 or i is not None:
                    act.wait_ge(sm["tile_full"], TB[f"f{l}"] + at - 3 + (0 if i is None else i * 4))
                f(wsplit[:, at % 4, 0], ring[:, at % 2], ACT.Copy).then_inc(FF[l]["w_hi"], 1)

            def ffn_first(l):
                act.wait_ge(sm["tile_full"], TB[("wo", "co")[l]] + KT)
                for at in range(LOOK):
                    w_hi(l, at)

            act.wait_ge(sm["tile_read"], TB["wo"])
            outputs("wo")
            norm("n1", mb, (sm["tile_read"], TB["wo"]))
            ffn_first(0)
            state_cols("fst0")
            norm("n2", x, (sm["x_ready"], 0), split=0)

            def ffn(l):
                w = FF[l]
                t0 = TB[f"f{l}"]
                at = 0
                for part, (f0, nf) in enumerate(PARTS):
                    with act.Fori(0, nf // 2) as i:
                        for q in range(2):
                            for z in range(2):
                                w_hi(l, at + 2 * q + z + LOOK, i)
                            act.wait_ge(w["conv_ready"], i * 4 + (2 * f0 + 2 * q + 1))
                            f(cv[:, 2 * q, :], cv[:, 2 * q, :], ACT.Silu).then_inc(w["gate_ready"], 1)
                            act.wait_ge(w["hid32_ready"], i * 2 + (f0 + q + 1))
                            f(hidsplit[:, 0, bass.ds(i * 2 + q, 1), :], cv[:, 2 * q:2 * q + 1, :], ACT.Copy).then_inc(w["hid_hi"], 1)
                    at += 2 * nf
                    for n in range(KT):
                        if at + n + LOOK < NFFN:
                            w_hi(l, at + n + LOOK)
                    at += KT
                act.wait_ge(sm["tile_read"], TB[f"fo{l}"])
                for t in range(2):
                    take(TB[f"fo{l}"] + t)
                    if l == 1 and t == 0:
                        act.wait_ge(sm["out_done"], 16 * (16 + 1 + NSOUT + 88 + KT * (1 + DB) + 1))
                    if l == 0 and t == 0:
                        act.wait_ge(sm["out_done"], 16 * (16 + 1 + NSOUT))
                    s = tset(TB[f"fo{l}"] + t)
                    if t == 0:
                        ins = f(ost[0:126, 0:512], ps[0:126, s:s + 512], ACT.Copy)
                    else:
                        f(ost[0:126, 512:768], ps[0:126, s:s + 256], ACT.Copy)
                        ins = f(ost[0:36, 768:896], ps[0:36, s + 256:s + 384], ACT.Copy)
                    freed(ins)

            ffn(0)
            norm("n3", mb, (sm["tile_read"], TB["f0"] + NFFN - KT))
            for t in range(4):
                m = min(512, NGS - 512 * t)
                take(TB["gst"] + t)
                freed(f(gst[:, 512 * t:512 * t + m], bank2(TB["gst"] + t, m), ACT.Copy))
            norm("n4", x, (sm["x_ready"], KT))

            per = -(-len(DW_JOBS) // KT)
            for n in range(KT):
                for job in range(per * n, min(per * n + per, len(DW_JOBS))):
                    kt, tap = DW_JOBS[job]
                    f(diag[:, job, :], ident, ACT.Copy, scale=pcol("conv_dw_w", tap * KT + kt)).then_inc(sm["diag_ready"], 1)
                ta, tb = TB["glu"] + 2 * n, TB["glu"] + 2 * n + 1
                if n >= 1:
                    act.wait_ge(sm["glu_ready"], n)
                take(ta)
                freed(f(gsig[:, 1, :], bank2(ta), ACT.Identity, bias=pcol("conv_b_in", n)))
                take(tb)
                freed(f(gsig[:, 0, :], bank2(tb), ACT.Sigmoid, bias=pcol("conv_b_in", KT + n)))
            for m, kt in enumerate(DW_PE):
                take(TB["dw"] + m)
                freed(f(cvo[:, kt, :], bank2(TB["dw"] + m), ACT.Identity, bias=pcol("conv_dw_b", kt)))
            take(TB["go"])
            act.wait_ge(sm["out_done"], 16 * (16 + 1 + NSOUT + 88))
            s = tset(TB["go"])
            freed(f(ost[0:120, 0:256], ps[0:120, s:s + 256], ACT.Copy))
            take(TB["go"] + 1)
            freed(f(ost[:, 256:768], bank2(TB["go"] + 1, 512), ACT.Copy))
            take(TB["ln"])
            freed(f(tmp[:, 3, :], bank2(TB["ln"]), ACT.Copy))
            norm("ln", cvo, (sm["ln_v"], 0), eps=1, first=1)
            tables(ACT.Silu)
            for kt in range(KT):
                act.wait_ge(sm["ln_v"], KT + kt + 1)
                f(cvo[:, kt, :], cvo[:, kt, :], ACT.Silu, scale=pcol("conv_ln_w", kt), bias=pcol("conv_ln_b", kt)).then_inc(sm["z_ready"], 1)
            for n in range(KT):
                take(TB["co"] + n)
                freed(f(mb[:, n, :], bank2(TB["co"] + n), ACT.Identity, bias=pcol("conv_b_out", n)))
            norm("n5", mb, (sm["tile_read"], TB["co"]))
            ffn_first(1)
            state_cols("fst1")
            norm("n6", x, (sm["x_ready"], 2 * KT), split=1)
            ffn(1)
            norm("n7", mb, (sm["tile_read"], TB["f1"] + NFFN - KT))
            for q in range(2):
                for g in range(5):
                    k = P if g < 4 else DEC
                    t = TB["yout"] + 5 * q + g
                    take(t)
                    freed(f(xrows[0:k, g, 512 * q:512 * q + 512], ps[0:k, tset(t):tset(t) + 512], ACT.Copy))

        @block.vector
        def _(dve):
            done = [0]
            v = nc.vector

            def seq(ins):
                ins.then_inc(sm["vec_done"], 1)
                done[0] += 1

            def after():
                if done[0]:
                    dve.wait_ge(sm["vec_done"], done[0])

            def norm_scale(name, first=0):
                dve.wait_ge(sm["tile_read"], TB[name] + first + 1)
                seq(v.reciprocal(tmp[:, 2, :], tmp[:, 2, :]))
                after()

            def prenorm(name, n, ready=None):
                norm_scale(name)
                if ready:
                    dve.wait_ge(sm["tile_read"], ready)
                for kt in range(KT):
                    v.scalar_tensor_tensor(h[:, kt, :], x[:, kt, :], gain(n, kt), tmp[:, 2, :], ALU.mult, ALU.mult)\
                        .then_inc(sm["h_ready"], 1)

            xs = [0]

            def postnorm(name, n, split=None):
                norm_scale(name)
                scaled = []
                for i in range(KT + 3):
                    if i < KT:
                        seq(v.scalar_tensor_tensor(mb[:, i, :], mb[:, i, :], gain(n, i), tmp[:, 2, :], ALU.mult, ALU.mult))
                        scaled.append(done[0])
                    if 1 <= i <= KT:
                        dve.wait_ge(sm["vec_done"], scaled[i - 1])
                        v.tensor_tensor(x[:, i - 1, :], x[:, i - 1, :], mb[:, i - 1, :], ALU.add).then_inc(sm["x_ready"], 1)
                    if split is not None and 2 <= i <= KT + 1:
                        w = FF[split[1]]
                        dve.wait_ge(sm["x_ready"], xs[0] + i - 1)
                        v.tensor_scalar(h32[:, i - 2, :], x[:, i - 2, :], gain(split[0], i - 2), None, ALU.mult).then_inc(w["h32_ready"], 1)
                    if split is not None and 3 <= i:
                        dve.wait_ge(w["h_hi"], i - 2)
                        v.tensor_tensor(hsplit[:, 1, i - 3, :], h32[:, i - 3, :], hsplit[:, 0, i - 3, :].bitcast(F32), ALU.subtract)\
                            .then_inc(w["h_lo"], 1)
                xs[0] += KT
                if split is not None:
                    norm_scale(("n2", "n6")[split[1]])

            dve.wait_ge(sm["const_in"], 16)
            prenorm("n0", 0, TB["par"] + 2)
            dve.wait_ge(sm["h_ready"], KT)
            hd = h[:, :, SEQ:T].rearrange("p k (b t) -> p k b t", b=DB)
            xd = xx[:, :, SEQ:T].rearrange("p k (b t) -> p k b t", b=DB)
            go = ost[:, 0:9 * KT].rearrange("p (k c) -> p k c", c=9)
            seq(v.tensor_copy(go[:, :, 0:1], h[:, :, SEQ - 1:SEQ]))
            v.tensor_copy(go[:, :, 1:9], hd[:, :, :, DS - 1]).then_inc(sm["gath_ready"], 1)
            shift = par[:, PCOL["state_rwkv_shift"]:PCOL["state_rwkv_shift"] + DB * KT].rearrange("p (b k) -> p k b", b=DB)
            seq(v.tensor_tensor(xx[:, :, 1:SEQ], h[:, :, 0:SEQ - 1], h[:, :, 1:SEQ], ALU.subtract))
            seq(v.tensor_scalar(xx[:, :, 0:1], h[:, :, 0:1], -1.0, None, ALU.mult))
            for kt in range(KT):
                seq(v.tensor_tensor(xd[:, kt, :, 1:DS], hd[:, kt, :, 0:DS - 1], hd[:, kt, :, 1:DS], ALU.subtract))
            seq(v.tensor_tensor(xd[:, :, :, 0], shift, hd[:, :, :, 0], ALU.subtract))
            seq(v.tensor_scalar(omka[:], par[:, PCOL["rwkv_k_a"]:PCOL["rwkv_k_a"] + KT], -1.0, 1.0, ALU.mult, ALU.add))
            after()
            free = {2: TB["lo1"] + 1, 3: TB["lo1"] + 2, 4: TB["lo1"] + 4, 5: TB["k"] + KT}
            for q, m in enumerate((1, 4, 5, 2, 0, 3)):
                if q in free:
                    dve.wait_ge(sm["tile_full"], free[q])
                for kt in range(KT):
                    v.scalar_tensor_tensor((bufA, bufB)[q % 2][:, kt, :], xx[:, kt, :], pcol("rwkv_mix", m * KT + kt),
                                           h[:, kt, :], ALU.mult, ALU.add).then_inc(sm["xm_ready"], 1)
            dve.wait_ge(sm["xm_ready"], 6 * KT)
            dve.wait_ge(sm["tile_read"], TB["k"] + KT)

            def sums(kt):
                t = tmp[:, 2 * (kt % 2), :]
                u = tmp[:, 2 * (kt % 2) + 1, :]
                after()
                if kt >= 2:
                    dve.wait_ge(sm["prep_done"], kt - 1)
                v.tensor_scalar(kkb[:, kt, :], kb[:, kt, :], pcol("rwkv_k_k", kt), None, ALU.mult).then_inc(sm["prep_s"], 1)
                dve.wait_ge(sm["prep_s"], kt + 1)
                seq(v.tensor_scalar(u, ag[:, kt, :], pcol("rwkv_k_a", kt), omka[:, kt:kt + 1], ALU.mult, ALU.add))
                seq(v.tensor_tensor_scan(t, con[:, C_SCAN:C_SCAN + T], sg[:, kt, :], 0.0, ALU.mult, ALU.add))
                after()
                seq(v.tensor_tensor(kb[:, kt, :], kb[:, kt, :], u, ALU.mult))
                seq(v.scalar_tensor_tensor(ag[:, kt, :], kkb[:, kt, :], -1.0, ag[:, kt, :], ALU.mult, ALU.mult))
                after()
                v.tensor_tensor(sg[:, kt, :], t, sg[:, kt, :], ALU.subtract).then_inc(sm["wide_ready"], 1)

            def scale(kt):
                t, u = tmp[:, 2 * (kt % 2), :], tmp[:, 2 * (kt % 2) + 1, :]
                dve.wait_ge(sm["v_ready"], 3 * kt + 3)
                dve.wait_ge(sm["tile_read"], TB["r"] + kt + 1)
                seq(v.tensor_tensor(kkb[:, kt, :], kkb[:, kt, :], sg[:, kt, :], ALU.mult))
                seq(v.tensor_tensor(rb[:, kt, :], rb[:, kt, :], u, ALU.mult))
                seq(v.tensor_tensor(kb[:, kt, :], kb[:, kt, :], t, ALU.mult))
                seq(v.tensor_tensor(ag[:, kt, :], ag[:, kt, :], t, ALU.mult))
                seq(v.tensor_copy(pend[:, kt, 0:NCH], u[:, CH - 1:SEQ:CH]))
                after()
                v.tensor_copy(pend[:, kt, NCH:NCH + DB], u[:, SEQ + DS - 1:T:DS]).then_inc(sm["prep_done"], 1)

            sums(0)
            for kt in range(KT):
                if kt + 1 < KT:
                    sums(kt + 1)
                scale(kt)
            def selector(n):
                src = ident[0:NH, 0:NH].unsqueeze(2).to_broadcast([NH, NH, HS])
                v.tensor_copy(sel[n].rearrange("p (r c) -> p r c", c=HS), src).then_inc(sm["sel_ready"], 1)

            dve.wait_ge(sm["tile_read"], TB["kks"] + 1)
            selector(0)
            seq(v.tensor_scalar(kn, kn, 1e-12, None, ALU.max))
            after()
            v.reciprocal(kn, kn).then_inc(sm["kn_ready"], 1)
            dve.wait_ge(sm["prep_done"], KT)
            for kt in range(KT):
                dve.wait_ge(sm["tile_read"], TB["kk"] + kt + 1)
                seq(v.tensor_tensor(kkb[:, kt, :], kkb[:, kt, :], rinv[kt], ALU.mult))
                v.tensor_tensor(ag[:, kt, :], ag[:, kt, :], rinv[kt], ALU.mult).then_inc(sm["unit_done"], 1)
            dve.wait_ge(sm["unit_done"], KT)
            after()
            for buf in (Bf, Kf, Af, Vf):
                if buf is Vf:
                    dve.wait_ge(sm["tile_full"], VTILES[-1] + 1)
                v.memset(buf, 0.0).then_inc(sm["zeroed"], 1)
            mmn = [0, 0]

            def bk(g, b, n, w):
                o = 2048 * g + 512 * b
                return ps[:, o:o + n * w].rearrange("p (k n) -> p k n", n=w)

            def turn(g):
                mmn[g] += 1
                dve.wait_ge(mm_done[g], mmn[g])

            def skip(n):
                for g in range(2):
                    mmn[g] += n

            def fin(g, ins):
                ins.then_inc(ev_done[g], 1)

            def heads(ap):
                return ap.rearrange("p k (e n) -> p k e n", e=2)

            def mask2(col):
                return con[:, col:col + 64].unsqueeze(1).unsqueeze(1).to_broadcast([P, 4, 2, 64])

            def maskbd(n):
                m = con[:, C_BD + P * n:C_BD + P * n + P].rearrange("p (e n) -> p e n", e=2)
                return m.unsqueeze(1).to_broadcast([P, 4, 2, 64])

            def twice(ap):
                return ap.unsqueeze(2).to_broadcast([P, 4, 2, 64])

            ident4 = ident.unsqueeze(1).to_broadcast([P, 4, P])

            def factors(g, c):
                turn(g)
                k = slice(4 * g, 4 * g + 4)
                seq(v.tensor_tensor(heads(TT[:, k, :]), twice(bk(g, 0, 4, P)[:, :, 0:64]), maskbd(2), ALU.mult))
                after()
                fin(g, v.tensor_tensor(TT[:, k, :], TT[:, k, :], ident4, ALU.add))

            def start_ti(g, c):
                k = slice(4 * g, 4 * g + 4)
                dve.wait_ge(mn_ready[g], c + 1)
                seq(v.tensor_tensor(heads(TI[:, k, :]), heads(Mn[:, k, :]), mask2(C_LOW1), ALU.mult))
                after()
                seq(v.tensor_tensor(TI[:, k, :], TI[:, k, :], ident4, ALU.add))

            def lower(g, n, last, mask, bd):
                k = slice(4 * g, 4 * g + 4)
                m = con[:, mask:mask + 64].unsqueeze(1).to_broadcast([P, 4, 64])
                if n == 1:
                    seq(v.tensor_tensor(MbTr[:, k, :], bk(g, 0, 4, P)[:, :, 64:P], m, ALU.mult))
                if n == 2:
                    seq(v.tensor_tensor(MkTr[:, k, :], bk(g, 1, 4, P)[:, :, 64:P], m, ALU.mult))
                if n == 3 or last and n < 3:
                    seq(v.tensor_tensor(heads(MkT[:, k, :]), twice(bk(g, 1, 4, P)[:, :, 0:64]), maskbd(bd), ALU.mult))

            def level(g, n, last, part):
                turn(g)
                k = slice(4 * g, 4 * g + 4)
                after()
                if part == 0:
                    fin(g, v.tensor_tensor(heads(Y[:, k, :]), heads(bk(g, 2 if n == 1 else 0, 4, P)), mask2(C_LVL + 64 * (n - 1)), ALU.mult))
                else:
                    fin(g, v.tensor_tensor(TT[:, k, :], TT[:, k, :], bk(g, 3, 4, P), ALU.add))

            def add_ti(g):
                k = slice(4 * g, 4 * g + 4)
                seq(v.tensor_tensor(TI[:, k, :], TI[:, k, :], bk(g, 2, 4, P), ALU.add))

            def inverse(levels, mask, bd, c):
                for n in range(1, levels):
                    last = n == levels - 1
                    for part in range(2):
                        for g in range(2):
                            if part == 0 and n == 1:
                                start_ti(g, c)
                            if part == 0 and n > 1 and g == 1:
                                add_ti(1)
                            level(g, n, last, part)
                            if part == 0:
                                lower(g, n, last, mask, bd)
                            if part == 1 and g == 0 and not last:
                                add_ti(0)

            for c in range(NCH):
                skip(1)
                for g in range(2):
                    factors(g, c)
                inverse(len(LEVELS), C_MASK, 0, c)
                for g in range(2):
                    turn(g)
                    after()
                    fin(g, v.tensor_copy(Rm[:, 4 * g:4 * g + 4, :], bk(g, 2, 4, P)))
                skip(1)
                for g in range(2):
                    turn(g)
                    pe4 = pend[:, 4 * g:4 * g + 4, c:c + 1].to_broadcast([P, 4, P])
                    if c:
                        seq(v.tensor_tensor(S[g], S[g], bk(g, 0, 4, P), ALU.add))
                        after()
                        fin(g, v.tensor_tensor(S[g], S[g], pe4, ALU.mult))
                    else:
                        fin(g, v.tensor_tensor(S[g], bk(g, 0, 4, P), pe4, ALU.mult))
            skip(1)
            for g in range(2):
                factors(g, NCH)
            inverse(3, C_MASKD, 1, NCH)
            own = con[:, C_B8:C_B8 + 8].unsqueeze(2).to_broadcast([P, DB, 64])

            def masked_rows(g, i):
                for m, src in enumerate((SA, Vt)):
                    o = tmp[:, 2 * g + m, 0:512].rearrange("p (b n) -> p b n", b=DB)
                    for e in (0, 64):
                        seq(v.tensor_tensor(o[e:e + 64], src[e:e + 64, 4 * g + i, e:e + 64].unsqueeze(1).to_broadcast([64, DB, 64]),
                                            own[e:e + 64], ALU.mult))
                after()

            for i in range(4):
                for g in range(2):
                    turn(g)
                    k = 4 * g + i
                    after()
                    for m in range(2):
                        o = tmp[:, 2 * g + m, 0:512].rearrange("p (b n) -> p b n", b=DB)
                        seq(v.tensor_tensor(o, bk(g, m, DB, 64), own, ALU.mult))
                    seq(v.tensor_copy(Rm[:, k, :], bk(g, 2, 1, P)[:, 0, :]))
                    after()
                    for m in range(2):
                        o = tmp[:, 2 * g + m, 0:512].rearrange("p (b n) -> p n b", b=DB)
                        seq(v.tensor_reduce(tmp[:, 2 * g + m, 512:576], o, mybir.AxisListType.X, ALU.add))
                    after()
                    for e in (0, 64):
                        seq(v.tensor_copy(Yr[e:e + 64, k, e:e + 64], tmp[e:e + 64, 2 * g + 1, 512:576]))
                        ins = v.tensor_tensor(Rm[e:e + 64, k, e:e + 64], Rm[e:e + 64, k, e:e + 64], tmp[e:e + 64, 2 * g, 512:576], ALU.add)
                        if e:
                            after()
                            fin(g, ins)
                        else:
                            seq(ins)
            skip(1)
            for g in range(2):
                dve.wait_ge(ev_done[g], mmn[g])
                masked_rows(g, 0)
                v.tensor_copy(omka[:, g:g + 1], omka[:, g:g + 1]).then_inc(sm["rows_ready"], 1)
            for i in range(4):
                for g in range(2):
                    k = 4 * g + i
                    turn(g)
                    seq(v.tensor_copy(yb[:, k, SEQ:T], bk(g, 1, 1, 64)[:, 0, :]))
                    if i < 3:
                        masked_rows(g, i + 1)
                    o = Sd[:, k, :].rearrange("p (b n) -> p b n", b=DB)
                    seq(v.tensor_tensor(o, o, bk(g, 0, DB, 64), ALU.add))
                    after()
                    fin(g, v.tensor_tensor(o, o, pend[:, k, NCH:NCH + DB].unsqueeze(2).to_broadcast([P, DB, 64]), ALU.mult))
            for kt in range(KT):
                v.scalar_tensor_tensor(rb[:, kt, :], rb[:, kt, :], pcol("rwkv_r_k", kt), kb[:, kt, :], ALU.mult, ALU.mult)\
                    .then_inc(sm["rk_ready"], 1)
            dve.wait_ge(sm["snat_ready"], 1)
            selector(1)
            dve.wait_ge(sm["tile_read"], TB["pv"] + 1)
            after()
            v.reciprocal(hsum[0], hsum[0]).then_inc(sm["rstd_ready"], 1)
            dve.wait_ge(sm["tile_read"], TB["pz"])
            for kt in range(KT):
                t = TB["pz"] + 3 * kt
                g, b = tmp[:, 2 * (kt % 2), :], tmp[:, 2 * (kt % 2) + 1, :]
                if kt >= 2:
                    dve.wait_ge(sm["z_ready"], kt - 1)
                dve.wait_ge(sm["tile_full"], t + 1)
                v.tensor_copy(g, bank2(t)).then_inc(sm["tile_read"], 1)
                dve.wait_ge(sm["tile_full"], t + 2)
                v.tensor_tensor(b, vb[:, kt, :], bank2(t + 1), ALU.mult).then_inc(sm["tile_read"], 1)
                dve.wait_ge(sm["tile_full"], t + 3)
                v.scalar_tensor_tensor(yg[:, kt, :], yg[:, kt, :], pcol("rwkv_lnx_w", kt), bank2(t + 2), ALU.mult, ALU.mult)\
                    .then_inc(sm["tile_read"], 1)
                dve.wait_ge(sm["tile_read"], t + 3)
                seq(v.scalar_tensor_tensor(yg[:, kt, :], yg[:, kt, :], pcol("rwkv_lnx_b", kt), b, ALU.add, ALU.add))
                after()
                v.tensor_tensor(yg[:, kt, :], yg[:, kt, :], g, ALU.mult).then_inc(sm["z_ready"], 1)
            postnorm("n1", 1, (2, 0))

            def ffn(l):
                w = FF[l]
                chain = w["cvd"]
                per = 4 * 5
                for z in range(4):
                    v.memset(raw[:, z, 0:2], 0.0).then_inc(w["no_hist"], 1)
                t0 = TB[f"f{l}"]
                at = 0
                for part, (f0, nf) in enumerate(PARTS):
                    with dve.Fori(0, nf // 2) as i:
                        for q in range(2):
                            for z in range(2):
                                j = 2 * q + z
                                dve.wait_ge(sm["tile_full"], i * 4 + (t0 + at + j + 1))
                                dve.wait_ge(w["hist_ready"], i * 4 + (2 * f0 + j + 1))
                                s = tset(t0 + j)
                                v.tensor_tensor(raw[:, j, 2:2 + HALF], ps[:, s:s + HALF], tmp[:, 2, 0:HALF], ALU.mult)
                                v.tensor_tensor(raw[:, j, 2 + HALF:2 + SEQ], ps[:, s + 512:s + 512 + SEQ - HALF], tmp[:, 2, HALF:SEQ], ALU.mult)
                                v.tensor_tensor(raw[:, j, 2 + SEQ:RAW].rearrange("p (b t) -> p b t", b=DB)[:, :, 2:2 + DS],
                                                ps[:, s + 512 + SEQ - HALF:s + 512 + HALF].rearrange("p (b t) -> p b t", b=DB),
                                                tmp[:, 2, SEQ:T].rearrange("p (b t) -> p b t", b=DB), ALU.mult)\
                                    .then_inc(sm["tile_read"], 1)
                                dve.wait_ge(sm["tile_read"], i * 4 + (t0 + at + j + 1))
                                rp = raw[:, j, 0:2 + SEQ]
                                rd = raw[:, j, 2 + SEQ:RAW].rearrange("p (b t) -> p b t", b=DB)
                                cd = cv[:, j, SEQ:T].rearrange("p (b t) -> p b t", b=DB)

                                def tap(n):
                                    o = PCOL["ffn_dw_w"] + (3 * l + n) * 2 * FT + z * FT + f0 + q
                                    return par[:, bass.ds(i * 2 + o, 1)]

                                bias = par[:, bass.ds(i * 2 + (PCOL["ffn_dw_b"] + l * 2 * FT + z * FT + f0 + q), 1)]
                                v.tensor_scalar(cv[:, j, 0:SEQ], rp[:, 0:SEQ], tap(0), bias, ALU.mult, ALU.add).then_inc(chain, 1)
                                v.tensor_scalar(cd, rd[:, :, 0:DS], tap(0), bias, ALU.mult, ALU.add).then_inc(chain, 1)
                                for n in (1, 2):
                                    dve.wait_ge(chain, i * per + (f0 // 2 * per + 5 * j + 2 * n))
                                    v.scalar_tensor_tensor(cv[:, j, 0:SEQ], rp[:, n:n + SEQ], tap(n), cv[:, j, 0:SEQ], ALU.mult, ALU.add).then_inc(chain, 1)
                                    ins = v.scalar_tensor_tensor(cd, rd[:, :, n:n + DS], tap(n), cd, ALU.mult, ALU.add)
                                    ins.then_inc(chain if n == 1 else w["conv_ready"], 1)
                            dve.wait_ge(w["gate_ready"], i * 2 + (f0 + q + 1))
                            dve.wait_ge(w["conv_ready"], i * 4 + (2 * f0 + 2 * q + 2))
                            dve.wait_ge(chain, i * per + (f0 // 2 * per + 10 * q + 10))
                            v.tensor_tensor(cv[:, 2 * q, :], cv[:, 2 * q, :], cv[:, 2 * q + 1, :], ALU.mult)\
                                .then_inc(w["hid32_ready"], 1)
                            dve.wait_ge(w["hid_hi"], i * 2 + (f0 + q + 1))
                            v.tensor_tensor(hidsplit[:, 1, bass.ds(i * 2 + q, 1), :], cv[:, 2 * q:2 * q + 1, :],
                                            hidsplit[:, 0, bass.ds(i * 2 + q, 1), :].bitcast(F32), ALU.subtract)\
                                .then_inc(w["hid_lo"], 1)
                    at += 2 * nf
                    for n in range(KT):
                        t = t0 + at + n
                        dve.wait_ge(sm["tile_full"], t + 1)
                        o = mb[:, n, :].rearrange("p (z n) -> p z n", z=2)
                        b = ps[:, tset(t):tset(t) + 1024].rearrange("p (z n) -> p z n", z=2)[:, :, 0:HALF]
                        if part:
                            ins = v.tensor_tensor(o, o, b, ALU.add)
                        else:
                            ins = v.tensor_copy(o, b)
                        ins.then_inc(sm["tile_read"], 1)
                    at += KT

            ffn(0)
            postnorm("n3", 3)
            dve.wait_ge(sm["x_ready"], 2 * KT)
            prenorm("n4", 4)
            dve.wait_ge(sm["tile_read"], TB["gst"] + 4)
            seq(v.memset(gb[:, :, 0:NSTATE], 0.0))
            gs = gst.rearrange("p (b w k) -> p k b w", b=DB, k=KT)
            for kt in range(KT):
                seq(v.tensor_copy(gd[:, kt, :, 0:NSTATE], gs[:, kt]))

            def glu(kt):
                dve.wait_ge(sm["tile_read"], TB["glu"] + 2 * kt + 2)
                seq(v.tensor_tensor(gb[:, kt, NSTATE:NSTATE + SEQ], gsig[:, 1, 0:SEQ], gsig[:, 0, 0:SEQ], ALU.mult))
                after()
                v.tensor_tensor(gd[:, kt, :, NSTATE:NSTATE + DS], gsig[:, 1, SEQ:T].rearrange("p (b t) -> p b t", b=DB),
                                gsig[:, 0, SEQ:T].rearrange("p (b t) -> p b t", b=DB), ALU.mult).then_inc(sm["glu_ready"], 1)

            def newest():
                dve.wait_ge(sm["tile_full"], TB["glu"] + 2 * KT)
                dve.wait_ge(sm["glu_ready"], KT)
                gp = arena[:, A_H:A_H + 240].rearrange("p (k w) -> p k w", w=NSTATE)
                gt = arena[:, A_H + 240:A_H + 752].rearrange("p (k b t) -> p k b t", k=KT, b=DB)
                seq(v.tensor_copy(gp, gb[:, :, SEQ:SEQ + NSTATE]))
                for kt in range(KT):
                    ins = v.tensor_copy(gt[:, kt], gd[:, kt, :, NSTATE:NSTATE + DS])
                    if kt < KT - 1:
                        seq(ins)
                ins.then_inc(sm["gath_ready"], 1)

            turned, done_glu, step, waiting, active, last = False, 0, 0, [(kt, 0) for kt in DW_DVE] + [(DW_PE[0], DW_TAPS[DW_PE[0]])], [], {}
            while waiting or active:
                if not active or (step % GLU_EVERY == 0 and done_glu < KT):
                    glu(done_glu)
                    done_glu += 1
                while len(active) < 2 and waiting and waiting[0][0] < done_glu:
                    kt, n = waiting.pop(0)
                    dve.wait_ge(sm["glu_ready"], kt + 1)
                    if n:
                        dve.wait_ge(sm["tile_read"], TB["dw"] + 1)
                    active.append([kt, n])
                if not active:
                    continue
                if not waiting and not turned:
                    newest()
                    turned = True
                step += 1
                kt, n = active.pop(0)
                cd = cvo[:, kt, SEQ:T].rearrange("p (b t) -> p b t", b=DB)
                w = pcol("conv_dw_w", n * KT + kt)
                for part, dst, src in ((0, cvo[:, kt, 0:SEQ], gb[:, kt, n:n + SEQ]), (1, cd, gd[:, kt, :, n:n + DS])):
                    if (kt, part) in last:
                        dve.wait_ge(sm["vec_done"], last[kt, part])
                    if n:
                        ins = v.scalar_tensor_tensor(dst, src, w, dst, ALU.mult, ALU.add)
                    else:
                        ins = v.tensor_scalar(dst, src, w, pcol("conv_dw_b", kt), ALU.mult, ALU.add)
                    if n == CW - 1 and part:
                        ins.then_inc(sm["conv_done"], 1)
                    else:
                        seq(ins)
                        last[kt, part] = done[0]
                if n < CW - 1:
                    active.append([kt, n + 1])
            dve.wait_ge(sm["tile_read"], TB["ln"] + 1)
            dve.wait_ge(sm["conv_done"], len(DW_DVE) + 1)
            dve.wait_ge(sm["conv_pool"], 1)
            after()
            for kt in range(KT):
                v.tensor_tensor(cvo[:, kt, :], cvo[:, kt, :], tmp[:, 3, :], ALU.subtract).then_inc(sm["ln_v"], 1)
            norm_scale("ln", 1)
            dve.wait_ge(sm["ln_v"], KT)
            for kt in range(KT):
                v.tensor_tensor(cvo[:, kt, :], cvo[:, kt, :], tmp[:, 2, :], ALU.mult).then_inc(sm["ln_v"], 1)
            postnorm("n5", 5, (6, 1))
            ffn(1)
            postnorm("n7", 7)

        @block.gpsimd
        def _(pool):
            p = nc.gpsimd
            def ffn(l):
                w = FF[l]
                st = fst[:].rearrange("p (b w f) -> p b w f", b=DB, w=2)

                def decode(j):
                    return raw[:, j, 2 + SEQ:RAW].rearrange("p (b t) -> p b t", b=DB)

                def w_lo(at, i=None):
                    pool.wait_ge(w["w_hi"], at + 1 + (0 if i is None else i * 4))
                    p.tensor_tensor(wsplit[:, at % 4, 1], ring[:, at % 2], wsplit[:, at % 4, 0].bitcast(F32), ALU.subtract)\
                        .then_inc(w["w_lo"], 1)

                def tails(i, j):
                    pool.wait_ge(sm["tile_read"], i * 4 + (t0 + at + j + 1))
                    f = (j % 2) * FT + j // 2 + f0
                    o = fo[:, bass.ds(i * 2 + f, 1), :]
                    p.tensor_copy(o[:, :, 0:2], raw[:, j:j + 1, SEQ:SEQ + 2]).then_inc(w["tails"], 1)
                    p.tensor_copy(o[:, :, 2:18].rearrange("p o (b t) -> p (o b) t", t=2), decode(j)[:, :, DS:DS + 2])\
                        .then_inc(w["tails"], 1)

                t0 = TB[f"f{l}"]
                for n in range(LOOK):
                    w_lo(n)
                pool.wait_ge(w["no_hist"], 4)
                pool.wait_ge(sm["tile_read"], TB[f"fst{l}"] + 2)
                for j in range(4):
                    p.tensor_copy(decode(j)[:, :, 0:2], st[:, :, :, (j % 2) * FT + j // 2]).then_inc(w["hist_ready"], 1)
                at = 0
                for part, (f0, nf) in enumerate(PARTS):
                    last = part == len(PARTS) - 1
                    with pool.Fori(0, nf // 2 - last) as i:
                        for j in range(4):
                            w_lo(at + j + LOOK, i)
                            tails(i, j)
                            pool.wait_ge(w["conv_ready"], i * 4 + (2 * f0 + j + 1))
                            pool.wait_ge(w["tails"], i * 8 + (4 * f0 + 2 * j + 2))
                            f = (j % 2) * FT + j // 2 + 2 + f0
                            src = st[:, :, :, bass.ds(i * 2 + f, 1)].rearrange("p b w o -> p b (w o)")
                            p.tensor_copy(decode(j)[:, :, 0:2], src).then_inc(w["hist_ready"], 1)
                    if last:
                        for j in range(4):
                            w_lo(at + 2 * nf - 4 + j + LOOK)
                            tails(nf // 2 - 1, j)
                    at += 2 * nf
                    for n in range(KT):
                        if at + n + LOOK < NFFN:
                            w_lo(at + n + LOOK)
                    at += KT

            ffn(0)
            kt = DW_POOL
            ptmp = arena[:, A_PTMP:A_PTMP + T]
            pool.wait_ge(sm["glu_ready"], kt + 1)
            for n in range(CW):
                dst = ptmp if n else cvo[:, kt, :]
                w = pcol("conv_dw_w", n * KT + kt)
                add = pcol("conv_dw_b", kt) if n == 0 else 0.0
                if n > 1:
                    pool.wait_ge(sm["pool_tap"], 2 * n - 1)
                p.tensor_scalar(dst[:, 0:SEQ], gb[:, kt, n:n + SEQ], w, add, ALU.mult, ALU.add)
                p.tensor_scalar(dst[:, SEQ:T].rearrange("p (b t) -> p b t", b=DB), gd[:, kt, :, n:n + DS], w, add, ALU.mult, ALU.add)\
                    .then_inc(sm["pool_tap"], 1)
                if n:
                    pool.wait_ge(sm["pool_tap"], 2 * n)
                    p.tensor_tensor(cvo[:, kt, :], cvo[:, kt, :], ptmp, ALU.add)\
                        .then_inc(sm["pool_tap"] if n < CW - 1 else sm["conv_pool"], 1)
            ffn(1)


def n_par_dmas():
    n = r = 0
    for _, m in PARAMS:
        at = 0
        while at < m:
            k = min(m - at, P - (r + at) % P)
            n += 1
            at += k
        r += m
    return n


OUTS = [("y_prompt", (1, SEQ, D)), ("y_sample", (DB, DS, D)), ("p_wkv", (1, 1, NH, HS, HS)), ("p_shift", (1, 1, D)),
        ("p_glu", (1, 1, NSTATE, D)), ("p_ffn", (2, 1, 2, 2 * F)), ("s_wkv", (1, DB, NH, HS, HS)), ("s_shift", (1, DB, D)),
        ("s_glu", (1, DB, NSTATE, D)), ("s_ffn", (2, DB, 2, 2 * F))]


def kernel(**inputs):
    import concourse.bacc as bacc
    from concourse.bass_utils import run_bass_kernel_spmd

    nc = bacc.Bacc("TRN2", target_bir_lowering=False, num_devices=1)
    arrays = {n: np.ascontiguousarray(v) for n, v in inputs.items() if np.asarray(v).size}
    arrays["consts"] = constants()
    args = {n: nc.dram_tensor(n, v.shape, mybir.dt.from_np(v.dtype), kind="ExternalInput").ap() for n, v in arrays.items()}
    outs = {n: nc.dram_tensor("out_" + n, s, F32, kind="ExternalOutput").ap() for n, s in OUTS}
    build(nc, args, outs)
    got = run_bass_kernel_spmd(nc, [arrays], core_ids=[0]).results[0]
    return tuple(got["out_" + n] for n, _ in OUTS)
```
